# Optimizing a Trainium2 kernel written in Bass

```python
import jax, jax.numpy as jnp
from jax import lax
import numpy as np

D_MODEL = 1024
BATCH = 1
SEQ = 512
DEPTH = 1

CHUNK = 64
D_MIX = D_MODEL
D_GMLP = D_MIX // 2
GMLP_GROUPS = 4
GMLP_GROUP_DIM = D_GMLP // GMLP_GROUPS
GMLP_BLOCK = 128
D_SB = D_MIX - D_GMLP
SB_HEADS = 8
SB_HEAD_DIM = D_SB // SB_HEADS
SB_QBLOCK = 128
N_EXPERTS = 64
TOP_K = 8
N_GROUPS = 8
TOPK_GROUPS = 4
D_EXPERT = D_MODEL // 4
D_SHARED = D_EXPERT
ROUTED_SCALE = 2.5
EPS = 1e-6
D_IN = 2 * D_GMLP + 3 * D_SB

kernel_name = 'hybrid_gmlp_stickbreak_moe_block'

def rmsnorm(x, g):
    xf = x.astype(jnp.float32)
    y = xf * lax.rsqrt(jnp.mean(xf * xf, axis=-1, keepdims=True) + EPS)
    return (y * g.astype(jnp.float32)).astype(x.dtype)

def layernorm(x, g, b):
    xf = x.astype(jnp.float32)
    mu = jnp.mean(xf, axis=-1, keepdims=True)
    var = jnp.mean(jnp.square(xf - mu), axis=-1, keepdims=True)
    y = (xf - mu) * lax.rsqrt(var + EPS)
    return (y * g.astype(jnp.float32) + b.astype(jnp.float32)).astype(x.dtype)

def gmlp_spatial_gating(u, v, ln_g, ln_b, w_s, b_s):
    B, S, _ = v.shape
    v = layernorm(v, ln_g, ln_b)
    i = jnp.arange(GMLP_BLOCK)
    mask = (i[None, :] // CHUNK) <= (i[:, None] // CHUNK)
    w = jnp.where(mask, w_s, 0.0)
    vb = v.reshape(B, S // GMLP_BLOCK, GMLP_BLOCK, GMLP_GROUPS, GMLP_GROUP_DIM)
    mixed = jnp.einsum('gij,bnjgc->bnigc', w, vb) + b_s.T[None, None, :, :, None]
    return u * mixed.reshape(B, S, D_GMLP)

def stick_breaking_attention(q, k, v):
    S = q.shape[2]
    scale = SB_HEAD_DIM ** -0.5
    outs = []
    for blk in range(S // SB_QBLOCK):
        q0 = blk * SB_QBLOCK
        kv_len = q0 + SB_QBLOCK
        qb = q[:, :, q0:kv_len].astype(jnp.float32)
        kb = k[:, :, :kv_len].astype(jnp.float32)
        vb = v[:, :, :kv_len]
        z = jnp.einsum('bhqd,bhkd->bhqk', qb, kb) * scale
        t = q0 + jnp.arange(SB_QBLOCK)[:, None]
        s = jnp.arange(kv_len)[None, :]
        mask = s < t
        log_1mb = jnp.where(mask, jax.nn.log_sigmoid(-z), 0.0)
        between = lax.cumsum(log_1mb, axis=3, reverse=True) - log_1mb
        a = jnp.where(mask, jnp.exp(jax.nn.log_sigmoid(z) + between), 0.0)
        outs.append(jnp.einsum('bhqk,bhkd->bhqd', a.astype(vb.dtype), vb))
    return jnp.concatenate(outs, axis=2)

def route(h, w_router, router_bias):
    T = h.shape[0]
    scores = jax.nn.sigmoid(h.astype(jnp.float32) @ w_router.astype(jnp.float32))
    biased = scores + router_bias.astype(jnp.float32)
    grouped = biased.reshape(T, N_GROUPS, N_EXPERTS // N_GROUPS)
    group_score = lax.top_k(grouped, 2)[0].sum(-1)
    _, top_groups = lax.top_k(group_score, TOPK_GROUPS)
    group_mask = (top_groups[:, :, None] == jnp.arange(N_GROUPS)[None, None, :]).any(axis=1)
    expert_mask = jnp.repeat(group_mask, N_EXPERTS // N_GROUPS, axis=1)
    masked = jnp.where(expert_mask, biased, -jnp.inf)
    _, idx = lax.top_k(masked, TOP_K)
    w = jnp.take_along_axis(scores, idx, axis=1)
    w = w / jnp.sum(w, axis=-1, keepdims=True) * ROUTED_SCALE
    return jnp.einsum('tk,tke->te', w, jax.nn.one_hot(idx, N_EXPERTS, dtype=jnp.float32))

def moe_ffn(h, w_router, router_bias, w_gate, w_up, w_down, ws_gate, ws_up, ws_down):
    B, S, D = h.shape
    gates = route(h.reshape(B * S, D), w_router, router_bias).reshape(B, S, N_EXPERTS).astype(h.dtype)

    def per_seq(args):
        hs, gs = args
        g = jnp.einsum('sd,edf->sef', hs, w_gate)
        u = jnp.einsum('sd,edf->sef', hs, w_up)
        act = jax.nn.silu(g) * u * gs[:, :, None]
        return jnp.einsum('sef,efd->sd', act, w_down)

    routed = lax.map(per_seq, (h, gates))
    shared = (jax.nn.silu(h @ ws_gate) * (h @ ws_up)) @ ws_down
    return routed + shared

def setup_inputs(seed: int = 0) -> dict:
    key = jax.random.key(seed)
    ks = jax.random.split(key, 24)
    n = lambda k, shape, s: jax.random.normal(k, shape, jnp.float32) * s
    L, D, E, F = DEPTH, D_MODEL, N_EXPERTS, D_EXPERT
    return {
        'x': n(ks[0], (BATCH, SEQ, D), 1.0),
        'c': n(ks[1], (BATCH, D), 1.0),
        'w_ada': n(ks[2], (L, D, 6 * D), 0.5 * D ** -0.5),
        'b_ada': n(ks[3], (L, 6 * D), 0.02),
        'g_pre_mix': 1.0 + n(ks[4], (L, D), 0.02),
        'w_in': n(ks[5], (L, D, D_IN), D ** -0.5),
        'ln_sgu_g': 1.0 + n(ks[6], (L, D_GMLP), 0.02),
        'ln_sgu_b': n(ks[7], (L, D_GMLP), 0.02),
        'w_spatial': n(ks[8], (L, GMLP_GROUPS, GMLP_BLOCK, GMLP_BLOCK), GMLP_BLOCK ** -0.5),
        'b_spatial': 1.0 + n(ks[9], (L, GMLP_GROUPS, GMLP_BLOCK), 0.1),
        'g_branch': 1.0 + n(ks[10], (L, D_MIX), 0.02),
        'w_out': n(ks[11], (L, D_MIX, D), D_MIX ** -0.5),
        'g_post_mix': 1.0 + n(ks[12], (L, D), 0.02),
        'g_pre_ffn': 1.0 + n(ks[13], (L, D), 0.02),
        'w_router': n(ks[14], (L, D, E), D ** -0.5),
        'router_bias': n(ks[15], (L, E), 0.01),
        'w_gate': n(ks[16], (L, E, D, F), D ** -0.5),
        'w_up': n(ks[17], (L, E, D, F), D ** -0.5),
        'w_down': n(ks[18], (L, E, F, D), F ** -0.5),
        'ws_gate': n(ks[19], (L, D, D_SHARED), D ** -0.5),
        'ws_up': n(ks[20], (L, D, D_SHARED), D ** -0.5),
        'ws_down': n(ks[21], (L, D_SHARED, D), D_SHARED ** -0.5),
        'g_post_ffn': 1.0 + n(ks[22], (L, D), 0.02),
    }

def reference(x, c, w_ada, b_ada, g_pre_mix, w_in, ln_sgu_g, ln_sgu_b, w_spatial, b_spatial,
              g_branch, w_out, g_post_mix, g_pre_ffn, w_router, router_bias, w_gate, w_up,
              w_down, ws_gate, ws_up, ws_down, g_post_ffn):
    B, S, D = x.shape
    sc = jax.nn.silu(c)
    for l in range(DEPTH):
        mod = (sc @ w_ada[l] + b_ada[l])[:, None, :]
        sh1, sc1, ga1, sh2, sc2, ga2 = jnp.split(mod, 6, axis=-1)

        h = rmsnorm(x, g_pre_mix[l]) * (1.0 + sc1) + sh1
        proj = h @ w_in[l]
        uv = jax.nn.gelu(proj[..., :2 * D_GMLP])
        u, v = uv[..., :D_GMLP], uv[..., D_GMLP:]
        q, k, vv = jnp.split(proj[..., 2 * D_GMLP:], 3, axis=-1)
        to_heads = lambda t: t.reshape(B, S, SB_HEADS, SB_HEAD_DIM).transpose(0, 2, 1, 3)
        o_sb = stick_breaking_attention(to_heads(q), to_heads(k), to_heads(vv))
        o_sb = o_sb.transpose(0, 2, 1, 3).reshape(B, S, D_SB)
        o_g = gmlp_spatial_gating(u, v, ln_sgu_g[l], ln_sgu_b[l], w_spatial[l], b_spatial[l])
        mixed = jnp.concatenate([rmsnorm(o_g, g_branch[l, :D_GMLP]),
                                 rmsnorm(o_sb, g_branch[l, D_GMLP:])], axis=-1)
        x = x + ga1 * rmsnorm(mixed @ w_out[l], g_post_mix[l])

        h = rmsnorm(x, g_pre_ffn[l]) * (1.0 + sc2) + sh2
        y = moe_ffn(h, w_router[l], router_bias[l], w_gate[l], w_up[l], w_down[l],
                    ws_gate[l], ws_up[l], ws_down[l])
        x = x + ga2 * rmsnorm(y, g_post_ffn[l])
    return x


_drawn_inputs = setup_inputs


def setup_inputs(seed=0):
    import zlib

    import numpy as np

    out = dict(_drawn_inputs(seed))
    spreads = {}
    factors = {'g_pre_mix': 3.143,
     'ln_sgu_g': 6.824,
     'ln_sgu_b': 7.047,
     'g_branch': 4.027,
     'g_post_mix': 3.784,
     'g_post_ffn': 8.0}
    for name, (base, spread) in spreads.items():
        noise = np.random.default_rng([zlib.crc32(name.encode()), seed]).standard_normal(out[name].shape)
        drawn = base * np.exp(spread * noise) if base else spread * noise
        out[name] = __import__('jax').numpy.asarray(drawn.astype(out[name].dtype))
    for name, factor in factors.items():
        out[name] = (out[name] * factor).astype(out[name].dtype)
    return out
```

```python
from contextlib import ExitStack

import concourse.bass as bass
from concourse import mybir

F32 = mybir.dt.float32
F32R = mybir.dt.float32r
BF16 = mybir.dt.bfloat16
I32 = mybir.dt.int32
U32 = mybir.dt.uint32
ALU = mybir.AluOpType
ACT = mybir.ActivationFunctionType
AX_X = mybir.AxisListType.X

P = 128
D = 1024
T = 512
TT = T // P
KD = D // P
DG = 512
GROUPS = 4
HEADS = 8
HD = 64
CHUNK = 64
E = 64
TOPK = 8
EG = 8
EPG = E // EG
TOPG = 4
F = 256
KF = F // P
SCALE_ROUTED = 2.5
EPS = 1e-6
NEG = -1.0e30
CAP = 40.0
BANK = 512
OVER = TOPK * T // P
COLS = E + OVER + 2
VC = 6
BIG_ROW = 1 << 17
POOL_K = 2


def block_kernel(nc, x, c, w_ada, b_ada, g_pre_mix, w_in, ln_sgu_g, ln_sgu_b, w_spatial, b_spatial,
                 g_branch, w_out, g_post_mix, g_pre_ffn, w_router, router_bias, w_gate, w_up,
                 w_down, ws_gate, ws_up, ws_down, g_post_ffn, out):
    with ExitStack() as ctx:
        def sem(name):
            return ctx.enter_context(nc.semaphore(name))

        base = 16512

        def at(name, shape, dt, off):
            return nc.alloc_sbuf_tensor_at(name, shape, dt, offset=base + off)

        KB = 1024
        raw = at("raw", [P, 2, 3, 2048], F32, 0)
        whi = at("whi", [P, 2, 3, 2048], F32R, 48 * KB)
        wlo = at("wlo", [P, 2, 3, 2048], F32R, 96 * KB)
        yall = at("yall", [P, TT, 9, D], F32, 0)
        ada = at("ada", [P, 2, 2, D], F32, 0)
        acc = at("acc", [P, 2, D], F32, 16 * KB)
        grow = at("grow", [P, D], F32, 24 * KB)
        lng = at("lng", [P, DG], F32, 28 * KB)
        lnb = at("lnb", [P, DG], F32, 30 * KB)
        win3 = at("win3", [P, KD, 512], F32, 32 * KB)
        win012 = at("win012", [P, 3, KD, 512], F32, 48 * KB)
        h1t = at("h1t", [P, KD, T], F32, 96 * KB)
        mixt = at("mixt", [P, KD, T], F32, 96 * KB)
        qt = at("qt", [P, 4, T], F32, 112 * KB)
        kt = at("kt", [P, 4, T], F32, 120 * KB)
        h2t = at("h2t", [P, KD, T], F32, 112 * KB)
        vv = at("vv", [P, TT, 512], F32, 128 * KB)
        wsd = at("wsd", [P, KF, D], F32, 128 * KB)
        ga1 = at("ga1", [P, D], F32, 136 * KB)
        a2 = at("a2", [P, D], F32, 140 * KB)
        wo = at("wo", [P, KD, D], F32, 48 * KB)
        ta = at("ta", [P, 1280], F32, 80 * KB)
        sp_sb = at("sp_sb", [P, 2, 1280], F32, 85 * KB)
        wsgu = at("wsgu", [P, 2, KD, F], F32, 80 * KB)
        xs = at("xs", [P, TT, D], F32, 144 * KB)
        z1 = at("z1", [P, TT, KD, P], F32, 160 * KB)
        u_sb = at("u_sb", [P, TT, DG], F32, 160 * KB)
        v_sb = at("v_sb", [P, TT, DG], F32, 168 * KB)
        sq = at("sq", [P, T], F32, 168 * KB)
        o_sb = at("o_sb", [P, 2, D], F32, 160 * KB)
        h2p = at("h2p", [P, 2, KD, P], F32, 168 * KB)
        hg = at("hg", [P, KD, P], F32, 160 * KB)
        hthi = at("hthi", [P, KD, P], F32R, 164 * KB)
        htlo = at("htlo", [P, KD, P], F32R, 168 * KB)
        ysb = at("ysb", [P, D], F32, 172 * KB)
        tabt = at("tabt", [E, 3, T], F32, 168 * KB)
        b2 = at("b2", [P, D], F32, 176 * KB)
        ga2 = at("ga2", [P, D], F32, 180 * KB)
        junk = at("junk", [P, D], F32, 184 * KB)
        at_sb = at("at_sb", [P, 2, 1280], F32, 184 * KB)
        scores = at("scores", [P, TT, E], F32, 184 * KB)
        biased = at("biased", [P, TT, E], F32, 185 * KB)
        masked = at("masked", [P, TT, E], F32, 186 * KB)
        picked = at("picked", [P, TT, E], F32, 187 * KB)
        sel = at("sel", [P, TT, E], F32, 188 * KB)
        gates = at("gates", [P, TT, COLS], F32, 189 * KB)
        posm = at("posm", [P, TT, E], F32, 191 * KB)
        rank = at("rank", [P, TT, E], F32, 192 * KB)
        selb = at("selb", [P, TT, E], BF16, 193 * KB)
        small0 = 194 * KB
        smalls = [small0]

        def small(name, shape, dt):
            n = 1
            for s in shape[1:]:
                n *= s
            n *= 2 if dt == BF16 else 4
            t = at(name, shape, dt, smalls[0])
            smalls[0] += -(-n // 32) * 32
            return t

        posb = small("posb", [P, TT, COLS], F32)
        vtab = small("vtab", [P, TT, COLS, VC], BF16)
        negtri = at("negtri", [P, P], F32, small0)
        negones = at("negones", [P, P], F32, small0 + 512)
        negmask = at("negmask", [P, P], BF16, small0 + 1024)
        wsp = at("wsp", [P, GROUPS, P], F32, small0 + 1280)
        wspt = at("wspt", [P, GROUPS, P], F32, small0 + 3328)
        ident = small("ident", [P, P], F32)
        identb = small("identb", [P, P], BF16)
        ones = small("ones", [P, P], F32)
        ustrb = small("ustrb", [P, P], BF16)
        onesb = small("onesb", [P, P], BF16)
        iotab = small("iotab", [P, P], BF16)
        s_onehot = at("s_onehot", [P, TT, P], BF16, 186 * KB)
        sg = small("sg", [P, F], F32)
        act_s = small("act_s", [P, KF, P], F32)
        acthi = at("acthi", [P, KF, P], F32R, 184 * KB)
        actlo = at("actlo", [P, KF, P], F32R, 185 * KB)
        sht = at("sht", [P, KF, P], F32, 172 * KB)
        ysh = at("ysh", [P, D], F32, 160 * KB)
        c_col = small("c_col", [P, KD], F32)
        sc_col = small("sc_col", [P, KD], F32)
        a1c = small("a1c", [P, KD], F32)
        b1c = small("b1c", [P, KD], F32)
        bsc = small("bsc", [P, KD], F32)
        bsh = small("bsh", [P, KD], F32)
        gpm = small("gpm", [P, KD], F32)
        gb = small("gb", [P, KD], F32)
        bsp = small("bsp", [P, GROUPS], F32)
        rb = small("rb", [P, E], F32)
        wr = at("wr", [P, KD, E], F32, 28 * KB)
        stat = small("stat", [P, 6, TT], F32)
        var = small("var", [P, 6, TT], F32)
        root = small("root", [P, 6, TT], F32)
        rs = small("rs", [P, 6, TT], F32)
        nt = small("nt", [P, TT], F32)
        ss16 = small("ss16", [P, TT, 4], F32)
        top2 = at("top2", [P, TT, EG, 8], F32, 186 * KB)
        gs = small("gs", [P, TT, EG], F32)
        gcmp = at("gcmp", [P, TT, EG, EG], F32, 187 * KB)
        gcmp2 = at("gcmp2", [P, TT, EG, EG], F32, 188 * KB)
        gtri = at("gtri", [P, EG, EG], F32, 193 * KB + 512)
        gm = small("gm", [P, TT, EG], F32)
        top8 = small("top8", [P, TT, 8], F32)
        wsum = small("wsum", [P, TT], F32)
        ext = small("ext", [E, 2], F32)
        extb = small("extb", [E, 1], BF16)
        iot32 = small("iot32", [E, OVER], F32)
        iote = small("iote", [E, 1], F32)
        tmp32 = small("tmp32", [E, OVER], F32)
        selx = small("selx", [E, OVER], F32)
        jm = small("jm", [E, OVER], F32)
        nover = small("nover", [1, 1], I32)
        eid = small("eid", [1, OVER], I32)
        pair = small("pair", [P, 2], F32)
        inval = small("inval", [P, 1], F32)
        desti = small("desti", [P, 1], I32)
        idxg = small("idxg", [P, 1], I32)
        idxs = small("idxs", [P, 1], I32)
        destr = at("destr", [P, COLS], I32, 187 * KB)
        gater = at("gater", [P, COLS], F32, 187 * KB + 512)
        assert base + smalls[0] <= nc.sbuf_usable_end, (base + smalls[0], nc.sbuf_usable_end)

        ps = ctx.enter_context(nc.psum_tensor("ps", [P, 8 * BANK], F32))

        def bank(b, n=1):
            return ps[:, b * BANK:(b + n) * BANK]

        h_rows = nc.dram_tensor("h_rows", [T, D], F32, kind="Internal").ap()
        y_rows = nc.dram_tensor("y_rows", [9 * T, D], F32, kind="Internal").ap()

        c_in = sem("c_in")
        x_in = [sem(f"x_in{t}") for t in range(TT)]
        vec_in = sem("vec_in")
        grow_in = sem("grow_in")
        ada_in = [sem(f"ada_in{s}") for s in range(2)]
        ada_used = sem("ada_used")
        win_in = [sem(f"win_in{i}") for i in range(5)]
        wo_in = sem("wo_in")
        wsgu_in = sem("wsgu_in")
        wsd_in = sem("wsd_in")
        wr_in = sem("wr_in")
        const_ok = sem("const_ok")
        pool_step = sem("pool_step")
        v_step = sem("v_step")
        a_step = sem("a_step")
        sc_ok = sem("sc_ok")
        sumsq = sem("sumsq")
        var_ok = sem("var_ok")
        root_ok = sem("root_ok")
        rs_g_ok = sem("rs_g_ok")
        rs_sb_ok = sem("rs_sb_ok")
        z_ok = sem("z_ok")
        acc_ok = sem("acc_ok")
        mod_mm = sem("mod_mm")
        row_ok = sem("row_ok")
        ab_ok = sem("ab_ok")
        h1_tr = sem("h1_tr")
        h1_act = sem("h1_act")
        h1_dve = sem("h1_dve")
        wsp_tr = sem("wsp_tr")
        wsp_ok = sem("wsp_ok")
        proj_mm = sem("proj_mm")
        proj_ev = sem("proj_ev")
        vmean_ok = sem("vmean_ok")
        vn_ok = sem("vn_ok")
        mixed_mm = sem("mixed_mm")
        og_ok = sem("og_ok")
        og_tr = sem("og_tr")
        og_ev = sem("og_ev")
        z_mm = sem("z_mm")
        cap_ok = sem("cap_ok")
        ln_ok = sem("ln_ok")
        sp_ok = sem("sp_ok")
        x_mm = sem("x_mm")
        a_ok = sem("a_ok")
        o_mm = sem("o_mm")
        o_ev = sem("o_ev")
        ss_mm = sem("ss_mm")
        wo_mm = sem("wo_mm")
        wo_a = sem("wo_a")
        wo_o = sem("wo_o")
        wo_x = sem("wo_x")
        h2_ok = sem("h2_ok")
        h2_out = [sem(f"h2_out{s}") for s in range(2)]
        h2_tr = sem("h2_tr")
        h2_ev = sem("h2_ev")
        lg_mm = sem("lg_mm")
        sig_ok = sem("sig_ok")
        sgu_mm = sem("sgu_mm")
        ssg_ok = sem("ssg_ok")
        sact_ok = sem("sact_ok")
        sat_tr = sem("sat_tr")
        sat_ev = sem("sat_ev")
        sdn_mm = sem("sdn_mm")
        sdn_ev = sem("sdn_ev")
        ysh_out = sem("ysh_out")
        sel_ok = sem("sel_ok")
        cnt_mm = sem("cnt_mm")
        ext_ok = sem("ext_ok")
        start_mm = sem("start_mm")
        selx_ok = sem("selx_ok")
        tab_tr = sem("tab_tr")
        tab_ev = sem("tab_ev")
        over_mm = sem("over_mm")
        tables_ok = sem("tables_ok")
        w_in_sem = [[sem(f"w_in{s}{p}") for p in range(3)] for s in range(2)]
        wx_in = [sem(f"wx_in{p}") for p in range(3)]
        hi_ok = sem("hi_ok")
        lo_dve = sem("lo_dve")
        lo_pool = sem("lo_pool")
        onehot_ok = sem("onehot_ok")
        idx_mm = sem("idx_mm")
        idx_ok = sem("idx_ok")
        gather_go = sem("gather_go")
        scatter_go = sem("scatter_go")
        gathered = sem("gathered")
        ht_tr = sem("ht_tr")
        hthi_ok = sem("hthi_ok")
        htlo_ok = sem("htlo_ok")
        gu_mm = sem("gu_mm")
        silu_ok = sem("silu_ok")
        act_ok = sem("act_ok")
        at_tr = sem("at_tr")
        acthi_ok = sem("acthi_ok")
        actlo_ok = sem("actlo_ok")
        dn_mm = sem("dn_mm")
        y_ok = sem("y_ok")
        idxs_ok = sem("idxs_ok")
        scattered = sem("scattered")
        hg_zero = sem("hg_zero")
        v_loop = sem("v_loop")
        y_in = [sem(f"y_in{t}") for t in range(TT)]
        ysum_ok = sem("ysum_ok")
        out_ok = sem("out_ok")
        out_done = sem("out_done")

        ada_v = w_ada.rearrange("(p k) n -> p k n", k=KD)
        win_v = w_in.rearrange("(p k) n -> p k n", k=KD)
        wo_v = w_out.rearrange("(k p) n -> p k n", p=P)
        wg_v = w_gate.rearrange("e (p k) f -> e p (k f)", k=KD)
        wu_v = w_up.rearrange("e (p k) f -> e p (k f)", k=KD)
        wd_v = w_down.rearrange("e (p k) n -> e p (k n)", k=KF)
        y_v = y_rows.rearrange("(r t p) n -> t p r n", r=9, p=P)

        SC1, SH1, GA1, SC2, SH2, GA2 = 1, 0, 2, 4, 3, 5
        CHUNKS = [SC1, SH1, GA1, SC2, SH2, GA2]
        COLG = [2 * DG, 2 * DG + 512, 2 * DG + 1024, DG, 0]

        def win_tile(i):
            return win3 if i == 3 else win012[:, (0 if i == 4 else i)]

        ZOFF = {0: 0, 1: 512, 3: 896, 2: 1024}
        ZW = {j: T - P * j for j in range(TT)}

        def zbank(h):
            return ps[:, (h % 2) * 3 * BANK:(h % 2) * 3 * BANK + 1280]

        ST_X, ST_VS, ST_V, ST_G, ST_S, ST_O = range(6)

        def part(tile, slot, piece, c0, c1):
            if isinstance(slot, int):
                return tile[:, slot, piece, c0:c1]
            return tile[:, bass.ds(slot, 1), piece, c0:c1].rearrange("p s f -> p (s f)")

        def pair_out(ac, A, ct):
            ac.wait_ge(o_mm, 2 * ct + 2)
            if ct >= 1:
                ac.wait_ge(ss_mm, ct)
            A(sq[:, :], bank(6), ACT.Square)
            A(mixt[:, 4 + ct, :], bank(6), ACT.Copy, scale=gb[:, 4 + ct:5 + ct]).then_inc(o_ev, 1)

        block = ctx.enter_context(nc.Block())

        @block.sync
        def _(sp):
            sp.dma_start(c_col[:, :], c.rearrange("(p k) -> p k", k=KD)).then_inc(c_in, 16)
            for t in range(TT):
                sp.dma_start(xs[:, t, :], x[t * P:(t + 1) * P, :]).then_inc(x_in[t], 16)
            for n in range(4 * len(CHUNKS)):
                g, q = CHUNKS[n // 4], n % 4
                if n >= 2:
                    sp.wait_ge(ada_used, n - 1)
                if n == 12:
                    sp.wait_ge(row_ok, 1)
                    sp.dma_start(grow[:, :], g_pre_ffn.partition_broadcast(P)).then_inc(grow_in, 16)
                if n == 20:
                    sp.wait_ge(row_ok, 3)
                    sp.dma_start(grow[:, :], g_post_ffn.partition_broadcast(P)).then_inc(grow_in, 16)
                sp.dma_start(ada[:, n % 2, :, :], ada_v[:, 2 * q:2 * q + 2, g * D:(g + 1) * D])\
                  .then_inc(ada_in[n % 2], 16)
            sp.wait_ge(row_ok, 4)
            sp.wait_ge(vn_ok, 1)
            sp.wait_ge(proj_mm, 20)
            sp.dma_start(wr[:, :, :], w_router.rearrange("(p k) e -> p k e", k=KD)).then_inc(wr_in, 16)

            def load(e, slot, sems, before=None):
                for p_, v_ in enumerate((wg_v, wu_v, wd_v)):
                    if before is not None:
                        before(p_)
                    sp.dma_start(raw[:, slot, p_, :], v_[bass.ds(e, 1)].rearrange("e p f -> p (e f)"))\
                      .then_inc(sems[p_], 16)

            def freed(n):
                sp.wait_ge(hi_ok, n)
                sp.wait_ge(lo_dve, n)
                sp.wait_ge(lo_pool, n)

            for t in range(TT):
                sp.wait_ge(h2_ok, t + 1)
                sp.dma_start(h_rows[t * P:(t + 1) * P, :], h2p[:, t % 2].rearrange("p k q -> p (k q)"))\
                  .then_inc(h2_out[t % 2], 16)
            sp.wait_ge(lg_mm, 1)
            load(0, 0, w_in_sem[0])
            load(1, 1, w_in_sem[1])
            for t in range(TT):
                sp.wait_ge(sdn_ev, t + 1)
                sp.dma_start(y_rows[8 * T + t * P:8 * T + (t + 1) * P, :], ysh[:, :]).then_inc(ysh_out, 16)
            with sp.Fori(1, E // 2) as i:
                for s in range(2):
                    load(i * 2 + s, s, w_in_sem[s], lambda p_: freed(i * 6 + (3 * s - 5 + p_)))
            sp.wait_ge(tables_ok, 1)
            n = sp.value_load(nover[0:1, 0:1], min_val=0, max_val=OVER)
            with sp.If(n > 0):
                with sp.Fori(0, n) as j:
                    e = sp.value_load(eid[0:1, bass.ds(j, 1)], min_val=0, max_val=E - 1)
                    load(e, 0, wx_in, lambda p_: freed(j * 3 + (3 * (E - 1) + 1 + p_)))
            sp.wait_ge(scattered, n * 16 + 16 * E)
            for t in range(TT):
                if t == 0:
                    sp.wait_ge(ysh_out, 16 * TT)
                sp.dma_start(yall[:, t], y_v[t]).then_inc(y_in[t], 16)
            for t in range(TT):
                sp.wait_ge(out_ok, t + 1)
                sp.dma_start(out[t * P:(t + 1) * P, :], xs[:, t, :]).then_inc(out_done, 16)
            sp.wait_ge(out_done, 16 * TT)

        @block.gpsimd
        def _(gp):
            step = [0]

            def then(ins):
                step[0] += 1
                ins.then_inc(pool_step, 1)
                gp.wait_ge(pool_step, step[0])

            last_row, last_routed = gp.to_reg(T - 1), gp.to_reg(TOPK * T - 1)

            def pick(tile, op, fill, pattern, mult, base_=0):
                return gp.affine_select(out=tile, in_=tile, compare_op=op, fill=fill, base=base_,
                                        pattern=pattern, channel_multiplier=mult)

            gp.memset(ones[:, :], 1.0)
            gp.memset(onesb[:, :], 1.0)
            gp.memset(ident[:, :], 0.0)
            gp.memset(identb[:, :], 0.0)
            gp.memset(negtri[:, :], -1.0)
            gp.memset(negones[:, :], -1.0)
            gp.memset(negmask[:, :], 0.0)
            gp.memset(ustrb[:, :], 1.0)
            gp.iota(iotab[:, :], [[1, P]], base=0, channel_multiplier=0, allow_small_or_imprecise_dtypes=True)
            gp.iota(iot32[:, :], [[1, OVER]], base=0, channel_multiplier=0, allow_small_or_imprecise_dtypes=True)
            then(gp.iota(iote[:, :], [[0, 1]], base=0, channel_multiplier=1, allow_small_or_imprecise_dtypes=True))
            pick(ident[:, :], ALU.not_equal, 1.0, [[-1, P]], 1)
            pick(identb[:, :], ALU.not_equal, 1.0, [[-1, P]], 1)
            pick(negtri[:, :], ALU.is_ge, 0.0, [[-1, P]], 1)
            pick(negmask[:, :], ALU.is_gt, NEG, [[1, P]], -1)
            then(pick(ustrb[:, :], ALU.is_gt, 0.0, [[1, P]], -1))
            gp.sem_inc(const_ok, 1)

            for i in range(5):
                if i == 0:
                    gp.wait_ge(ada_used, 5)
                if i == 4:
                    gp.wait_ge(proj_mm, 4)
                dst = win_tile(i)
                gp.dma_start(dst[:, :, :] if i == 3 else dst, win_v[:, :, COLG[i]:COLG[i] + 512])\
                  .then_inc(win_in[i], 16)
            gp.wait_ge(proj_mm, 20)
            for k in range(0, KD, 4):
                gp.dma_start(wo[:, k:k + 4, :], wo_v[:, k:k + 4, :]).then_inc(wo_in, 16)
            gp.wait_ge(o_mm, HEADS)
            gp.wait_ge(x_mm, HEADS)
            gp.wait_ge(a_ok, HEADS)
            gp.dma_start(wsgu[:, 0], ws_gate.rearrange("(p k) f -> p k f", k=KD)).then_inc(wsgu_in, 16)
            gp.dma_start(wsgu[:, 1], ws_up.rearrange("(p k) f -> p k f", k=KD)).then_inc(wsgu_in, 16)
            gp.dma_start(wsd[:, :, :], ws_down.rearrange("(p k) n -> p k n", k=KF)).then_inc(wsd_in, 16)
            gp.wait_ge(sel_ok, 1)
            gp.memset(posb[:, :, E:COLS], -1.0)
            gp.memset(gates[:, :, E:COLS], 0.0)
            then(gp.memset(vtab[:, :, :, :], 0.0))
            for t in range(TT):
                then(gp.iota(vtab[:, t, :, 0], [[0, COLS]], base=t * P, channel_multiplier=0,
                             allow_small_or_imprecise_dtypes=True))
                then(gp.iota(vtab[:, t, :, 1], [[0, COLS]], base=1, channel_multiplier=1,
                             allow_small_or_imprecise_dtypes=True))
            gp.sem_inc(const_ok, 1)

            def gather(b):
                gp.wait_ge(idx_ok, b + 1)
                gp.wait_ge(ht_tr, b)
                gp.sem_inc(gather_go, 1)
                gp.indirect_dma_start(out=hg[:, :, :].rearrange("p k q -> p (k q)"), out_offset=None,
                                      in_=h_rows, in_offset=bass.IndirectOffsetOnAxis(ap=idxg[:, 0:1], axis=0),
                                      bounds_check=last_row, oob_is_err=False).then_inc(gathered, 16)

            def scatter(b):
                gp.wait_ge(y_ok, b + 1)
                gp.wait_ge(idxs_ok, b + 1)
                gp.sem_inc(scatter_go, 1)
                gp.indirect_dma_start(out=y_rows, out_offset=bass.IndirectOffsetOnAxis(ap=idxs[:, 0:1], axis=0),
                                      in_=ysb[:, :], in_offset=None,
                                      bounds_check=last_routed, oob_is_err=False).then_inc(scattered, 16)

            def low_raw(b, wslot, rslot, piece):
                gp.wait_ge(hi_ok, b * 3 + (piece + 1))
                c0 = 2048 - POOL_K * 256
                gp.tensor_tensor(part(wlo, wslot, piece, c0, 2048), raw[:, rslot, piece, c0:2048],
                                 part(whi, wslot, piece, c0, 2048).bitcast(F32), ALU.subtract)\
                  .then_inc(lo_pool, 1)

            def one(b, wslot, rslot, first):
                if first != 0:
                    if first != 1:
                        gp.wait_ge(gu_mm, b - 1)
                low_raw(b, wslot, rslot, 0)
                low_raw(b, wslot, rslot, 1)
                gather(b + 1)
                if first != 0 and first != 1:
                    gp.wait_ge(dn_mm, b - 1)
                low_raw(b, wslot, rslot, 2)
                if first != 0 and first != 1:
                    scatter(b - 2)

            gp.wait_ge(hg_zero, 1)
            gp.wait_ge(h2_out[0], 16 * TT // 2)
            gp.wait_ge(h2_out[1], 16 * TT // 2)
            gp.wait_ge(idx_ok, 1)
            gp.indirect_dma_start(out=hg[:, :, :].rearrange("p k q -> p (k q)"), out_offset=None,
                                  in_=h_rows, in_offset=bass.IndirectOffsetOnAxis(ap=idxg[:, 0:1], axis=0),
                                  bounds_check=last_row, oob_is_err=False).then_inc(gathered, 16)
            one(0, 0, 0, 0)
            one(1, 1, 1, 1)
            with gp.Fori(1, E // 2) as i:
                for s in range(2):
                    one(i * 2 + s, s, s, 2)
            gp.wait_ge(tables_ok, 1)
            n = gp.value_load(nover[0:1, 0:1], min_val=0, max_val=OVER)
            with gp.If(n > 0):
                with gp.Fori(E, n + E) as b:
                    one(b, b % 2, 0, 2)
            scatter(n + (E - 2))
            scatter(n + (E - 1))

        @block.scalar
        def _(ac):
            A = nc.scalar.activation
            step = [0]

            def then(ins):
                step[0] += 1
                ins.then_inc(a_step, 1)
                ac.wait_ge(a_step, step[0])

            def load(dst, src):
                ac.dma_start(dst, src).then_inc(vec_in, 16)

            load(bsc[:, :], b_ada[SC1 * D:(SC1 + 1) * D].rearrange("(p k) -> p k", k=KD))
            load(bsh[:, :], b_ada[SH1 * D:(SH1 + 1) * D].rearrange("(p k) -> p k", k=KD))
            load(gpm[:, :], g_pre_mix.rearrange("(p k) -> p k", k=KD))
            load(wsp[:, :, :], w_spatial.rearrange("g i j -> i g j"))
            with nc.allow_non_contiguous_dma(reason="two short vectors by column"):
                load(gb[:, :], g_branch.rearrange("(k p) -> p k", p=P))
                load(bsp[:, :], b_spatial.rearrange("g i -> i g"))
            load(lng[:, :], ln_sgu_g.partition_broadcast(P))
            load(lnb[:, :], ln_sgu_b.partition_broadcast(P))
            load(ga1[:, :], b_ada[GA1 * D:(GA1 + 1) * D].partition_broadcast(P))
            load(a2[:, :], b_ada[SC2 * D:(SC2 + 1) * D].partition_broadcast(P))
            load(b2[:, :], b_ada[SH2 * D:(SH2 + 1) * D].partition_broadcast(P))
            load(ga2[:, :], b_ada[GA2 * D:(GA2 + 1) * D].partition_broadcast(P))
            load(rb[:, :], router_bias.partition_broadcast(P))
            ac.dma_start(grow[:, :], g_post_mix.partition_broadcast(P)).then_inc(grow_in, 16)

            ac.wait_ge(c_in, 16)
            A(sc_col[:, :], c_col[:, :], ACT.Silu).then_inc(sc_ok, 1)
            roots = [0]

            def take_root(st, c0=0, c1=TT):
                roots[0] += 1
                ac.wait_ge(var_ok, roots[0])
                A(root[:, st, c0:c1], var[:, st, c0:c1], ACT.Sqrt).then_inc(root_ok, 1)

            for t in range(TT):
                ac.wait_ge(x_in[t], 16)
                ins = A(junk[:, :], xs[:, t, :], ACT.Square, accum_out=stat[:, ST_X, t:t + 1])
                ins.then_inc(sumsq, 1) if t == TT - 1 else then(ins)
            take_root(ST_X)
            ac.wait_ge(ab_ok, 1)
            for k in range(0, KD, 2):
                ac.wait_ge(h1_tr, k + 1)
                A(h1t[:, k, :], bank(k % 6), ACT.Identity, bias=b1c[:, k:k + 1], scale=a1c[:, k:k + 1])\
                    .then_inc(h1_act, 1)
            for n in range(20):
                ac.wait_ge(proj_mm, n + 1)
                src = bank(n % 4)
                if n < 4:
                    A(qt[:, n, :], src, ACT.Copy, scale=HD ** -0.5).then_inc(proj_ev, 1)
                elif n < 8:
                    A(kt[:, n - 4, :], src, ACT.Copy).then_inc(proj_ev, 1)
                elif n < 12:
                    A(vv[:, n - 8, :], src, ACT.Copy).then_inc(proj_ev, 1)
                elif n < 16:
                    t = n - 12
                    A(v_sb[:, t, :], src, ACT.Gelu_apprx_tanh, accum_out=stat[:, ST_VS, t:t + 1])\
                        .then_inc(proj_ev, 1)
                else:
                    A(u_sb[:, n - 16, :], src, ACT.Gelu_apprx_tanh).then_inc(proj_ev, 1)
            ac.wait_ge(vmean_ok, 1)
            for t in range(TT):
                ins = A(junk[:, 0:DG], v_sb[:, t, :], ACT.Square, accum_out=stat[:, ST_V, t:t + 1])
                ins.then_inc(sumsq, 1) if t == TT - 1 else then(ins)
            take_root(ST_V)
            ac.wait_ge(og_ok, GROUPS)
            for t in range(TT):
                ins = A(junk[:, 0:DG], u_sb[:, t, :], ACT.Square, accum_out=stat[:, ST_G, t:t + 1])
                ins.then_inc(sumsq, 1) if t == TT - 1 else then(ins)
            take_root(ST_G)
            for k in range(4):
                ac.wait_ge(og_tr, k + 1)
                A(mixt[:, k, :], bank(4 + k), ACT.Copy, scale=gb[:, k:k + 1]).then_inc(og_ev, 1)
            for h in range(HEADS + 1):
                if h < HEADS:
                    ac.wait_ge(cap_ok, h + 1)
                    then(A(ta[:, :], ta[:, :], ACT.Exp))
                    A(ta[:, :], ta[:, :], ACT.Ln, bias=1.0).then_inc(ln_ok, 1)
                if h >= 1:
                    g = h - 1
                    ac.wait_ge(x_mm, g + 1)
                    if g >= 2:
                        ac.wait_ge(o_mm, g - 1)
                    A(at_sb[:, g % 2, :], zbank(g), ACT.Exp).then_inc(a_ok, 1)
                if h >= 3 and h % 2 == 1:
                    pair_out(ac, A, (h - 3) // 2)
            pair_out(ac, A, 3)
            take_root(ST_X)
            for t in range(TT):
                ac.wait_ge(wo_mm, t + 1)
                if t == 0:
                    ac.wait_ge(rs_g_ok, 1)
                    ac.wait_ge(rs_sb_ok, 1)
                pa = ps[:, (t % 2) * 4 * BANK:(t % 2) * 4 * BANK + 2 * BANK]
                if t >= 2:
                    ac.wait_ge(h2_ok, t - 1)
                A(o_sb[:, t % 2, :], pa, ACT.Copy, scale=rs[:, ST_G, t:t + 1]).then_inc(wo_a, 1)
                ac.wait_ge(wo_o, t + 1)
                A(junk[:, :], o_sb[:, t % 2, :], ACT.Square, accum_out=stat[:, ST_S, t:t + 1]).then_inc(sumsq, 1)
                take_root(ST_S, t, t + 1)
                ac.wait_ge(wo_x, t + 1)
                A(junk[:, :], xs[:, t, :], ACT.Square, accum_out=stat[:, ST_O, t:t + 1]).then_inc(sumsq, 1)
                take_root(ST_O, t, t + 1)
                ac.wait_ge(h2_tr, t + 1)
                A(h2t[:, :, t * P:(t + 1) * P], pa.rearrange("p (k q) -> p k q", k=KD), ACT.Copy)\
                    .then_inc(h2_ev, 1)
            ac.wait_ge(lg_mm, 1)
            A(scores[:, :, :], ps[:, 7 * BANK:7 * BANK + TT * E].rearrange("p (t e) -> p t e", t=TT),
              ACT.Sigmoid).then_inc(sig_ok, 1)
            for t in range(TT + 1):
                if t < TT:
                    ac.wait_ge(sgu_mm, t + 1)
                    if t >= 1:
                        ac.wait_ge(sact_ok, t)
                    A(sg[:, :], bank(t % 2)[:, 0:F], ACT.Silu).then_inc(ssg_ok, 1)
                if t >= 1:
                    g = t - 1
                    ac.wait_ge(sat_tr, g + 1)
                    if g >= 1:
                        ac.wait_ge(sdn_mm, g)
                    else:
                        ac.wait_ge(h2_out[0], 16 * TT // 2)
                        ac.wait_ge(h2_out[1], 16 * TT // 2)
                    A(sht[:, :, :], bank(2)[:, 0:F].rearrange("p (k q) -> p k q", k=KF), ACT.Copy)\
                        .then_inc(sat_ev, 1)
                    ac.wait_ge(sdn_mm, g + 1)
                    if g >= 1:
                        ac.wait_ge(ysh_out, 16 * g)
                    A(ysh[:, :], bank(3, 2), ACT.Copy).then_inc(sdn_ev, 1)
            ac.wait_ge(tab_tr, 1)
            for q in range(3):
                A(tabt[:, q, :], ps[0:E, q * BANK:(q + 1) * BANK], ACT.Copy).then_inc(tab_ev, 1)

            def high(b, wslot, rslot, piece, landed):
                ac.wait_ge(*landed)
                A(part(whi, wslot, piece, 0, 2048), raw[:, rslot, piece, :], ACT.Copy).then_inc(hi_ok, 1)

            def silu(b):
                ac.wait_ge(gu_mm, b + 1)
                ac.wait_ge(act_ok, b)
                A(sg[:, :], bank(2)[:, 0:F], ACT.Silu).then_inc(silu_ok, 1)

            def ht_high(b):
                ac.wait_ge(ht_tr, b + 1)
                ac.wait_ge(gu_mm, b)
                A(hthi[:, :, :], bank(0, 2).rearrange("p (k q) -> p k q", k=KD), ACT.Copy).then_inc(hthi_ok, 1)

            def y_out(b):
                ac.wait_ge(dn_mm, b + 1)
                ac.wait_ge(scattered, b * 16)
                A(ysb[:, :], bank(4, 2), ACT.Copy).then_inc(y_ok, 1)

            def one(b, wslot, rslot, landed, first):
                if first >= 2:
                    ac.wait_ge(gu_mm, b - 1)
                high(b, wslot, rslot, 0, landed[0])
                high(b, wslot, rslot, 1, landed[1])
                if first >= 1:
                    if first == 1:
                        ac.wait_ge(gu_mm, b)
                        A(sg[:, :], bank(2)[:, 0:F], ACT.Silu).then_inc(silu_ok, 1)
                    else:
                        silu(b - 1)
                    ht_high(b)
                else:
                    ac.wait_ge(ht_tr, 1)
                    A(hthi[:, :, :], bank(0, 2).rearrange("p (k q) -> p k q", k=KD), ACT.Copy)\
                        .then_inc(hthi_ok, 1)
                if first >= 2:
                    ac.wait_ge(dn_mm, b - 1)
                high(b, wslot, rslot, 2, landed[2])
                if first == 2:
                    ac.wait_ge(dn_mm, 1)
                    A(ysb[:, :], bank(4, 2), ACT.Copy).then_inc(y_ok, 1)
                if first > 2:
                    y_out(b - 2)

            ac.wait_ge(tables_ok, 1)
            one(0, 0, 0, [(w_in_sem[0][p_], 16) for p_ in range(3)], 0)
            one(1, 1, 1, [(w_in_sem[1][p_], 16) for p_ in range(3)], 1)
            one(2, 0, 0, [(w_in_sem[0][p_], 32) for p_ in range(3)], 2)
            one(3, 1, 1, [(w_in_sem[1][p_], 32) for p_ in range(3)], 3)
            with ac.Fori(2, E // 2) as i:
                for s in range(2):
                    one(i * 2 + s, s, s, [(w_in_sem[s][p_], i * 16 + 16) for p_ in range(3)], 3)
            n = ac.value_load(nover[0:1, 0:1], min_val=0, max_val=OVER)
            with ac.If(n > 0):
                with ac.Fori(E, n + E) as b:
                    one(b, b % 2, 0, [(wx_in[p_], b * 16 - 16 * (E - 1)) for p_ in range(3)], 3)
            silu(n + (E - 1))
            y_out(n + (E - 2))
            y_out(n + (E - 1))
            for t in range(TT):
                ac.wait_ge(ysum_ok, t + 1)
                A(junk[:, :], yall[:, t, 0, :], ACT.Square, accum_out=stat[:, ST_S, t:t + 1]).then_inc(sumsq, 1)
                take_root(ST_S, t, t + 1)

        @block.tensor
        def _(pe):
            mm = pe.matmul

            def transpose(o, i):
                return pe.transpose(o, i, ident[:, :])

            pe.wait_ge(const_ok, 1)
            pe.wait_ge(z_ok, TT)

            def h1_transposes(k):
                for t in range(TT):
                    ins = transpose(bank(k % 6)[:, t * P:(t + 1) * P], z1[:, t, k, :])
                ins.then_inc(h1_tr, 1)

            for k in range(6):
                h1_transposes(k)
            for ch in range(2):
                pe.wait_ge(acc_ok, ch + 1)
                cols = acc[:, ch, :].rearrange("p (q k) -> p k q", k=KD)
                for k in range(KD):
                    ins = mm(ps[:, 6 * BANK + ch * KD + k:6 * BANK + ch * KD + k + 1], cols[:, k, :],
                             ones[:, 0:1], start=True, stop=True)
                ins.then_inc(mod_mm, 1)
            pe.wait_ge(h1_act, 1)
            h1_transposes(6)
            pe.wait_ge(h1_dve, 1)
            h1_transposes(7)
            pe.wait_ge(h1_act, 4)
            pe.wait_ge(h1_dve, 4)
            pe.wait_ge(vec_in, 16 * 13)
            for g in range(GROUPS):
                ins = transpose(bank(4)[:, g * P:(g + 1) * P], wsp[:, g, :])
            ins.then_inc(wsp_tr, 1)

            def modulation_row(ch):
                pe.wait_ge(acc_ok, ch + 1)
                if ch > 2:
                    pe.wait_ge(row_ok, ch - 2)
                for hf in range(2):
                    ins = mm(bank(6 + hf), ones[:, :], acc[:, ch % 2, hf * 512:(hf + 1) * 512],
                             start=True, stop=True)
                ins.then_inc(mod_mm, 1)

            for n in range(20):
                g, m = n // 4, n % 4
                if m == 0:
                    pe.wait_ge(win_in[g], 16)
                    if g >= 2:
                        modulation_row(g)
                if n >= 4:
                    pe.wait_ge(proj_ev, n - 3)
                w = win_tile(g)
                for k in range(KD):
                    wk = w[:, k, :]
                    if g < 2:
                        ins = mm(bank(m), wk[:, m * P:(m + 1) * P], h1t[:, k, :], start=(k == 0), stop=(k == KD - 1))
                    else:
                        ins = mm(bank(m), h1t[:, k, m * P:(m + 1) * P], wk, start=(k == 0), stop=(k == KD - 1))
                ins.then_inc(proj_mm, 1)
            modulation_row(5)
            pe.wait_ge(wsp_ok, 1)
            pe.wait_ge(vn_ok, 1)
            pe.wait_ge(proj_ev, 20)
            for g in range(GROUPS):
                mm(bank(g), wspt[:, g, :], v_sb[:, :, g * P:(g + 1) * P], start=True, stop=True).then_inc(mixed_mm, 1)
            pe.wait_ge(row_ok, 4)
            pe.wait_ge(og_ok, GROUPS)
            for k in range(4):
                for t in range(TT):
                    ins = transpose(bank(4 + k)[:, t * P:(t + 1) * P], u_sb[:, t, k * P:(k + 1) * P])
                ins.then_inc(og_tr, 1)
            pe.wait_ge(og_ev, 4)

            def scores_mm(h):
                r0, ct = HD * (h % 2), h // 2
                if h >= 2:
                    pe.wait_ge(a_ok, h - 1)
                z = zbank(h)
                for j in (0, 1, 3, 2):
                    mm(z[:, ZOFF[j]:ZOFF[j] + ZW[j]], kt[r0:r0 + HD, ct, j * P:(j + 1) * P],
                       qt[r0:r0 + HD, ct, j * P:T], start=(j != 3), stop=True, skip_group_check=True)
                for j in (0, 1, 3, 2):
                    ins = mm(z[:, ZOFF[j]:ZOFF[j] + P], identb[:, :], negmask[:, :], start=False, stop=True,
                             skip_group_check=True)
                ins.then_inc(z_mm, 1)

            def sums_mm(h):
                pe.wait_ge(sp_ok, h + 1)
                z = zbank(h)
                for j in range(TT):
                    for j2 in range(j, TT):
                        o = ZOFF[j] + P * (j2 - j)
                        ins = mm(z[:, o:o + ZW[j2]], (negtri if j == j2 else negones)[:, :],
                                 sp_sb[:, h % 2, ZOFF[j2]:ZOFF[j2] + ZW[j2]], start=False, stop=True,
                                 skip_group_check=True)
                ins.then_inc(x_mm, 1)

            def values_mm(h):
                r0, ct = HD * (h % 2), h // 2
                pe.wait_ge(a_ok, h + 1)
                if h % 2 == 0 and h >= 2:
                    pe.wait_ge(o_ev, ct)
                for j in range(TT):
                    ins = mm(bank(6)[r0:r0 + HD, j * P:T], vv[:, j, h * HD:(h + 1) * HD],
                             at_sb[:, h % 2, ZOFF[j]:ZOFF[j] + ZW[j]], start=(j == 0), stop=(j == TT - 1),
                             skip_group_check=True)
                ins.then_inc(o_mm, 1)

            def squares_mm(ct):
                pe.wait_ge(o_ev, ct + 1)
                for t in range(TT):
                    ins = mm(ps[:, 7 * BANK + 4 * t + ct:7 * BANK + 4 * t + ct + 1], sq[:, t * P:(t + 1) * P],
                             ones[:, 0:1], start=True, stop=True)
                ins.then_inc(ss_mm, 1)

            scores_mm(0)
            for h in range(HEADS):
                if h + 1 < HEADS:
                    scores_mm(h + 1)
                sums_mm(h)
                if h >= 1:
                    if h >= 3 and h % 2 == 1:
                        squares_mm((h - 3) // 2)
                    values_mm(h - 1)
            values_mm(HEADS - 1)
            squares_mm(3)

            def out_proj(t):
                b0 = (t % 2) * 4
                if t == 0:
                    pe.wait_ge(wo_in, 32)
                if t == 1:
                    pe.wait_ge(rs_sb_ok, 1)
                if t >= 2:
                    pe.wait_ge(h2_ev, t - 1)
                for br in range(2):
                    for hf in range(2):
                        for k in range(4):
                            ins = mm(bank(b0 + 2 * br + hf), mixt[:, 4 * br + k, t * P:(t + 1) * P],
                                     wo[:, 4 * br + k, hf * 512:(hf + 1) * 512], start=(k == 0), stop=(k == 3))
                ins.then_inc(wo_mm, 1)

            def h2_transposes(t):
                pe.wait_ge(h2_ok, t + 1)
                for k in range(KD):
                    ins = transpose(ps[:, (t % 2) * 4 * BANK + k * P:(t % 2) * 4 * BANK + (k + 1) * P],
                                    h2p[:, t % 2, k, :])
                ins.then_inc(h2_tr, 1)

            out_proj(0)
            out_proj(1)
            h2_transposes(0)
            out_proj(2)
            h2_transposes(1)
            out_proj(3)
            h2_transposes(2)
            h2_transposes(3)
            pe.wait_ge(h2_ev, TT)
            pe.wait_ge(wr_in, 16)
            for t in range(TT):
                for k in range(KD):
                    ins = mm(ps[:, 7 * BANK + t * E:7 * BANK + (t + 1) * E], h2t[:, k, t * P:(t + 1) * P],
                             wr[:, k, :], start=(k == 0), stop=(k == KD - 1))
            ins.then_inc(lg_mm, 1)

            def shared_up(t):
                if t == 0:
                    pe.wait_ge(wsgu_in, 32)
                if t >= 2:
                    pe.wait_ge(sact_ok, t - 1)
                for k in range(KD):
                    ins = mm(bank(t % 2), h2t[:, k, t * P:(t + 1) * P], wsgu[:, :, k, :],
                             start=(k == 0), stop=(k == KD - 1))
                ins.then_inc(sgu_mm, 1)

            def shared_down(t):
                pe.wait_ge(sact_ok, t + 1)
                for k in range(KF):
                    ins = transpose(bank(2)[:, k * P:(k + 1) * P], act_s[:, k, :])
                ins.then_inc(sat_tr, 1)
                pe.wait_ge(sat_ev, t + 1)
                if t == 0:
                    pe.wait_ge(wsd_in, 16)
                if t >= 1:
                    pe.wait_ge(sdn_ev, t)
                for hf in range(2):
                    for k in range(KF):
                        ins = mm(bank(3 + hf), sht[:, k, :], wsd[:, k, hf * 512:(hf + 1) * 512],
                                 start=(k == 0), stop=(k == KF - 1))
                ins.then_inc(sdn_mm, 1)

            shared_up(0)
            for t in range(TT):
                if t + 1 < TT:
                    shared_up(t + 1)
                shared_down(t)

            pe.wait_ge(sel_ok, 1)
            for t in range(TT):
                for t2 in range(t + 1):
                    mm(ps[:, 6 * BANK + t * E:6 * BANK + (t + 1) * E], (ustrb if t2 == t else onesb)[:, :],
                       selb[:, t2, :], start=(t2 == 0), stop=(t2 == t))
            for t in range(TT):
                ins = mm(ps[0:E, 5 * BANK:5 * BANK + 1], selb[:, t, :], onesb[:, 0:1],
                         start=(t == 0), stop=(t == TT - 1))
            ins.then_inc(cnt_mm, 1)
            pe.wait_ge(sdn_ev, TT)
            pe.wait_ge(ext_ok, 1)
            mm(ps[0:E, 3 * BANK:3 * BANK + 1], ustrb[0:E, 0:E], extb[:, :], start=True, stop=True)
            mm(ps[0:1, 3 * BANK + 1:3 * BANK + 2], extb[:, :], onesb[0:E, 0:1], start=True, stop=True)\
                .then_inc(start_mm, 1)
            for q, tab in enumerate((posm, gates, rank)):
                for t in range(TT):
                    ins = pe.transpose(ps[0:E, q * BANK + t * P:q * BANK + (t + 1) * P], tab[:, t, 0:E], ident[:, :])
            ins.then_inc(tab_tr, 1)
            pe.wait_ge(selx_ok, 1)
            pe.wait_ge(tab_ev, 3)
            mm(ps[0:1, 3 * BANK + 64:3 * BANK + 64 + OVER], iote[:, :], selx[:, :], start=True, stop=True)
            for q in range(3):
                for t in range(TT):
                    o = ps[:, 4 * BANK + (q * TT + t) * OVER:4 * BANK + (q * TT + t + 1) * OVER]
                    ins = mm(o, tabt[:, q, t * P:(t + 1) * P], selx[:, :], start=True, stop=(q != 0))
                    if q == 0:
                        ins = mm(o, ones[0:E, :], jm[:, :], start=False, stop=True)
            ins.then_inc(over_mm, 1)

            def indices(b):
                pe.wait_ge(onehot_ok, b + 1)
                pe.wait_ge(idx_ok, b)
                for t in range(TT):
                    v = (vtab[:, t, b, :] if isinstance(b, int) else
                         vtab[:, t, bass.ds(b, 1), :].rearrange("p b v -> p (b v)"))
                    ins = mm(ps[:, 7 * BANK:7 * BANK + VC], s_onehot[:, t, :], v, start=(t == 0), stop=(t == TT - 1))
                ins.then_inc(idx_mm, 1)

            def rows_in(b):
                pe.wait_ge(gathered, b * 16 + 16)
                pe.wait_ge(htlo_ok, b)
                for k in range(KD):
                    ins = transpose(ps[:, k * P:(k + 1) * P], hg[:, k, :])
                ins.then_inc(ht_tr, 1)

            def wpart(tile, slot, lo, n_, k):
                if n_ == 2:
                    v = tile[:, slot, 0:2, k * F:(k + 1) * F] if isinstance(slot, int) else \
                        tile[:, bass.ds(slot, 1), 0:2, k * F:(k + 1) * F].rearrange("p s g f -> p (s g) f")
                    return v
                return part(tile, slot, 2, k * 512, (k + 1) * 512)

            def gate_up(b, slot):
                pe.wait_ge(hi_ok, b * 3 + 2)
                pe.wait_ge(lo_dve, b * 3 + 2)
                pe.wait_ge(lo_pool, b * 3 + 2)
                pe.wait_ge(hthi_ok, b + 1)
                pe.wait_ge(htlo_ok, b + 1)
                for k in range(KD):
                    hi, lo = wpart(whi, slot, 0, 2, k), wpart(wlo, slot, 0, 2, k)
                    mm(bank(2), hthi[:, k, :], hi, start=(k == 0), stop=False)
                    mm(bank(2), hthi[:, k, :], lo, start=False, stop=False)
                    ins = mm(bank(2), htlo[:, k, :], hi, start=False, stop=(k == KD - 1))
                ins.then_inc(gu_mm, 1)

            def down(b, slot, first=False):
                pe.wait_ge(hi_ok, b * 3 + 3)
                pe.wait_ge(lo_dve, b * 3 + 3)
                pe.wait_ge(lo_pool, b * 3 + 3)
                pe.wait_ge(acthi_ok, b + 1)
                pe.wait_ge(actlo_ok, b + 1)
                if not first:
                    pe.wait_ge(y_ok, b)
                for k in range(KF):
                    for st, w in ((acthi, whi), (acthi, wlo), (actlo, whi)):
                        for hf in range(2):
                            ins = mm(bank(4 + hf), st[:, k, :], wpart(w, slot, 2, 1, 2 * k + hf),
                                     start=(k == 0 and st is acthi and w is whi),
                                     stop=(k == KF - 1 and st is actlo))
                ins.then_inc(dn_mm, 1)

            def acts_tr(b):
                pe.wait_ge(act_ok, b + 1)
                for k in range(KF):
                    ins = transpose(ps[:, 3 * BANK + k * P:3 * BANK + (k + 1) * P], act_s[:, k, :])
                ins.then_inc(at_tr, 1)

            def one(b, slot, prev, first):
                indices(b + 2)
                gate_up(b, slot)
                rows_in(b + 1)
                if first >= 1:
                    down(b - 1, prev, first == 1)
                acts_tr(b)

            pe.wait_ge(tables_ok, 1)
            pe.wait_ge(onehot_ok, 1)
            for t in range(TT):
                ins = mm(ps[:, 7 * BANK:7 * BANK + VC], s_onehot[:, t, :], vtab[:, t, 0, :],
                         start=(t == 0), stop=(t == TT - 1))
            ins.then_inc(idx_mm, 1)
            indices(1)
            pe.wait_ge(gathered, 16)
            for k in range(KD):
                ins = transpose(ps[:, k * P:(k + 1) * P], hg[:, k, :])
            ins.then_inc(ht_tr, 1)
            one(0, 0, 1, 0)
            one(1, 1, 0, 1)
            with pe.Fori(1, E // 2) as i:
                for s in range(2):
                    one(i * 2 + s, s, 1 - s, 2)
            n = pe.value_load(nover[0:1, 0:1], min_val=0, max_val=OVER)
            with pe.If(n > 0):
                with pe.Fori(E, n + E) as b:
                    one(b, b % 2, (b + 1) % 2, 2)
            down(n + (E - 1), (n + 1) % 2)

        @block.vector
        def _(v):
            V = nc.vector
            step = [0]

            def then(ins):
                step[0] += 1
                ins.then_inc(v_step, 1)
                v.wait_ge(v_step, step[0])

            sums = [0]
            vars_ = [0]

            def factor(st, width, c0=0, c1=TT, src=None, wait=True):
                if wait:
                    sums[0] += 1
                    v.wait_ge(sumsq, sums[0])
                vv_, rr, r = var[:, st, c0:c1], root[:, st, c0:c1], rs[:, st, c0:c1]
                V.tensor_scalar(vv_, stat[:, st, c0:c1] if src is None else src, 1.0 / width, EPS,
                                ALU.mult, ALU.add).then_inc(var_ok, 1)
                vars_[0] += 1
                v.wait_ge(root_ok, vars_[0])
                then(V.reciprocal(r, rr))
                then(V.tensor_tensor(nt[:, c0:c1], r, r, ALU.mult))
                then(V.tensor_tensor(nt[:, c0:c1], nt[:, c0:c1], vv_, ALU.mult))
                then(V.tensor_scalar(nt[:, c0:c1], nt[:, c0:c1], -0.5, 1.5, ALU.mult, ALU.add))
                then(V.tensor_tensor(r, r, nt[:, c0:c1], ALU.mult))

            factor(ST_X, D)
            for t in range(TT):
                V.tensor_scalar(z1[:, t].rearrange("p k q -> p q k"),
                                xs[:, t, :].rearrange("p (q k) -> p q k", k=KD), rs[:, ST_X, t:t + 1], None,
                                ALU.mult).then_inc(z_ok, 1)
            v.wait_ge(sc_ok, 1)

            def weigh(ch):
                if ch >= 2:
                    v.wait_ge(mod_mm, ch - 1)
                for q in range(4):
                    n = 4 * ch + q
                    v.wait_ge(ada_in[n % 2], 16 * (n // 2 + 1))
                    for r in range(2):
                        k = 2 * q + r
                        src = ada[:, n % 2, r, :]
                        if k == 0:
                            ins = V.tensor_scalar(acc[:, ch % 2, :], src, sc_col[:, 0:1], None, ALU.mult)
                        else:
                            ins = V.scalar_tensor_tensor(out=acc[:, ch % 2, :], in0=src, scalar=sc_col[:, k:k + 1],
                                                         in1=acc[:, ch % 2, :], op0=ALU.mult, op1=ALU.add)
                        if r == 0:
                            then(ins)
                        else:
                            ins.then_inc(ada_used, 1)
                            v.wait_ge(ada_used, n + 1)
                v.sem_inc(acc_ok, 1)

            weigh(0)
            weigh(1)
            v.wait_ge(vec_in, 16 * 13)
            v.wait_ge(mod_mm, 2)
            m = ps[:, 6 * BANK:6 * BANK + 2 * KD]
            then(V.scalar_tensor_tensor(out=a1c[:, :], in0=m[:, 0:KD], scalar=1.0, in1=bsc[:, :],
                                        op0=ALU.add, op1=ALU.add))
            then(V.tensor_tensor(a1c[:, :], a1c[:, :], gpm[:, :], ALU.mult))
            V.tensor_tensor(b1c[:, :], m[:, KD:2 * KD], bsh[:, :], ALU.add).then_inc(ab_ok, 1)
            v.wait_ge(ab_ok, 1)
            for k in range(1, KD, 2):
                v.wait_ge(h1_tr, k + 1)
                V.tensor_scalar(h1t[:, k, :], bank(k % 6), a1c[:, k:k + 1], b1c[:, k:k + 1],
                                ALU.mult, ALU.add).then_inc(h1_dve, 1)
            v.wait_ge(wsp_tr, 1)
            then(V.tensor_copy(wspt[:, :, :], bank(4).rearrange("p (g q) -> p g q", g=GROUPS)))
            V.memset(wspt[CHUNK:P, :, 0:CHUNK], 0.0).then_inc(wsp_ok, 1)

            def mod_row(ch, dst, gain, plus_one):
                v.wait_ge(mod_mm, ch + 1)
                if plus_one:
                    ins = V.scalar_tensor_tensor(out=dst[:, :], in0=bank(6, 2), scalar=1.0, in1=dst[:, :],
                                                 op0=ALU.add, op1=ALU.add)
                else:
                    ins = V.tensor_tensor(dst[:, :], bank(6, 2), dst[:, :], ALU.add)
                if gain:
                    then(ins)
                    v.wait_ge(grow_in, 16 * gain)
                    ins = V.tensor_tensor(dst[:, :], dst[:, :], grow[:, :], ALU.mult)
                ins.then_inc(row_ok, 1)

            weigh(2)
            mod_row(2, ga1, 1, False)
            weigh(3)
            mod_row(3, a2, 2, True)
            weigh(4)
            mod_row(4, b2, 0, False)
            v.wait_ge(proj_ev, 16)
            then(V.tensor_scalar(nt[:, :], stat[:, ST_VS, :], -1.0 / DG, None, ALU.mult))
            for t in range(TT):
                ins = V.tensor_scalar(v_sb[:, t, :], v_sb[:, t, :], nt[:, t:t + 1], None, ALU.add)
            ins.then_inc(vmean_ok, 1)
            weigh(5)
            factor(ST_V, DG)
            for t in range(TT):
                then(V.scalar_tensor_tensor(out=v_sb[:, t, :], in0=v_sb[:, t, :], scalar=rs[:, ST_V, t:t + 1],
                                            in1=lng[:, :], op0=ALU.mult, op1=ALU.mult))
                ins = V.tensor_tensor(v_sb[:, t, :], v_sb[:, t, :], lnb[:, :], ALU.add)
                ins.then_inc(vn_ok, 1) if t == TT - 1 else then(ins)
            mod_row(5, ga2, 3, False)
            for g in range(GROUPS):
                v.wait_ge(mixed_mm, g + 1)
                V.scalar_tensor_tensor(out=u_sb[:, :, g * P:(g + 1) * P],
                                       in0=bank(g).rearrange("p (t q) -> p t q", t=TT), scalar=bsp[:, g:g + 1],
                                       in1=u_sb[:, :, g * P:(g + 1) * P], op0=ALU.add, op1=ALU.mult)\
                    .then_inc(og_ok, 1)
            factor(ST_G, DG)
            v.sem_inc(rs_g_ok, 1)
            for h in range(HEADS + 1):
                if h < HEADS:
                    v.wait_ge(z_mm, h + 1)
                    if h >= 1:
                        v.wait_ge(sp_ok, h)
                    V.tensor_scalar(ta[:, :], zbank(h), CAP, None, ALU.min).then_inc(cap_ok, 1)
                    v.wait_ge(ln_ok, h + 1)
                    if h >= 2:
                        v.wait_ge(x_mm, h - 1)
                    V.tensor_tensor(sp_sb[:, h % 2, :], zbank(h), ta[:, :], ALU.max).then_inc(sp_ok, 1)
            v.wait_ge(ss_mm, 4)
            then(V.tensor_reduce(stat[:, ST_X, :],
                                 ps[:, 7 * BANK:7 * BANK + 16].rearrange("p (t c) -> p t c", t=TT), AX_X, ALU.add))
            factor(ST_X, DG, wait=False)
            v.sem_inc(rs_sb_ok, 1)
            for t in range(TT):
                o = o_sb[:, t % 2, :]
                pb = ps[:, ((t % 2) * 4 + 2) * BANK:((t % 2) * 4 + 4) * BANK]
                v.wait_ge(wo_a, t + 1)
                V.scalar_tensor_tensor(out=o, in0=pb, scalar=rs[:, ST_X, t:t + 1], in1=o,
                                       op0=ALU.mult, op1=ALU.add).then_inc(wo_o, 1)
                factor(ST_S, D, t, t + 1)
                then(V.scalar_tensor_tensor(out=o, in0=o, scalar=rs[:, ST_S, t:t + 1], in1=ga1[:, :],
                                            op0=ALU.mult, op1=ALU.mult))
                V.tensor_tensor(xs[:, t, :], xs[:, t, :], o, ALU.add).then_inc(wo_x, 1)
                factor(ST_O, D, t, t + 1)
                then(V.scalar_tensor_tensor(out=o, in0=xs[:, t, :], scalar=rs[:, ST_O, t:t + 1], in1=a2[:, :],
                                            op0=ALU.mult, op1=ALU.mult))
                if t >= 2:
                    v.wait_ge(h2_out[t % 2], 16)
                    v.wait_ge(h2_tr, t - 1)
                V.tensor_tensor(h2p[:, t % 2].rearrange("p k q -> p q k"),
                                o.rearrange("p (q k) -> p q k", k=KD),
                                b2[:, :].rearrange("p (q k) -> p q k", k=KD), ALU.add).then_inc(h2_ok, 1)

            def shared_act(t):
                v.wait_ge(ssg_ok, t + 1)
                if t >= 1:
                    v.wait_ge(sat_tr, t)
                V.tensor_tensor(act_s[:, :, :].rearrange("p k q -> p q k"),
                                bank(t % 2)[:, F:2 * F].rearrange("p (q k) -> p q k", k=KF),
                                sg[:, :].rearrange("p (q k) -> p q k", k=KF), ALU.mult).then_inc(sact_ok, 1)

            v.wait_ge(sig_ok, 1)
            then(V.tensor_tensor(biased[:, :, :], scores[:, :, :],
                                 rb[:, :].unsqueeze(1).to_broadcast([P, TT, E]), ALU.add))
            for t in range(TT):
                for g in range(EG):
                    ins = V.max(top2[:, t, g, :], biased[:, t, g * EPG:(g + 1) * EPG])
            then(ins)
            then(V.tensor_tensor(gs[:, :, :], top2[:, :, :, 0], top2[:, :, :, 1], ALU.add))
            shared_act(0)
            mine = gs[:, :, :].unsqueeze(3).to_broadcast([P, TT, EG, EG])
            other = gs[:, :, :].unsqueeze(2).to_broadcast([P, TT, EG, EG])
            then(V.memset(gtri[:, :, :], 0.0))
            for g in range(1, EG):
                ins = V.memset(gtri[:, g, 0:g], 1.0)
            then(ins)
            then(V.tensor_tensor(gcmp[:, :, :, :], other, mine, ALU.is_gt))
            then(V.tensor_tensor(gcmp2[:, :, :, :], other, mine, ALU.is_equal))
            for t in range(TT):
                ins = V.tensor_tensor(gcmp2[:, t], gcmp2[:, t], gtri[:, :, :], ALU.mult)
            then(ins)
            then(V.tensor_tensor(gcmp[:, :, :, :], gcmp[:, :, :, :], gcmp2[:, :, :, :], ALU.add))
            then(V.tensor_reduce(gm[:, :, :], gcmp[:, :, :, :], AX_X, ALU.add))
            then(V.tensor_scalar(gm[:, :, :], gm[:, :, :], float(TOPG), None, ALU.is_lt))
            shared_act(1)
            gmb = gm[:, :, :].unsqueeze(3).to_broadcast([P, TT, EG, EPG])
            then(V.tensor_tensor(masked[:, :, :].rearrange("p t (g e) -> p t g e", g=EG),
                                 biased[:, :, :].rearrange("p t (g e) -> p t g e", g=EG), gmb, ALU.mult))
            then(V.tensor_scalar(gm[:, :, :], gm[:, :, :], -NEG, NEG, ALU.mult, ALU.add))
            then(V.tensor_tensor(masked[:, :, :].rearrange("p t (g e) -> p t g e", g=EG),
                                 masked[:, :, :].rearrange("p t (g e) -> p t g e", g=EG), gmb, ALU.add))
            for t in range(TT):
                ins = V.max(top8[:, t, :], masked[:, t, :])
            then(ins)
            for t in range(TT):
                ins = V.match_replace(picked[:, t, :], top8[:, t, :], masked[:, t, :], 3.0e38)
            then(ins)
            then(V.tensor_tensor(sel[:, :, :], picked[:, :, :], masked[:, :, :], ALU.not_equal))
            V.tensor_copy(selb[:, :, :], sel[:, :, :]).then_inc(sel_ok, 1)
            shared_act(2)
            then(V.tensor_tensor(gates[:, :, 0:E], scores[:, :, :], sel[:, :, :], ALU.mult))
            then(V.tensor_reduce(wsum[:, :], gates[:, :, 0:E], AX_X, ALU.add))
            then(V.reciprocal(wsum[:, :], wsum[:, :]))
            for t in range(TT):
                ins = V.tensor_scalar(gates[:, t, 0:E], gates[:, t, 0:E], wsum[:, t:t + 1], SCALE_ROUTED,
                                      ALU.mult, ALU.mult)
            then(ins)
            for t in range(TT):
                ins = V.tensor_tensor_scan(rank[:, t, :], ones[:, 0:E], sel[:, t, :], 0.0, ALU.mult, ALU.add)
            then(ins)
            then(V.tensor_tensor(rank[:, :, :], rank[:, :, :], sel[:, :, :], ALU.subtract))
            then(V.tensor_scalar(rank[:, :, :], rank[:, :, :], float(T), None, ALU.mult))
            shared_act(3)
            v.wait_ge(cnt_mm, 1)
            then(V.scalar_tensor_tensor(out=posm[:, :, :],
                                        in0=ps[:, 6 * BANK:6 * BANK + TT * E].rearrange("p (t e) -> p t e", t=TT),
                                        scalar=1.0, in1=sel[:, :, :], op0=ALU.add, op1=ALU.mult))
            cnt = ps[0:E, 5 * BANK:5 * BANK + 1]
            then(V.tensor_scalar(ext[:, 0:1], cnt, 128.5, None, ALU.is_gt))
            for lim in (256.5, 384.5):
                then(V.scalar_tensor_tensor(out=ext[:, 0:1], in0=cnt, scalar=lim, in1=ext[:, 0:1],
                                            op0=ALU.is_gt, op1=ALU.add))
            V.tensor_copy(extb[:, :], ext[:, 0:1]).then_inc(ext_ok, 1)
            v.wait_ge(const_ok, 2)
            V.tensor_scalar(posb[:, :, 0:E], posm[:, :, :], -1.0, None, ALU.add)
            v.wait_ge(start_mm, 1)
            then(V.tensor_copy(ext[:, 1:2], ps[0:E, 3 * BANK:3 * BANK + 1]))
            then(V.tensor_copy(nover[:, :], ps[0:1, 3 * BANK + 1:3 * BANK + 2]))
            then(V.tensor_scalar(tmp32[:, :], iot32[:, :], ext[:, 1:2], None, ALU.subtract))
            then(V.tensor_scalar(selx[:, :], tmp32[:, :], 0.0, None, ALU.is_ge))
            then(V.scalar_tensor_tensor(out=selx[:, :], in0=tmp32[:, :], scalar=ext[:, 0:1], in1=selx[:, :],
                                        op0=ALU.is_lt, op1=ALU.mult))
            then(V.scalar_tensor_tensor(out=jm[:, :], in0=tmp32[:, :], scalar=1.0, in1=selx[:, :],
                                        op0=ALU.add, op1=ALU.mult))
            then(V.tensor_scalar(jm[:, :], jm[:, :], -float(P), None, ALU.mult))
            v.sem_inc(selx_ok, 1)
            v.wait_ge(over_mm, 1)
            ov = ps[:, 4 * BANK:4 * BANK + 3 * TT * OVER].rearrange("p (q t o) -> p q t o", q=3, t=TT)
            V.tensor_scalar(posb[:, :, E:E + OVER], ov[:, 0], -1.0, None, ALU.add)
            V.tensor_copy(vtab[:, :, E:E + OVER, 2], ov[:, 2])
            V.tensor_copy(vtab[:, :, 0:E, 2], rank[:, :, :])
            then(V.tensor_copy(eid[:, :], ps[0:1, 3 * BANK + 64:3 * BANK + 64 + OVER]))
            then(V.tensor_copy(gates[:, :, E:E + OVER], ov[:, 1]))
            for part_ in range(3):
                then(V.tensor_copy(vtab[:, :, :, 3 + part_], gates[:, :, :]))
                if part_ < 2:
                    then(V.tensor_tensor(gates[:, :, :], gates[:, :, :], vtab[:, :, :, 3 + part_], ALU.subtract))
            v.wait_ge(ysh_out, 16 * TT)
            then(V.memset(hg[:, :, :], 0.0))
            v.sem_inc(hg_zero, 1)
            v.sem_inc(tables_ok, 1)

            PER = 6

            def col(tile, b, *rest):
                if isinstance(b, int):
                    return tile[:, b:b + 1]
                return tile[:, bass.ds(b, 1)]

            def onehot(b, wait=True):
                if wait:
                    v.wait_ge(idx_mm, b)
                for t in range(TT):
                    pcol = posb[:, t, b:b + 1] if isinstance(b, int) else posb[:, t, bass.ds(b, 1)]
                    ins = V.tensor_scalar(s_onehot[:, t, :], iotab[:, :], pcol, None, ALU.is_equal)
                ins.then_inc(onehot_ok, 1)

            def tables(b):
                v.wait_ge(idx_mm, b + 1)
                k = [0]

                def chained(ins):
                    k[0] += 1
                    ins.then_inc(v_loop, 1)
                    v.wait_ge(v_loop, b * PER + k[0])

                chained(V.tensor_reduce(pair[:, :], ps[:, 7 * BANK:7 * BANK + VC].rearrange("p (a c) -> p a c", a=2),
                                        AX_X, ALU.add))
                chained(V.tensor_scalar(inval[:, :], pair[:, 0:1], 0.0, float(BIG_ROW), ALU.is_equal, ALU.mult))
                chained(V.scalar_tensor_tensor(out=desti[:, :], in0=pair[:, 0:1], scalar=-1.0, in1=inval[:, :],
                                               op0=ALU.add, op1=ALU.add))
                chained(V.tensor_copy(col(gater, b), pair[:, 1:2]))
                chained(V.tensor_copy(col(destr, b), desti[:, :]))
                if not (isinstance(b, int) and b == 0):
                    v.wait_ge(gathered, b * 16)
                chained(V.tensor_scalar(idxg[:, :], desti[:, :], (BIG_ROW >> 1) | (T - 1), None, ALU.bitwise_and))
                assert k[0] == PER
                v.sem_inc(idx_ok, 1)

            def low(b, wslot, rslot, piece):
                v.wait_ge(hi_ok, b * 3 + (piece + 1))
                c1 = 2048 - POOL_K * 256
                V.tensor_tensor(part(wlo, wslot, piece, 0, c1), raw[:, rslot, piece, 0:c1],
                                part(whi, wslot, piece, 0, c1).bitcast(F32), ALU.subtract).then_inc(lo_dve, 1)

            def times_up(b):
                v.wait_ge(silu_ok, b + 1)
                if not (isinstance(b, int) and b == 0):
                    v.wait_ge(at_tr, b)
                V.scalar_tensor_tensor(out=act_s[:, :, :].rearrange("p k q -> p q k"),
                                       in0=sg[:, :].rearrange("p (q k) -> p q k", k=KF), scalar=col(gater, b),
                                       in1=bank(2)[:, F:2 * F].rearrange("p (q k) -> p q k", k=KF),
                                       op0=ALU.mult, op1=ALU.mult).then_inc(act_ok, 1)

            def ht_low(b):
                v.wait_ge(hthi_ok, b + 1)
                if not (isinstance(b, int) and b == 0):
                    v.wait_ge(gu_mm, b)
                V.tensor_tensor(htlo[:, :, :], bank(0, 2).rearrange("p (k q) -> p k q", k=KD),
                                hthi[:, :, :].bitcast(F32), ALU.subtract).then_inc(htlo_ok, 1)

            def acts_split(b):
                v.wait_ge(at_tr, b + 1)
                if not (isinstance(b, int) and b == 0):
                    v.wait_ge(dn_mm, b)
                src = bank(3)[:, 0:F].rearrange("p (k q) -> p k q", k=KF)
                V.tensor_copy(acthi[:, :, :], src).then_inc(acthi_ok, 1)
                v.wait_ge(acthi_ok, b + 1)
                V.tensor_tensor(actlo[:, :, :], src, acthi[:, :, :].bitcast(F32), ALU.subtract).then_inc(actlo_ok, 1)

            def rows_of(b):
                if not (isinstance(b, int) and b == 0):
                    v.wait_ge(scattered, b * 16)
                V.tensor_copy(idxs[:, :], col(destr, b)).then_inc(idxs_ok, 1)

            def one(b, wslot, rslot, first):
                if first >= 2:
                    v.wait_ge(gu_mm, b - 1)
                low(b, wslot, rslot, 0)
                low(b, wslot, rslot, 1)
                if first >= 1:
                    times_up(b - 1)
                ht_low(b)
                onehot(b + 2)
                tables(b + 1)
                if first >= 2:
                    v.wait_ge(dn_mm, b - 1)
                low(b, wslot, rslot, 2)
                if first >= 1:
                    acts_split(b - 1)
                if first >= 2:
                    rows_of(b - 2)

            onehot(0, wait=False)
            tables(0)
            onehot(1)
            one(0, 0, 0, 0)
            one(1, 1, 1, 1)
            one(2, 0, 0, 2)
            one(3, 1, 1, 2)
            with v.Fori(2, E // 2) as i:
                for s in range(2):
                    one(i * 2 + s, s, s, 2)
            n = v.value_load(nover[0:1, 0:1], min_val=0, max_val=OVER)
            with v.If(n > 0):
                with v.Fori(E, n + E) as b:
                    one(b, b % 2, 0, 2)
            times_up(n + (E - 1))
            acts_split(n + (E - 1))
            rows_of(n + (E - 2))
            rows_of(n + (E - 1))

            for t in range(TT):
                v.wait_ge(y_in[t], 16)
                for r in range(1, 9):
                    ins = V.tensor_tensor(yall[:, t, 0, :], yall[:, t, 0, :], yall[:, t, r, :], ALU.add)
                    ins.then_inc(ysum_ok, 1) if r == 8 else then(ins)
                factor(ST_S, D, t, t + 1)
                then(V.scalar_tensor_tensor(out=yall[:, t, 0, :], in0=yall[:, t, 0, :], scalar=rs[:, ST_S, t:t + 1],
                                            in1=ga2[:, :], op0=ALU.mult, op1=ALU.mult))
                V.tensor_tensor(xs[:, t, :], xs[:, t, :], yall[:, t, 0, :], ALU.add).then_inc(out_ok, 1)


_INS = ['x', 'c', 'w_ada', 'b_ada', 'g_pre_mix', 'w_in', 'ln_sgu_g', 'ln_sgu_b', 'w_spatial', 'b_spatial',
        'g_branch', 'w_out', 'g_post_mix', 'g_pre_ffn', 'w_router', 'router_bias', 'w_gate', 'w_up',
        'w_down', 'ws_gate', 'ws_up', 'ws_down', 'g_post_ffn']


def kernel(**inputs):
    import numpy as _np
    import concourse.bacc as _bacc
    from concourse import mybir as _mybir
    from concourse.bass_utils import run_bass_kernel_spmd as _run

    nc = _bacc.Bacc("TRN2", target_bir_lowering=False, num_devices=1)
    arrays, args = {}, []
    for name in _INS:
        a = _np.ascontiguousarray(inputs[name])
        a = a.reshape(a.shape[1:])
        arrays[f"in_{name}_dram"] = a
        args.append(nc.dram_tensor(f"in_{name}_dram", a.shape, _mybir.dt.from_np(a.dtype),
                                   kind="ExternalInput").ap())
    args.append(nc.dram_tensor("out_0_dram", (T, D), _mybir.dt.float32, kind="ExternalOutput").ap())
    block_kernel(nc, *args)
    r = _run(nc, [arrays], core_ids=[0])
    return r.results[0]["out_0_dram"].reshape(1, T, D)
```

```python
from contextlib import ExitStack

import concourse.bass as bass
from concourse import mybir

F32 = mybir.dt.float32
F32R = mybir.dt.float32r
BF16 = mybir.dt.bfloat16
I32 = mybir.dt.int32
U32 = mybir.dt.uint32
ALU = mybir.AluOpType
ACT = mybir.ActivationFunctionType
AX_X = mybir.AxisListType.X

P = 128
D = 1024
T = 512
TT = T // P
KD = D // P
DG = 512
GROUPS = 4
HEADS = 8
HD = 64
CHUNK = 64
E = 64
TOPK = 8
EG = 8
EPG = E // EG
TOPG = 4
F = 256
KF = F // P
SCALE_ROUTED = 2.5
EPS = 1e-6
NEG = -1.0e30
CAP = 40.0
BANK = 512
OVER = TOPK * T // P
COLS = E + OVER + 2
VC = 6
BIG_ROW = 1 << 17
POOL_K = 2


def block_kernel(nc, x, c, w_ada, b_ada, g_pre_mix, w_in, ln_sgu_g, ln_sgu_b, w_spatial, b_spatial,
                 g_branch, w_out, g_post_mix, g_pre_ffn, w_router, router_bias, w_gate, w_up,
                 w_down, ws_gate, ws_up, ws_down, g_post_ffn, out):
    with ExitStack() as ctx:
        def sem(name):
            return ctx.enter_context(nc.semaphore(name))

        base = 16512

        def at(name, shape, dt, off):
            return nc.alloc_sbuf_tensor_at(name, shape, dt, offset=base + off)

        KB = 1024
        raw = at("raw", [P, 2, 3, 2048], F32, 0)
        whi = at("whi", [P, 2, 3, 2048], F32R, 48 * KB)
        wlo = at("wlo", [P, 2, 3, 2048], F32R, 96 * KB)
        yall = at("yall", [P, TT, 9, D], F32, 0)
        ada = at("ada", [P, 2, 2, D], F32, 0)
        acc = at("acc", [P, 2, D], F32, 16 * KB)
        grow = at("grow", [P, D], F32, 24 * KB)
        lng = at("lng", [P, DG], F32, 28 * KB)
        lnb = at("lnb", [P, DG], F32, 30 * KB)
        win3 = at("win3", [P, KD, 512], F32, 32 * KB)
        win012 = at("win012", [P, 3, KD, 512], F32, 48 * KB)
        h1t = at("h1t", [P, KD, T], F32, 96 * KB)
        mixt = at("mixt", [P, KD, T], F32, 96 * KB)
        qt = at("qt", [P, 4, T], F32, 112 * KB)
        kt = at("kt", [P, 4, T], F32, 120 * KB)
        h2t = at("h2t", [P, KD, T], F32, 120 * KB)
        vv = at("vv", [P, TT, 512], F32, 128 * KB)
        wsd = at("wsd", [P, KF, D], F32, 40 * KB)
        ga1 = at("ga1", [P, D], F32, 136 * KB)
        a2 = at("a2", [P, D], F32, 140 * KB)
        wo = at("wo", [P, KD, D], F32, 48 * KB)
        beta = at("beta", [P, 2, 1280], F32, 32 * KB)
        rest = at("rest", [P, 2, 1280], F32, 80 * KB)
        wsgu = at("wsgu", [P, 2, KD, F], F32, 80 * KB)
        xs = at("xs", [P, TT, D], F32, 144 * KB)
        z1 = at("z1", [P, TT, KD, P], F32, 160 * KB)
        u_sb = at("u_sb", [P, TT, DG], F32, 160 * KB)
        v_sb = at("v_sb", [P, TT, DG], F32, 168 * KB)
        sq = at("sq", [P, T], F32, 168 * KB)
        o_sb = at("o_sb", [P, 2, D], F32, 160 * KB)
        h2p = at("h2p", [P, 2, KD, P], F32, 168 * KB)
        hg = at("hg", [P, KD, P], F32, 160 * KB)
        hthi = at("hthi", [P, KD, P], F32R, 164 * KB)
        htlo = at("htlo", [P, KD, P], F32R, 168 * KB)
        ysb = at("ysb", [P, D], F32, 172 * KB)
        b2 = at("b2", [P, D], F32, 176 * KB)
        ga2 = at("ga2", [P, D], F32, 180 * KB)
        junk = at("junk", [P, D], F32, 184 * KB)
        at_sb = at("at_sb", [P, 2, 1280], F32, 184 * KB)
        scores = at("scores", [P, TT, E], F32, 184 * KB)
        biased = at("biased", [P, TT, E], F32, 185 * KB)
        masked = at("masked", [P, TT, E], F32, 186 * KB)
        picked = at("picked", [P, TT, E], F32, 187 * KB)
        sel = at("sel", [P, TT, E], F32, 188 * KB)
        gates = at("gates", [P, TT, E], F32, 189 * KB)
        posm = at("posm", [P, TT, E], F32, 191 * KB)
        rank = at("rank", [P, TT, E], F32, 192 * KB)
        selb = at("selb", [P, TT, E], BF16, 193 * KB)
        small0 = 194 * KB
        smalls = [small0]

        def small(name, shape, dt):
            n = 1
            for s in shape[1:]:
                n *= s
            n *= 2 if dt == BF16 else 4
            t = at(name, shape, dt, smalls[0])
            smalls[0] += -(-n // 32) * 32
            return t

        posb = small("posb", [P, TT, COLS], F32)
        vtab = small("vtab", [P, TT, COLS, VC], BF16)
        restart = at("restart", [P, 1280], F32, 90 * KB)
        negmask = at("negmask", [P, P], BF16, small0 + 1024)
        wsp = at("wsp", [P, GROUPS, P], F32, small0 + 1280)
        wspt = at("wspt", [P, GROUPS, P], F32, small0 + 3328)
        ident = small("ident", [P, P], F32)
        identb = small("identb", [P, P], BF16)
        ones = small("ones", [P, P], F32)
        ustrb = small("ustrb", [P, P], BF16)
        onesb = small("onesb", [P, P], BF16)
        iotab = small("iotab", [P, P], BF16)
        s_onehot = at("s_onehot", [P, TT, P], BF16, 186 * KB)
        sg = small("sg", [P, F], F32)
        act_s = small("act_s", [P, KF, P], F32)
        acthi = at("acthi", [P, KF, P], F32R, 184 * KB)
        actlo = at("actlo", [P, KF, P], F32R, 185 * KB)
        sht = at("sht", [P, 2, KF, P], F32, 136 * KB)
        ysh = at("ysh", [P, 2, D], F32, 72 * KB)
        c_col = small("c_col", [P, KD], F32)
        sc_col = small("sc_col", [P, KD], F32)
        a1c = small("a1c", [P, KD], F32)
        b1c = small("b1c", [P, KD], F32)
        bsc = small("bsc", [P, KD], F32)
        bsh = small("bsh", [P, KD], F32)
        gpm = small("gpm", [P, KD], F32)
        gb = small("gb", [P, KD], F32)
        bsp = small("bsp", [P, GROUPS], F32)
        rb = small("rb", [P, E], F32)
        wr = at("wr", [P, KD, E], F32, 36 * KB)
        stat = small("stat", [P, 6, TT], F32)
        var = small("var", [P, 6, TT], F32)
        root = small("root", [P, 6, TT], F32)
        rs = small("rs", [P, 6, TT], F32)
        nt = small("nt", [P, TT], F32)
        ss16 = small("ss16", [P, TT, 4], F32)
        top2 = at("top2", [P, TT, EG, 8], F32, 186 * KB)
        gs = small("gs", [P, TT, EG], F32)
        gcmp = at("gcmp", [P, TT, EG, EG], F32, 187 * KB)
        gcmp2 = at("gcmp2", [P, TT, EG, EG], F32, 188 * KB)
        gtri = at("gtri", [P, EG, EG], F32, 193 * KB + 512)
        gm = small("gm", [P, TT, EG], F32)
        top8 = small("top8", [P, TT, 8], F32)
        wsum = small("wsum", [P, TT], F32)
        ext = small("ext", [E, 2], F32)
        extb = small("extb", [E, 1], BF16)
        iot32 = small("iot32", [E, OVER], F32)
        iote = small("iote", [E, 1], F32)
        tmp32 = small("tmp32", [E, OVER], F32)
        selx = small("selx", [E, OVER], F32)
        jm = small("jm", [E, OVER], F32)
        nover = small("nover", [1, 1], I32)
        eid = small("eid", [1, OVER], I32)
        offs = small("offs", [P, OVER], F32)
        pair = small("pair", [P, 2], F32)
        inval = small("inval", [P, 1], F32)
        desti = small("desti", [P, 1], I32)
        idxg = small("idxg", [P, 1], I32)
        idxs = small("idxs", [P, 1], I32)
        vcur = small("vcur", [P, TT, VC], BF16)
        destr = at("destr", [P, COLS], I32, 187 * KB)
        gater = at("gater", [P, COLS], F32, 187 * KB + 512)
        assert base + smalls[0] <= nc.sbuf_usable_end, (base + smalls[0], nc.sbuf_usable_end)

        ps = ctx.enter_context(nc.psum_tensor("ps", [P, 8 * BANK], F32))

        def bank(b, n=1):
            return ps[:, b * BANK:(b + n) * BANK]

        h_rows = nc.dram_tensor("h_rows", [T, D], F32, kind="Internal").ap()
        y_rows = nc.dram_tensor("y_rows", [9 * T, D], F32, kind="Internal").ap()

        c_in = sem("c_in")
        x_in = [sem(f"x_in{t}") for t in range(TT)]
        vec_in = sem("vec_in")
        grow_in = sem("grow_in")
        ada_in = [sem(f"ada_in{s}") for s in range(2)]
        ada_used = sem("ada_used")
        win_in = [sem(f"win_in{i}") for i in range(5)]
        wo_in = sem("wo_in")
        wsgu_in = sem("wsgu_in")
        wsd_in = sem("wsd_in")
        wr_in = sem("wr_in")
        const_ok = sem("const_ok")
        pool_step = sem("pool_step")
        v_step = sem("v_step")
        a_step = sem("a_step")
        sc_ok = sem("sc_ok")
        sumsq = sem("sumsq")
        var_ok = sem("var_ok")
        root_ok = sem("root_ok")
        rs_g_ok = sem("rs_g_ok")
        rs_sb_ok = sem("rs_sb_ok")
        z_ok = sem("z_ok")
        acc_ok = sem("acc_ok")
        mod_mm = sem("mod_mm")
        row_ok = sem("row_ok")
        ab_ok = sem("ab_ok")
        h1_tr = sem("h1_tr")
        h1_act = sem("h1_act")
        h1_dve = sem("h1_dve")
        wsp_tr = sem("wsp_tr")
        wsp_ok = sem("wsp_ok")
        proj_mm = sem("proj_mm")
        proj_ev = sem("proj_ev")
        vmean_ok = sem("vmean_ok")
        vn_ok = sem("vn_ok")
        mixed_mm = sem("mixed_mm")
        og_ok = sem("og_ok")
        og_tr = sem("og_tr")
        og_ev = sem("og_ev")
        z_mm = sem("z_mm")
        restart_ok = sem("restart_ok")
        beta_ok = sem("beta_ok")
        att_ok = sem("att_ok")
        att_tr = sem("att_tr")
        a_ok = sem("a_ok")
        o_mm = sem("o_mm")
        o_ev = sem("o_ev")
        ss_mm = sem("ss_mm")
        wo_mm = sem("wo_mm")
        wo_a = sem("wo_a")
        wo_o = sem("wo_o")
        wo_x = sem("wo_x")
        h2_ok = sem("h2_ok")
        h2_out = [sem(f"h2_out{s}") for s in range(2)]
        h2_tr = sem("h2_tr")
        h2_ev = sem("h2_ev")
        lg_mm = sem("lg_mm")
        sig_ok = sem("sig_ok")
        sgu_mm = sem("sgu_mm")
        ssg_ok = sem("ssg_ok")
        sact_ok = sem("sact_ok")
        sat_tr = sem("sat_tr")
        sat_ev = sem("sat_ev")
        sdn_mm = sem("sdn_mm")
        sdn_ev = sem("sdn_ev")
        ysh_out = [sem(f"ysh_out{s}") for s in range(2)]
        sel_ok = sem("sel_ok")
        cnt_mm = sem("cnt_mm")
        count_mm = sem("count_mm")
        ext_ok = sem("ext_ok")
        start_mm = sem("start_mm")
        selx_ok = sem("selx_ok")
        over_mm = sem("over_mm")
        over_ok = sem("over_ok")
        fill_ok = sem("fill_ok")
        w_in_sem = [[sem(f"w_in{s}{p}") for p in range(3)] for s in range(2)]
        wx_in = [sem(f"wx_in{p}") for p in range(3)]
        hi_ok = sem("hi_ok")
        lo_dve = sem("lo_dve")
        lo_pool = sem("lo_pool")
        onehot_ok = sem("onehot_ok")
        idx_mm = sem("idx_mm")
        idx_ok = sem("idx_ok")
        gather_go = sem("gather_go")
        scatter_go = sem("scatter_go")
        gathered = sem("gathered")
        ht_tr = sem("ht_tr")
        hthi_ok = sem("hthi_ok")
        htlo_ok = sem("htlo_ok")
        gu_mm = sem("gu_mm")
        silu_ok = sem("silu_ok")
        act_ok = sem("act_ok")
        at_tr = sem("at_tr")
        acthi_ok = sem("acthi_ok")
        actlo_ok = sem("actlo_ok")
        dn_mm = sem("dn_mm")
        y_ok = sem("y_ok")
        idxs_ok = sem("idxs_ok")
        scattered = sem("scattered")
        v_loop = sem("v_loop")
        y_in = [sem(f"y_in{t}") for t in range(TT)]
        ysum_ok = sem("ysum_ok")
        out_ok = sem("out_ok")
        out_done = sem("out_done")

        ada_v = w_ada.rearrange("(p k) n -> p k n", k=KD)
        win_v = w_in.rearrange("(p k) n -> p k n", k=KD)
        wo_v = w_out.rearrange("(k p) n -> p k n", p=P)
        wg_v = w_gate.rearrange("e (p k) f -> e p (k f)", k=KD)
        wu_v = w_up.rearrange("e (p k) f -> e p (k f)", k=KD)
        wd_v = w_down.rearrange("e (p k) n -> e p (k n)", k=KF)
        y_v = y_rows.rearrange("(r t p) n -> t p r n", r=9, p=P)

        SC1, SH1, GA1, SC2, SH2, GA2 = 1, 0, 2, 4, 3, 5
        CHUNKS = [SC1, SH1, GA1, SC2, SH2, GA2]
        COLG = [2 * DG, 2 * DG + 512, 2 * DG + 1024, DG, 0]

        def win_tile(i):
            return win3 if i == 3 else win012[:, (0 if i == 4 else i)]

        SH_BANK = [3, 0, 1, 3]

        ZOFF = {3: 0, 2: 512, 0: 896, 1: 1024}
        ZW = {t: P * (t + 1) for t in range(TT)}
        AOFF = {j: ZOFF[TT - 1 - j] for j in range(TT)}
        AW = {j: T - P * j for j in range(TT)}

        ST_X, ST_VS, ST_V, ST_G, ST_S, ST_O = range(6)

        def part(tile, slot, piece, c0, c1):
            if isinstance(slot, int):
                return tile[:, slot, piece, c0:c1]
            return tile[:, bass.ds(slot, 1), piece, c0:c1].rearrange("p s f -> p (s f)")

        def pair_out(ac, A, ct):
            ac.wait_ge(o_mm, 2 * ct + 2)
            if ct >= 1:
                ac.wait_ge(ss_mm, ct)
            A(sq[:, :], bank(6), ACT.Square)
            A(mixt[:, 4 + ct, :], bank(6), ACT.Copy, scale=gb[:, 4 + ct:5 + ct]).then_inc(o_ev, 1)

        block = ctx.enter_context(nc.Block())

        @block.sync
        def _(sp):
            sp.dma_start(c_col[:, :], c.rearrange("(p k) -> p k", k=KD)).then_inc(c_in, 16)
            for t in range(TT):
                sp.dma_start(xs[:, t, :], x[t * P:(t + 1) * P, :]).then_inc(x_in[t], 16)
            for n in range(4 * len(CHUNKS)):
                g, q = CHUNKS[n // 4], n % 4
                if n >= 2:
                    sp.wait_ge(ada_used, n - 1)
                if n == 12:
                    sp.wait_ge(row_ok, 1)
                    sp.dma_start(grow[:, :], g_pre_ffn.partition_broadcast(P)).then_inc(grow_in, 16)
                if n == 20:
                    sp.wait_ge(row_ok, 3)
                    sp.dma_start(grow[:, :], g_post_ffn.partition_broadcast(P)).then_inc(grow_in, 16)
                sp.dma_start(ada[:, n % 2, :, :], ada_v[:, 2 * q:2 * q + 2, g * D:(g + 1) * D])\
                  .then_inc(ada_in[n % 2], 16)
            sp.wait_ge(row_ok, 4)
            sp.wait_ge(vn_ok, 1)
            sp.wait_ge(proj_mm, 20)

            def load_piece(e, slot, sems, p_):
                sp.dma_start(raw[:, slot, p_, :], (wg_v, wu_v, wd_v)[p_][bass.ds(e, 1)].rearrange("e p f -> p (e f)"))\
                  .then_inc(sems[p_], 16)

            def load(e, slot, sems, before):
                for p_ in range(3):
                    before(p_)
                    load_piece(e, slot, sems, p_)

            def freed(n):
                sp.wait_ge(hi_ok, n)
                sp.wait_ge(lo_dve, n)
                sp.wait_ge(lo_pool, n)

            for p_ in range(3):
                load_piece(0, 0, w_in_sem[0], p_)
            load_piece(1, 1, w_in_sem[1], 0)
            for t in range(TT):
                sp.wait_ge(h2_ok, t + 1)
                sp.dma_start(h_rows[t * P:(t + 1) * P, :], h2p[:, t % 2].rearrange("p k q -> p (k q)"))\
                  .then_inc(h2_out[t % 2], 16)
            sp.wait_ge(lg_mm, 1)
            load_piece(1, 1, w_in_sem[1], 1)
            for t in range(TT):
                sp.wait_ge(sdn_ev, t + 1)
                sp.dma_start(y_rows[8 * T + t * P:8 * T + (t + 1) * P, :], ysh[:, t % 2, :])\
                  .then_inc(ysh_out[t % 2], 16)
            load_piece(1, 1, w_in_sem[1], 2)
            with sp.Fori(1, E // 2) as i:
                for s in range(2):
                    load(i * 2 + s, s, w_in_sem[s], lambda p_: freed(i * 6 + (3 * s - 5 + p_)))
            sp.wait_ge(over_ok, 1)
            n = sp.value_load(nover[0:1, 0:1], min_val=0, max_val=OVER)
            with sp.If(n > 0):
                with sp.Fori(0, n) as j:
                    e = sp.value_load(eid[0:1, bass.ds(j, 1)], min_val=0, max_val=E - 1)
                    load(e, 0, wx_in, lambda p_: freed(j * 3 + (3 * (E - 1) + 1 + p_)))
            sp.wait_ge(scattered, n * 16 + 16 * E)
            for t in range(TT):
                if t == 0:
                    sp.wait_ge(ysh_out[0], 16 * TT // 2)
                    sp.wait_ge(ysh_out[1], 16 * TT // 2)
                sp.dma_start(yall[:, t], y_v[t]).then_inc(y_in[t], 16)
            for t in range(TT):
                sp.wait_ge(out_ok, t + 1)
                sp.dma_start(out[t * P:(t + 1) * P, :], xs[:, t, :]).then_inc(out_done, 16)
            sp.wait_ge(out_done, 16 * TT)

        @block.gpsimd
        def _(gp):
            step = [0]

            def then(ins):
                step[0] += 1
                ins.then_inc(pool_step, 1)
                gp.wait_ge(pool_step, step[0])

            last_row, last_routed = gp.to_reg(T - 1), gp.to_reg(TOPK * T - 1)

            def pick(tile, op, fill, pattern, mult, base_=0):
                return gp.affine_select(out=tile, in_=tile, compare_op=op, fill=fill, base=base_,
                                        pattern=pattern, channel_multiplier=mult)

            gp.memset(ones[:, :], 1.0)
            gp.memset(onesb[:, :], 1.0)
            gp.memset(ident[:, :], 0.0)
            gp.memset(identb[:, :], 0.0)
            gp.memset(negmask[:, :], 0.0)
            gp.memset(ustrb[:, :], 1.0)
            gp.iota(iotab[:, :], [[1, P]], base=0, channel_multiplier=0, allow_small_or_imprecise_dtypes=True)
            gp.iota(iot32[:, :], [[1, OVER]], base=0, channel_multiplier=0, allow_small_or_imprecise_dtypes=True)
            then(gp.iota(iote[:, :], [[0, 1]], base=0, channel_multiplier=1, allow_small_or_imprecise_dtypes=True))
            pick(ident[:, :], ALU.not_equal, 1.0, [[-1, P]], 1)
            pick(identb[:, :], ALU.not_equal, 1.0, [[-1, P]], 1)
            pick(negmask[:, :], ALU.is_gt, NEG, [[-1, P]], 1)
            then(pick(ustrb[:, :], ALU.is_gt, 0.0, [[1, P]], -1))
            gp.sem_inc(const_ok, 1)

            for i in range(5):
                if i == 0:
                    gp.wait_ge(ada_used, 5)
                if i == 4:
                    gp.wait_ge(proj_mm, 4)
                dst = win_tile(i)
                gp.dma_start(dst[:, :, :] if i == 3 else dst, win_v[:, :, COLG[i]:COLG[i] + 512])\
                  .then_inc(win_in[i], 16)
            gp.wait_ge(proj_mm, 20)
            then(gp.memset(restart[:, :], 0.0))
            for t in range(TT):
                ins = gp.memset(restart[:, ZOFF[t] + ZW[t] - 1:ZOFF[t] + ZW[t]], 1.0)
            ins.then_inc(restart_ok, 1)
            for k in range(0, KD, 4):
                gp.dma_start(wo[:, k:k + 4, :], wo_v[:, k:k + 4, :]).then_inc(wo_in, 16)
            gp.wait_ge(o_mm, HEADS)
            gp.wait_ge(a_ok, HEADS)
            gp.dma_start(wsgu[:, 0], ws_gate.rearrange("(p k) f -> p k f", k=KD)).then_inc(wsgu_in, 16)
            gp.dma_start(wsgu[:, 1], ws_up.rearrange("(p k) f -> p k f", k=KD)).then_inc(wsgu_in, 16)
            gp.dma_start(wr[:, :, :], w_router.rearrange("(p k) e -> p k e", k=KD)).then_inc(wr_in, 16)
            gp.dma_start(wsd[:, :, :], ws_down.rearrange("(p k) n -> p k n", k=KF)).then_inc(wsd_in, 16)
            gp.memset(posb[:, :, E:COLS], -1.0)
            then(gp.memset(vtab[:, :, :, :], 0.0))
            for t in range(TT):
                then(gp.iota(vtab[:, t, :, 0], [[0, COLS]], base=t * P, channel_multiplier=0,
                             allow_small_or_imprecise_dtypes=True))
                then(gp.iota(vtab[:, t, :, 1], [[0, COLS]], base=1, channel_multiplier=1,
                             allow_small_or_imprecise_dtypes=True))
            gp.sem_inc(const_ok, 1)

            def gather(b):
                gp.wait_ge(idx_ok, b + 1)
                gp.sem_inc(gather_go, 1)
                gp.indirect_dma_start(out=hg[:, :, :].rearrange("p k q -> p (k q)"), out_offset=None,
                                      in_=h_rows, in_offset=bass.IndirectOffsetOnAxis(ap=idxg[:, 0:1], axis=0),
                                      bounds_check=last_row, oob_is_err=False).then_inc(gathered, 16)

            def scatter(b):
                gp.wait_ge(y_ok, b + 1)
                gp.wait_ge(idxs_ok, b + 1)
                gp.sem_inc(scatter_go, 1)
                gp.indirect_dma_start(out=y_rows, out_offset=bass.IndirectOffsetOnAxis(ap=idxs[:, 0:1], axis=0),
                                      in_=ysb[:, :], in_offset=None,
                                      bounds_check=last_routed, oob_is_err=False).then_inc(scattered, 16)

            def low_raw(b, wslot, rslot, piece):
                gp.wait_ge(hi_ok, b * 3 + (piece + 1))
                c0 = 2048 - POOL_K * 256
                gp.tensor_tensor(part(wlo, wslot, piece, c0, 2048), raw[:, rslot, piece, c0:2048],
                                 part(whi, wslot, piece, c0, 2048).bitcast(F32), ALU.subtract)\
                  .then_inc(lo_pool, 1)

            def one(b, wslot, rslot, first):
                low_raw(b, wslot, rslot, 0)
                low_raw(b, wslot, rslot, 1)
                gather(b + 1)
                low_raw(b, wslot, rslot, 2)
                if first != 0 and first != 1:
                    scatter(b - 2)

            gp.wait_ge(h2_ok, TT)
            then(gp.memset(hg[:, :, :], 0.0))
            gp.wait_ge(h2_out[0], 16 * TT // 2)
            gp.wait_ge(h2_out[1], 16 * TT // 2)
            gp.wait_ge(idx_ok, 1)
            gp.indirect_dma_start(out=hg[:, :, :].rearrange("p k q -> p (k q)"), out_offset=None,
                                  in_=h_rows, in_offset=bass.IndirectOffsetOnAxis(ap=idxg[:, 0:1], axis=0),
                                  bounds_check=last_row, oob_is_err=False).then_inc(gathered, 16)
            one(0, 0, 0, 0)
            one(1, 1, 1, 1)
            one(2, 0, 0, 2)
            gp.wait_ge(over_ok, 1)
            n = gp.value_load(nover[0:1, 0:1], min_val=0, max_val=OVER)
            with gp.If(n > 0):
                with gp.Fori(0, n) as j:
                    e = gp.value_load(eid[0:1, bass.ds(j, 1)], min_val=0, max_val=E - 1)
                    gp.tensor_tensor(posb[:, :, bass.ds(j + E, 1)].rearrange("p t b -> p (t b)"),
                                     posb[:, :, bass.ds(e, 1)].rearrange("p t b -> p (t b)"),
                                     offs[:, bass.ds(j, 1)].to_broadcast([P, TT]), ALU.add)
                    gp.tensor_copy(vtab[:, :, bass.ds(j + E, 1), :].rearrange("p t b v -> p t (b v)"),
                                   vtab[:, :, bass.ds(e, 1), :].rearrange("p t b v -> p t (b v)"))
            gp.sem_inc(fill_ok, 1)
            one(3, 1, 1, 2)
            with gp.Fori(2, E // 2) as i:
                for s in range(2):
                    one(i * 2 + s, s, s, 2)
            with gp.If(n > 0):
                with gp.Fori(E, n + E) as b:
                    one(b, b % 2, 0, 2)
            scatter(n + (E - 2))
            scatter(n + (E - 1))

        @block.scalar
        def _(ac):
            A = nc.scalar.activation
            step = [0]

            def then(ins):
                step[0] += 1
                ins.then_inc(a_step, 1)
                ac.wait_ge(a_step, step[0])

            def load(dst, src):
                ac.dma_start(dst, src).then_inc(vec_in, 16)

            load(bsc[:, :], b_ada[SC1 * D:(SC1 + 1) * D].rearrange("(p k) -> p k", k=KD))
            load(bsh[:, :], b_ada[SH1 * D:(SH1 + 1) * D].rearrange("(p k) -> p k", k=KD))
            load(gpm[:, :], g_pre_mix.rearrange("(p k) -> p k", k=KD))
            load(wsp[:, :, :], w_spatial.rearrange("g i j -> i g j"))
            with nc.allow_non_contiguous_dma(reason="two short vectors by column"):
                load(gb[:, :], g_branch.rearrange("(k p) -> p k", p=P))
                load(bsp[:, :], b_spatial.rearrange("g i -> i g"))
            load(lng[:, :], ln_sgu_g.partition_broadcast(P))
            load(lnb[:, :], ln_sgu_b.partition_broadcast(P))
            load(ga1[:, :], b_ada[GA1 * D:(GA1 + 1) * D].partition_broadcast(P))
            load(a2[:, :], b_ada[SC2 * D:(SC2 + 1) * D].partition_broadcast(P))
            load(b2[:, :], b_ada[SH2 * D:(SH2 + 1) * D].partition_broadcast(P))
            load(ga2[:, :], b_ada[GA2 * D:(GA2 + 1) * D].partition_broadcast(P))
            load(rb[:, :], router_bias.partition_broadcast(P))
            ac.dma_start(grow[:, :], g_post_mix.partition_broadcast(P)).then_inc(grow_in, 16)

            ac.wait_ge(c_in, 16)
            A(sc_col[:, :], c_col[:, :], ACT.Silu).then_inc(sc_ok, 1)
            roots = [0]

            def take_root(st, c0=0, c1=TT):
                roots[0] += 1
                ac.wait_ge(var_ok, roots[0])
                A(root[:, st, c0:c1], var[:, st, c0:c1], ACT.Sqrt).then_inc(root_ok, 1)

            for t in range(TT):
                ac.wait_ge(x_in[t], 16)
                ins = A(junk[:, :], xs[:, t, :], ACT.Square, accum_out=stat[:, ST_X, t:t + 1])
                ins.then_inc(sumsq, 1) if t == TT - 1 else then(ins)
            take_root(ST_X)
            ac.wait_ge(ab_ok, 1)
            for k in range(0, KD, 2):
                ac.wait_ge(h1_tr, k + 1)
                A(h1t[:, k, :], bank(k % 6), ACT.Identity, bias=b1c[:, k:k + 1], scale=a1c[:, k:k + 1])\
                    .then_inc(h1_act, 1)
            for n in range(20):
                ac.wait_ge(proj_mm, n + 1)
                src = bank(n % 4)
                if n < 4:
                    A(qt[:, n, :], src, ACT.Copy, scale=HD ** -0.5).then_inc(proj_ev, 1)
                elif n < 8:
                    A(kt[:, n - 4, :], src, ACT.Copy).then_inc(proj_ev, 1)
                elif n < 12:
                    A(vv[:, n - 8, :], src, ACT.Copy).then_inc(proj_ev, 1)
                elif n < 16:
                    t = n - 12
                    A(v_sb[:, t, :], src, ACT.Gelu_apprx_tanh, accum_out=stat[:, ST_VS, t:t + 1])\
                        .then_inc(proj_ev, 1)
                else:
                    A(u_sb[:, n - 16, :], src, ACT.Gelu_apprx_tanh).then_inc(proj_ev, 1)
            ac.wait_ge(vmean_ok, 1)
            for t in range(TT):
                ins = A(junk[:, 0:DG], v_sb[:, t, :], ACT.Square, accum_out=stat[:, ST_V, t:t + 1])
                ins.then_inc(sumsq, 1) if t == TT - 1 else then(ins)
            take_root(ST_V)
            ac.wait_ge(og_ok, GROUPS)
            for t in range(TT):
                ins = A(junk[:, 0:DG], u_sb[:, t, :], ACT.Square, accum_out=stat[:, ST_G, t:t + 1])
                ins.then_inc(sumsq, 1) if t == TT - 1 else then(ins)
            take_root(ST_G)
            for k in range(4):
                ac.wait_ge(og_tr, k + 1)
                A(mixt[:, k, :], bank(4 + k), ACT.Copy, scale=gb[:, k:k + 1]).then_inc(og_ev, 1)
            for h in range(HEADS + 1):
                if h < HEADS:
                    ac.wait_ge(z_mm, h + 1)
                    if h >= 2:
                        ac.wait_ge(att_tr, h - 1)
                    A(beta[:, h % 2], ps[:, 0:1280], ACT.Sigmoid).then_inc(beta_ok, 1)
                    A(rest[:, h % 2], ps[:, 0:1280], ACT.Sigmoid, scale=-1.0).then_inc(beta_ok, 1)
                if h >= 1:
                    g = h - 1
                    ac.wait_ge(att_tr, g + 1)
                    if g >= 2:
                        ac.wait_ge(o_mm, g - 1)
                    A(at_sb[:, g % 2, :], ps[:, 3 * BANK:3 * BANK + 1280], ACT.Copy).then_inc(a_ok, 1)
                if h >= 3 and h % 2 == 1:
                    pair_out(ac, A, (h - 3) // 2)
            pair_out(ac, A, 3)
            take_root(ST_X)
            def shared_silu(t):
                ac.wait_ge(sgu_mm, t + 1)
                if t >= 1:
                    ac.wait_ge(sact_ok, t)
                A(sg[:, :], bank(SH_BANK[t])[:, 0:F], ACT.Silu).then_inc(ssg_ok, 1)

            def shared_evac(t):
                ac.wait_ge(sat_tr, t + 1)
                if t >= 2:
                    ac.wait_ge(sdn_mm, t - 1)
                A(sht[:, t % 2], bank(6)[:, 0:F].rearrange("p (k q) -> p k q", k=KF), ACT.Copy)\
                    .then_inc(sat_ev, 1)

            def shared_rows(t):
                ac.wait_ge(sdn_mm, t + 1)
                if t >= 2:
                    ac.wait_ge(ysh_out[t % 2], 16)
                A(ysh[:, t % 2, :], bank(4, 2), ACT.Copy).then_inc(sdn_ev, 1)

            def high(b, wslot, rslot, piece, landed):
                ac.wait_ge(*landed)
                A(part(whi, wslot, piece, 0, 2048), raw[:, rslot, piece, :], ACT.Copy).then_inc(hi_ok, 1)

            for t in range(TT):
                ac.wait_ge(wo_mm, t + 1)
                if t == 0:
                    ac.wait_ge(rs_g_ok, 1)
                    ac.wait_ge(rs_sb_ok, 1)
                pa = ps[:, (t % 2) * 4 * BANK:(t % 2) * 4 * BANK + 2 * BANK]
                if t >= 2:
                    ac.wait_ge(h2_ok, t - 1)
                A(o_sb[:, t % 2, :], pa, ACT.Copy, scale=rs[:, ST_G, t:t + 1]).then_inc(wo_a, 1)
                ac.wait_ge(wo_o, t + 1)
                A(junk[:, :], o_sb[:, t % 2, :], ACT.Square, accum_out=stat[:, ST_S, t:t + 1]).then_inc(sumsq, 1)
                take_root(ST_S, t, t + 1)
                ac.wait_ge(wo_x, t + 1)
                A(junk[:, :], xs[:, t, :], ACT.Square, accum_out=stat[:, ST_O, t:t + 1]).then_inc(sumsq, 1)
                take_root(ST_O, t, t + 1)
                if t == TT - 1:
                    shared_silu(0)
                ac.wait_ge(h2_tr, t + 1)
                A(h2t[:, :, t * P:(t + 1) * P], pa.rearrange("p (k q) -> p k q", k=KD), ACT.Copy)\
                    .then_inc(h2_ev, 1)
            ac.wait_ge(lg_mm, 1)
            A(scores[:, :, :], ps[:, 2 * BANK:2 * BANK + TT * E].rearrange("p (t e) -> p t e", t=TT),
              ACT.Sigmoid).then_inc(sig_ok, 1)
            shared_evac(0)
            shared_silu(1)
            high(0, 0, 0, 0, (w_in_sem[0][0], 16))
            shared_rows(0)
            shared_evac(1)
            high(0, 0, 0, 1, (w_in_sem[0][1], 16))
            shared_silu(2)
            shared_rows(1)
            shared_evac(2)
            shared_silu(3)
            shared_rows(2)
            shared_evac(3)
            shared_rows(3)

            def silu(b):
                ac.wait_ge(gu_mm, b + 1)
                A(sg[:, :], bank(2)[:, 0:F], ACT.Silu).then_inc(silu_ok, 1)

            def ht_high(b):
                ac.wait_ge(ht_tr, b + 1)
                A(hthi[:, :, :], bank(0, 2).rearrange("p (k q) -> p k q", k=KD), ACT.Copy).then_inc(hthi_ok, 1)

            def y_out(b):
                ac.wait_ge(scattered, b * 16)
                A(ysb[:, :], bank(4, 2), ACT.Copy).then_inc(y_ok, 1)

            def one(b, wslot, rslot, landed, first):
                if first >= 1:
                    high(b, wslot, rslot, 0, landed[0])
                    high(b, wslot, rslot, 1, landed[1])
                if first >= 1:
                    if first == 1:
                        ac.wait_ge(gu_mm, b)
                        A(sg[:, :], bank(2)[:, 0:F], ACT.Silu).then_inc(silu_ok, 1)
                    else:
                        silu(b - 1)
                    ht_high(b)
                else:
                    ac.wait_ge(ht_tr, 1)
                    A(hthi[:, :, :], bank(0, 2).rearrange("p (k q) -> p k q", k=KD), ACT.Copy)\
                        .then_inc(hthi_ok, 1)
                if first >= 2:
                    ac.wait_ge(dn_mm, b - 1)
                high(b, wslot, rslot, 2, landed[2])
                if first == 2:
                    A(ysb[:, :], bank(4, 2), ACT.Copy).then_inc(y_ok, 1)
                if first > 2:
                    y_out(b - 2)

            one(0, 0, 0, [(w_in_sem[0][p_], 16) for p_ in range(3)], 0)
            for s in range(2):
                ac.wait_ge(ysh_out[s], 16 * TT // 2)
            one(1, 1, 1, [(w_in_sem[1][p_], 16) for p_ in range(3)], 1)
            one(2, 0, 0, [(w_in_sem[0][p_], 32) for p_ in range(3)], 2)
            one(3, 1, 1, [(w_in_sem[1][p_], 32) for p_ in range(3)], 3)
            with ac.Fori(2, E // 2) as i:
                for s in range(2):
                    one(i * 2 + s, s, s, [(w_in_sem[s][p_], i * 16 + 16) for p_ in range(3)], 3)
            ac.wait_ge(over_ok, 1)
            n = ac.value_load(nover[0:1, 0:1], min_val=0, max_val=OVER)
            with ac.If(n > 0):
                with ac.Fori(E, n + E) as b:
                    one(b, b % 2, 0, [(wx_in[p_], b * 16 - 16 * (E - 1)) for p_ in range(3)], 3)
            silu(n + (E - 1))
            ac.wait_ge(dn_mm, n + (E - 1))
            y_out(n + (E - 2))
            ac.wait_ge(dn_mm, n + E)
            y_out(n + (E - 1))
            for t in range(TT):
                ac.wait_ge(ysum_ok, t + 1)
                A(junk[:, :], yall[:, t, 0, :], ACT.Square, accum_out=stat[:, ST_S, t:t + 1]).then_inc(sumsq, 1)
                take_root(ST_S, t, t + 1)

        @block.tensor
        def _(pe):
            mm = pe.matmul

            def transpose(o, i):
                return pe.transpose(o, i, ident[:, :])

            pe.wait_ge(const_ok, 1)
            pe.wait_ge(z_ok, TT)

            def h1_transposes(k):
                for t in range(TT):
                    ins = transpose(bank(k % 6)[:, t * P:(t + 1) * P], z1[:, t, k, :])
                ins.then_inc(h1_tr, 1)

            for k in range(6):
                h1_transposes(k)
            for ch in range(2):
                pe.wait_ge(acc_ok, ch + 1)
                cols = acc[:, ch, :].rearrange("p (q k) -> p k q", k=KD)
                for k in range(KD):
                    ins = mm(ps[:, 6 * BANK + ch * KD + k:6 * BANK + ch * KD + k + 1], cols[:, k, :],
                             ones[:, 0:1], start=True, stop=True)
                ins.then_inc(mod_mm, 1)
            pe.wait_ge(h1_act, 1)
            h1_transposes(6)
            pe.wait_ge(h1_dve, 1)
            h1_transposes(7)
            pe.wait_ge(h1_act, 4)
            pe.wait_ge(h1_dve, 4)
            pe.wait_ge(vec_in, 16 * 13)
            for g in range(GROUPS):
                ins = transpose(bank(4)[:, g * P:(g + 1) * P], wsp[:, g, :])
            ins.then_inc(wsp_tr, 1)

            def modulation_row(ch):
                pe.wait_ge(acc_ok, ch + 1)
                if ch > 2:
                    pe.wait_ge(row_ok, ch - 2)
                for hf in range(2):
                    ins = mm(bank(6 + hf), ones[:, :], acc[:, ch % 2, hf * 512:(hf + 1) * 512],
                             start=True, stop=True)
                ins.then_inc(mod_mm, 1)

            for n in range(20):
                g, m = n // 4, n % 4
                if m == 0:
                    pe.wait_ge(win_in[g], 16)
                    if g >= 2:
                        modulation_row(g)
                if n >= 4:
                    pe.wait_ge(proj_ev, n - 3)
                w = win_tile(g)
                for k in range(KD):
                    wk = w[:, k, :]
                    if g < 2:
                        ins = mm(bank(m), wk[:, m * P:(m + 1) * P], h1t[:, k, :], start=(k == 0), stop=(k == KD - 1))
                    else:
                        ins = mm(bank(m), h1t[:, k, m * P:(m + 1) * P], wk, start=(k == 0), stop=(k == KD - 1))
                ins.then_inc(proj_mm, 1)
            modulation_row(5)
            pe.wait_ge(wsp_ok, 1)
            pe.wait_ge(vn_ok, 1)
            pe.wait_ge(proj_ev, 20)
            for g in range(GROUPS):
                mm(bank(g), wspt[:, g, :], v_sb[:, :, g * P:(g + 1) * P], start=True, stop=True).then_inc(mixed_mm, 1)
            pe.wait_ge(row_ok, 4)
            pe.wait_ge(og_ok, GROUPS)
            for k in range(4):
                for t in range(TT):
                    ins = transpose(bank(4 + k)[:, t * P:(t + 1) * P], u_sb[:, t, k * P:(k + 1) * P])
                ins.then_inc(og_tr, 1)
            pe.wait_ge(og_ev, 4)

            def scores_mm(h):
                r0, ct = HD * (h % 2), h // 2
                if h >= 1:
                    pe.wait_ge(beta_ok, 2 * h)
                for t in (3, 2, 0, 1):
                    mm(ps[:, ZOFF[t]:ZOFF[t] + ZW[t]], qt[r0:r0 + HD, ct, t * P:(t + 1) * P],
                       kt[r0:r0 + HD, ct, 0:ZW[t]], start=(t != 0), stop=True, skip_group_check=True)
                for t in (3, 2, 0, 1):
                    o = ZOFF[t] + P * t
                    ins = mm(ps[:, o:o + P], identb[:, :], negmask[:, :], start=False, stop=True,
                             skip_group_check=True)
                ins.then_inc(z_mm, 1)

            def weights_tr(h):
                pe.wait_ge(att_ok, h + 1)
                if h >= 1:
                    pe.wait_ge(a_ok, h)
                for t in range(TT):
                    for j in range(t + 1):
                        o = 3 * BANK + AOFF[j] + P * (t - j)
                        i = ZOFF[t] + P * j
                        ins = transpose(ps[:, o:o + P], beta[:, h % 2, i:i + P])
                ins.then_inc(att_tr, 1)

            def values_mm(h):
                r0, ct = HD * (h % 2), h // 2
                pe.wait_ge(a_ok, h + 1)
                if h % 2 == 0 and h >= 2:
                    pe.wait_ge(o_ev, ct)
                for j in range(TT):
                    ins = mm(bank(6)[r0:r0 + HD, j * P:T], vv[:, j, h * HD:(h + 1) * HD],
                             at_sb[:, h % 2, AOFF[j]:AOFF[j] + AW[j]], start=(j == 0), stop=(j == TT - 1),
                             skip_group_check=True)
                ins.then_inc(o_mm, 1)

            def squares_mm(ct):
                pe.wait_ge(o_ev, ct + 1)
                for t in range(TT):
                    ins = mm(ps[:, 7 * BANK + 4 * t + ct:7 * BANK + 4 * t + ct + 1], sq[:, t * P:(t + 1) * P],
                             ones[:, 0:1], start=True, stop=True)
                ins.then_inc(ss_mm, 1)

            for h in range(HEADS + 2):
                if h < HEADS:
                    scores_mm(h)
                if h >= 2:
                    values_mm(h - 2)
                if 1 <= h <= HEADS:
                    weights_tr(h - 1)
                if h >= 4 and h % 2 == 0:
                    squares_mm((h - 4) // 2)
            squares_mm(3)

            def out_proj(t):
                b0 = (t % 2) * 4
                if t == 0:
                    pe.wait_ge(wo_in, 32)
                if t == 1:
                    pe.wait_ge(rs_sb_ok, 1)
                if t >= 2:
                    pe.wait_ge(h2_ev, t - 1)
                for br in range(2):
                    for hf in range(2):
                        for k in range(4):
                            ins = mm(bank(b0 + 2 * br + hf), mixt[:, 4 * br + k, t * P:(t + 1) * P],
                                     wo[:, 4 * br + k, hf * 512:(hf + 1) * 512], start=(k == 0), stop=(k == 3))
                ins.then_inc(wo_mm, 1)

            def h2_transposes(t):
                pe.wait_ge(h2_ok, t + 1)
                for k in range(KD):
                    ins = transpose(ps[:, (t % 2) * 4 * BANK + k * P:(t % 2) * 4 * BANK + (k + 1) * P],
                                    h2p[:, t % 2, k, :])
                ins.then_inc(h2_tr, 1)

            def router(t):
                pe.wait_ge(h2_ev, t + 1)
                for k in range(KD):
                    ins = mm(ps[:, 2 * BANK + t * E:2 * BANK + (t + 1) * E], h2t[:, k, t * P:(t + 1) * P],
                             wr[:, k, :], start=(k == 0), stop=(k == KD - 1))
                if t == TT - 1:
                    ins.then_inc(lg_mm, 1)

            def shared_up(t):
                if t == 3:
                    pe.wait_ge(sact_ok, 1)
                for k in range(KD):
                    ins = mm(bank(SH_BANK[t]), h2t[:, k, t * P:(t + 1) * P], wsgu[:, :, k, :],
                             start=(k == 0), stop=(k == KD - 1))
                ins.then_inc(sgu_mm, 1)

            def shared_tr(t):
                pe.wait_ge(sact_ok, t + 1)
                if t == 0:
                    pe.wait_ge(h2_ok, TT)
                for k in range(KF):
                    ins = transpose(bank(6)[:, k * P:(k + 1) * P], act_s[:, k, :])
                ins.then_inc(sat_tr, 1)

            def shared_down(t):
                pe.wait_ge(sat_ev, t + 1)
                if t >= 1:
                    pe.wait_ge(sdn_ev, t)
                for hf in range(2):
                    for k in range(KF):
                        ins = mm(bank(4 + hf), sht[:, t % 2, k, :], wsd[:, k, hf * 512:(hf + 1) * 512],
                                 start=(k == 0), stop=(k == KF - 1))
                ins.then_inc(sdn_mm, 1)

            def positions():
                pe.wait_ge(sel_ok, 1)
                for t in range(TT):
                    for t2 in range(t + 1):
                        ins = mm(ps[:, 7 * BANK + t * E:7 * BANK + (t + 1) * E], (ustrb if t2 == t else onesb)[:, :],
                                 selb[:, t2, :], start=(t2 == 0), stop=(t2 == t))
                ins.then_inc(cnt_mm, 1)

            def indices(b):
                pe.wait_ge(onehot_ok, b + 1)
                for t in range(TT):
                    ins = mm(ps[:, 7 * BANK:7 * BANK + VC], s_onehot[:, t, :], vcur[:, t, :],
                             start=(t == 0), stop=(t == TT - 1))
                ins.then_inc(idx_mm, 1)

            def rows_in(b):
                pe.wait_ge(gathered, b * 16 + 16)
                for k in range(KD):
                    ins = transpose(ps[:, k * P:(k + 1) * P], hg[:, k, :])
                ins.then_inc(ht_tr, 1)

            def wpart(tile, slot, lo, n_, k):
                if n_ == 2:
                    v = tile[:, slot, 0:2, k * F:(k + 1) * F] if isinstance(slot, int) else \
                        tile[:, bass.ds(slot, 1), 0:2, k * F:(k + 1) * F].rearrange("p s g f -> p (s g) f")
                    return v
                return part(tile, slot, 2, k * 512, (k + 1) * 512)

            def gate_up(b, slot):
                pe.wait_ge(lo_dve, b * 3 + 2)
                pe.wait_ge(lo_pool, b * 3 + 2)
                pe.wait_ge(htlo_ok, b + 1)
                for k in range(KD):
                    hi, lo = wpart(whi, slot, 0, 2, k), wpart(wlo, slot, 0, 2, k)
                    mm(bank(2), hthi[:, k, :], hi, start=(k == 0), stop=False)
                    mm(bank(2), hthi[:, k, :], lo, start=False, stop=False)
                    ins = mm(bank(2), htlo[:, k, :], hi, start=False, stop=(k == KD - 1))
                ins.then_inc(gu_mm, 1)

            def down(b, slot, first=False):
                pe.wait_ge(lo_dve, b * 3 + 3)
                pe.wait_ge(lo_pool, b * 3 + 3)
                pe.wait_ge(actlo_ok, b + 1)
                if not first:
                    pe.wait_ge(y_ok, b)
                for k in range(KF):
                    for st, w in ((acthi, whi), (acthi, wlo), (actlo, whi)):
                        for hf in range(2):
                            ins = mm(bank(4 + hf), st[:, k, :], wpart(w, slot, 2, 1, 2 * k + hf),
                                     start=(k == 0 and st is acthi and w is whi),
                                     stop=(k == KF - 1 and st is actlo))
                ins.then_inc(dn_mm, 1)

            def acts_tr(b):
                pe.wait_ge(act_ok, b + 1)
                for k in range(KF):
                    ins = transpose(ps[:, 3 * BANK + k * P:3 * BANK + (k + 1) * P], act_s[:, k, :])
                ins.then_inc(at_tr, 1)

            def one(b, slot, prev, first):
                gate_up(b, slot)
                rows_in(b + 1)
                if first >= 1:
                    down(b - 1, prev, first == 1)
                indices(b + 2)
                acts_tr(b)

            out_proj(0)
            out_proj(1)
            h2_transposes(0)
            out_proj(2)
            h2_transposes(1)
            out_proj(3)
            h2_transposes(2)
            pe.wait_ge(h2_ev, 2)
            pe.wait_ge(wsgu_in, 32)
            shared_up(0)
            pe.wait_ge(wr_in, 16)
            router(0)
            router(1)
            h2_transposes(3)
            router(2)
            router(3)
            shared_tr(0)
            shared_up(1)
            pe.wait_ge(wsd_in, 16)
            shared_down(0)
            shared_tr(1)
            shared_up(2)
            positions()
            shared_down(1)
            shared_tr(2)
            indices(0)
            shared_up(3)
            indices(1)
            shared_down(2)
            shared_tr(3)
            rows_in(0)
            shared_down(3)
            for t in range(TT):
                ins = mm(ps[0:E, 6 * BANK:6 * BANK + 1], selb[:, t, :], onesb[:, 0:1],
                         start=(t == 0), stop=(t == TT - 1))
            ins.then_inc(count_mm, 1)
            one(0, 0, 1, 0)
            pe.wait_ge(ext_ok, 1)
            mm(ps[0:E, 6 * BANK + 1:6 * BANK + 2], ustrb[0:E, 0:E], extb[:, :], start=True, stop=True)
            mm(ps[0:1, 6 * BANK + 2:6 * BANK + 3], extb[:, :], onesb[0:E, 0:1], start=True, stop=True)\
                .then_inc(start_mm, 1)
            one(1, 1, 0, 1)
            pe.wait_ge(selx_ok, 1)
            mm(ps[0:1, 6 * BANK + 64:6 * BANK + 64 + OVER], iote[:, :], selx[:, :], start=True, stop=True)
            mm(ps[:, 6 * BANK + 128:6 * BANK + 128 + OVER], ones[0:E, :], jm[:, :], start=True, stop=True)\
                .then_inc(over_mm, 1)
            with pe.Fori(1, E // 2) as i:
                for s in range(2):
                    one(i * 2 + s, s, 1 - s, 2)
            pe.wait_ge(over_ok, 1)
            n = pe.value_load(nover[0:1, 0:1], min_val=0, max_val=OVER)
            with pe.If(n > 0):
                with pe.Fori(E, n + E) as b:
                    one(b, b % 2, (b + 1) % 2, 2)
            down(n + (E - 1), (n + 1) % 2)

        @block.vector
        def _(v):
            V = nc.vector
            step = [0]

            def then(ins):
                step[0] += 1
                ins.then_inc(v_step, 1)
                v.wait_ge(v_step, step[0])

            sums = [0]
            vars_ = [0]

            def factor(st, width, c0=0, c1=TT, src=None, wait=True):
                if wait:
                    sums[0] += 1
                    v.wait_ge(sumsq, sums[0])
                vv_, rr, r = var[:, st, c0:c1], root[:, st, c0:c1], rs[:, st, c0:c1]
                V.tensor_scalar(vv_, stat[:, st, c0:c1] if src is None else src, 1.0 / width, EPS,
                                ALU.mult, ALU.add).then_inc(var_ok, 1)
                vars_[0] += 1
                v.wait_ge(root_ok, vars_[0])
                then(V.reciprocal(r, rr))
                then(V.tensor_tensor(nt[:, c0:c1], r, r, ALU.mult))
                then(V.tensor_tensor(nt[:, c0:c1], nt[:, c0:c1], vv_, ALU.mult))
                then(V.tensor_scalar(nt[:, c0:c1], nt[:, c0:c1], -0.5, 1.5, ALU.mult, ALU.add))
                then(V.tensor_tensor(r, r, nt[:, c0:c1], ALU.mult))

            factor(ST_X, D)
            for t in range(TT):
                V.tensor_scalar(z1[:, t].rearrange("p k q -> p q k"),
                                xs[:, t, :].rearrange("p (q k) -> p q k", k=KD), rs[:, ST_X, t:t + 1], None,
                                ALU.mult).then_inc(z_ok, 1)
            v.wait_ge(sc_ok, 1)

            def weigh(ch):
                if ch >= 2:
                    v.wait_ge(mod_mm, ch - 1)
                for q in range(4):
                    n = 4 * ch + q
                    v.wait_ge(ada_in[n % 2], 16 * (n // 2 + 1))
                    for r in range(2):
                        k = 2 * q + r
                        src = ada[:, n % 2, r, :]
                        if k == 0:
                            ins = V.tensor_scalar(acc[:, ch % 2, :], src, sc_col[:, 0:1], None, ALU.mult)
                        else:
                            ins = V.scalar_tensor_tensor(out=acc[:, ch % 2, :], in0=src, scalar=sc_col[:, k:k + 1],
                                                         in1=acc[:, ch % 2, :], op0=ALU.mult, op1=ALU.add)
                        if r == 0:
                            then(ins)
                        else:
                            ins.then_inc(ada_used, 1)
                            v.wait_ge(ada_used, n + 1)
                v.sem_inc(acc_ok, 1)

            weigh(0)
            weigh(1)
            v.wait_ge(vec_in, 16 * 13)
            v.wait_ge(mod_mm, 2)
            m = ps[:, 6 * BANK:6 * BANK + 2 * KD]
            then(V.scalar_tensor_tensor(out=a1c[:, :], in0=m[:, 0:KD], scalar=1.0, in1=bsc[:, :],
                                        op0=ALU.add, op1=ALU.add))
            then(V.tensor_tensor(a1c[:, :], a1c[:, :], gpm[:, :], ALU.mult))
            V.tensor_tensor(b1c[:, :], m[:, KD:2 * KD], bsh[:, :], ALU.add).then_inc(ab_ok, 1)
            v.wait_ge(ab_ok, 1)
            for k in range(1, KD, 2):
                v.wait_ge(h1_tr, k + 1)
                V.tensor_scalar(h1t[:, k, :], bank(k % 6), a1c[:, k:k + 1], b1c[:, k:k + 1],
                                ALU.mult, ALU.add).then_inc(h1_dve, 1)
            v.wait_ge(wsp_tr, 1)
            then(V.tensor_copy(wspt[:, :, :], bank(4).rearrange("p (g q) -> p g q", g=GROUPS)))
            V.memset(wspt[CHUNK:P, :, 0:CHUNK], 0.0).then_inc(wsp_ok, 1)

            def mod_row(ch, dst, gain, plus_one):
                v.wait_ge(mod_mm, ch + 1)
                if plus_one:
                    ins = V.scalar_tensor_tensor(out=dst[:, :], in0=bank(6, 2), scalar=1.0, in1=dst[:, :],
                                                 op0=ALU.add, op1=ALU.add)
                else:
                    ins = V.tensor_tensor(dst[:, :], bank(6, 2), dst[:, :], ALU.add)
                if gain:
                    then(ins)
                    v.wait_ge(grow_in, 16 * gain)
                    ins = V.tensor_tensor(dst[:, :], dst[:, :], grow[:, :], ALU.mult)
                ins.then_inc(row_ok, 1)

            weigh(2)
            mod_row(2, ga1, 1, False)
            weigh(3)
            mod_row(3, a2, 2, True)
            weigh(4)
            mod_row(4, b2, 0, False)
            v.wait_ge(proj_ev, 16)
            then(V.tensor_scalar(nt[:, :], stat[:, ST_VS, :], -1.0 / DG, None, ALU.mult))
            for t in range(TT):
                ins = V.tensor_scalar(v_sb[:, t, :], v_sb[:, t, :], nt[:, t:t + 1], None, ALU.add)
            ins.then_inc(vmean_ok, 1)
            weigh(5)
            factor(ST_V, DG)
            for t in range(TT):
                then(V.scalar_tensor_tensor(out=v_sb[:, t, :], in0=v_sb[:, t, :], scalar=rs[:, ST_V, t:t + 1],
                                            in1=lng[:, :], op0=ALU.mult, op1=ALU.mult))
                ins = V.tensor_tensor(v_sb[:, t, :], v_sb[:, t, :], lnb[:, :], ALU.add)
                ins.then_inc(vn_ok, 1) if t == TT - 1 else then(ins)
            mod_row(5, ga2, 3, False)
            for g in range(GROUPS):
                v.wait_ge(mixed_mm, g + 1)
                V.scalar_tensor_tensor(out=u_sb[:, :, g * P:(g + 1) * P],
                                       in0=bank(g).rearrange("p (t q) -> p t q", t=TT), scalar=bsp[:, g:g + 1],
                                       in1=u_sb[:, :, g * P:(g + 1) * P], op0=ALU.add, op1=ALU.mult)\
                    .then_inc(og_ok, 1)
            factor(ST_G, DG)
            v.sem_inc(rs_g_ok, 1)
            v.wait_ge(restart_ok, 1)
            for h in range(HEADS):
                v.wait_ge(beta_ok, 2 * h + 2)
                then(V.tensor_tensor_scan(rest[:, h % 2, ::-1], rest[:, h % 2, ::-1], restart[:, ::-1], 1.0,
                                          ALU.mult, ALU.max))
                V.tensor_tensor(beta[:, h % 2, 0:1279], beta[:, h % 2, 0:1279], rest[:, h % 2, 1:1280], ALU.mult)\
                    .then_inc(att_ok, 1)
            v.wait_ge(ss_mm, 4)
            then(V.tensor_reduce(stat[:, ST_X, :],
                                 ps[:, 7 * BANK:7 * BANK + 16].rearrange("p (t c) -> p t c", t=TT), AX_X, ALU.add))
            factor(ST_X, DG, wait=False)
            v.sem_inc(rs_sb_ok, 1)
            for t in range(TT):
                o = o_sb[:, t % 2, :]
                pb = ps[:, ((t % 2) * 4 + 2) * BANK:((t % 2) * 4 + 4) * BANK]
                v.wait_ge(wo_a, t + 1)
                V.scalar_tensor_tensor(out=o, in0=pb, scalar=rs[:, ST_X, t:t + 1], in1=o,
                                       op0=ALU.mult, op1=ALU.add).then_inc(wo_o, 1)
                factor(ST_S, D, t, t + 1)
                then(V.scalar_tensor_tensor(out=o, in0=o, scalar=rs[:, ST_S, t:t + 1], in1=ga1[:, :],
                                            op0=ALU.mult, op1=ALU.mult))
                V.tensor_tensor(xs[:, t, :], xs[:, t, :], o, ALU.add).then_inc(wo_x, 1)
                factor(ST_O, D, t, t + 1)
                then(V.scalar_tensor_tensor(out=o, in0=xs[:, t, :], scalar=rs[:, ST_O, t:t + 1], in1=a2[:, :],
                                            op0=ALU.mult, op1=ALU.mult))
                if t >= 2:
                    v.wait_ge(h2_out[t % 2], 16)
                    v.wait_ge(h2_tr, t - 1)
                V.tensor_tensor(h2p[:, t % 2].rearrange("p k q -> p q k"),
                                o.rearrange("p (q k) -> p q k", k=KD),
                                b2[:, :].rearrange("p (q k) -> p q k", k=KD), ALU.add).then_inc(h2_ok, 1)

            def shared_act(t):
                v.wait_ge(ssg_ok, t + 1)
                if t >= 1:
                    v.wait_ge(sat_tr, t)
                V.tensor_tensor(act_s[:, :, :].rearrange("p k q -> p q k"),
                                bank(SH_BANK[t])[:, F:2 * F].rearrange("p (q k) -> p q k", k=KF),
                                sg[:, :].rearrange("p (q k) -> p q k", k=KF), ALU.mult).then_inc(sact_ok, 1)

            shared_act(0)
            v.wait_ge(sig_ok, 1)
            then(V.tensor_tensor(biased[:, :, :], scores[:, :, :],
                                 rb[:, :].unsqueeze(1).to_broadcast([P, TT, E]), ALU.add))
            for t in range(TT):
                for g in range(EG):
                    ins = V.max(top2[:, t, g, :], biased[:, t, g * EPG:(g + 1) * EPG])
            then(ins)
            then(V.tensor_tensor(gs[:, :, :], top2[:, :, :, 0], top2[:, :, :, 1], ALU.add))
            mine = gs[:, :, :].unsqueeze(3).to_broadcast([P, TT, EG, EG])
            other = gs[:, :, :].unsqueeze(2).to_broadcast([P, TT, EG, EG])
            then(V.memset(gtri[:, :, :], 0.0))
            for g in range(1, EG):
                ins = V.memset(gtri[:, g, 0:g], 1.0)
            then(ins)
            then(V.tensor_tensor(gcmp[:, :, :, :], other, mine, ALU.is_gt))
            then(V.tensor_tensor(gcmp2[:, :, :, :], other, mine, ALU.is_equal))
            for t in range(TT):
                ins = V.tensor_tensor(gcmp2[:, t], gcmp2[:, t], gtri[:, :, :], ALU.mult)
            then(ins)
            then(V.tensor_tensor(gcmp[:, :, :, :], gcmp[:, :, :, :], gcmp2[:, :, :, :], ALU.add))
            then(V.tensor_reduce(gm[:, :, :], gcmp[:, :, :, :], AX_X, ALU.add))
            then(V.tensor_scalar(gm[:, :, :], gm[:, :, :], float(TOPG), None, ALU.is_lt))
            shared_act(1)
            gmb = gm[:, :, :].unsqueeze(3).to_broadcast([P, TT, EG, EPG])
            then(V.tensor_tensor(masked[:, :, :].rearrange("p t (g e) -> p t g e", g=EG),
                                 biased[:, :, :].rearrange("p t (g e) -> p t g e", g=EG), gmb, ALU.mult))
            then(V.tensor_scalar(gm[:, :, :], gm[:, :, :], -NEG, NEG, ALU.mult, ALU.add))
            then(V.tensor_tensor(masked[:, :, :].rearrange("p t (g e) -> p t g e", g=EG),
                                 masked[:, :, :].rearrange("p t (g e) -> p t g e", g=EG), gmb, ALU.add))
            for t in range(TT):
                ins = V.max(top8[:, t, :], masked[:, t, :])
            then(ins)
            for t in range(TT):
                ins = V.match_replace(picked[:, t, :], top8[:, t, :], masked[:, t, :], 3.0e38)
            then(ins)
            then(V.tensor_tensor(sel[:, :, :], picked[:, :, :], masked[:, :, :], ALU.not_equal))
            V.tensor_copy(selb[:, :, :], sel[:, :, :]).then_inc(sel_ok, 1)
            then(V.tensor_tensor(gates[:, :, 0:E], scores[:, :, :], sel[:, :, :], ALU.mult))
            then(V.tensor_reduce(wsum[:, :], gates[:, :, 0:E], AX_X, ALU.add))
            then(V.reciprocal(wsum[:, :], wsum[:, :]))
            for t in range(TT):
                ins = V.tensor_scalar(gates[:, t, 0:E], gates[:, t, 0:E], wsum[:, t:t + 1], SCALE_ROUTED,
                                      ALU.mult, ALU.mult)
            then(ins)
            for t in range(TT):
                ins = V.tensor_tensor_scan(rank[:, t, :], ones[:, 0:E], sel[:, t, :], 0.0, ALU.mult, ALU.add)
            then(ins)
            then(V.tensor_tensor(rank[:, :, :], rank[:, :, :], sel[:, :, :], ALU.subtract))
            then(V.tensor_scalar(rank[:, :, :], rank[:, :, :], float(T), None, ALU.mult))
            v.wait_ge(const_ok, 2)
            V.tensor_copy(vtab[:, :, 0:E, 2], rank[:, :, :])
            for part_ in range(3):
                then(V.tensor_copy(vtab[:, :, 0:E, 3 + part_], gates[:, :, :]))
                if part_ < 2:
                    then(V.tensor_tensor(gates[:, :, :], gates[:, :, :], vtab[:, :, 0:E, 3 + part_], ALU.subtract))
            v.wait_ge(cnt_mm, 1)
            then(V.scalar_tensor_tensor(out=posm[:, :, :],
                                        in0=ps[:, 7 * BANK:7 * BANK + TT * E].rearrange("p (t e) -> p t e", t=TT),
                                        scalar=1.0, in1=sel[:, :, :], op0=ALU.add, op1=ALU.mult))
            then(V.tensor_scalar(posb[:, :, 0:E], posm[:, :, :], -1.0, None, ALU.add))

            def over_count():
                v.wait_ge(count_mm, 1)
                cnt = ps[0:E, 6 * BANK:6 * BANK + 1]
                then(V.tensor_scalar(ext[:, 0:1], cnt, 128.5, None, ALU.is_gt))
                for lim in (256.5, 384.5):
                    then(V.scalar_tensor_tensor(out=ext[:, 0:1], in0=cnt, scalar=lim, in1=ext[:, 0:1],
                                                op0=ALU.is_gt, op1=ALU.add))
                V.tensor_copy(extb[:, :], ext[:, 0:1]).then_inc(ext_ok, 1)

            def over_select():
                v.wait_ge(start_mm, 1)
                then(V.tensor_copy(ext[:, 1:2], ps[0:E, 6 * BANK + 1:6 * BANK + 2]))
                V.tensor_copy(nover[:, :], ps[0:1, 6 * BANK + 2:6 * BANK + 3])
                then(V.tensor_scalar(tmp32[:, :], iot32[:, :], ext[:, 1:2], None, ALU.subtract))
                then(V.tensor_scalar(selx[:, :], tmp32[:, :], 0.0, None, ALU.is_ge))
                then(V.scalar_tensor_tensor(out=selx[:, :], in0=tmp32[:, :], scalar=ext[:, 0:1], in1=selx[:, :],
                                            op0=ALU.is_lt, op1=ALU.mult))
                then(V.scalar_tensor_tensor(out=jm[:, :], in0=tmp32[:, :], scalar=1.0, in1=selx[:, :],
                                            op0=ALU.add, op1=ALU.mult))
                V.tensor_scalar(jm[:, :], jm[:, :], -float(P), None, ALU.mult).then_inc(selx_ok, 1)

            def over_tables():
                v.wait_ge(over_mm, 1)
                V.tensor_copy(offs[:, :], ps[:, 6 * BANK + 128:6 * BANK + 128 + OVER])
                V.tensor_copy(eid[:, :], ps[0:1, 6 * BANK + 64:6 * BANK + 64 + OVER]).then_inc(over_ok, 1)

            PER = 6

            def col(tile, b, *rest):
                if isinstance(b, int):
                    return tile[:, b:b + 1]
                return tile[:, bass.ds(b, 1)]

            def onehot(b):
                src = vtab[:, :, b, :] if isinstance(b, int) else \
                    vtab[:, :, bass.ds(b, 1), :].rearrange("p t b v -> p t (b v)")
                V.tensor_copy(vcur[:, :, :], src)
                for t in range(TT):
                    pcol = posb[:, t, b:b + 1] if isinstance(b, int) else posb[:, t, bass.ds(b, 1)]
                    ins = V.tensor_scalar(s_onehot[:, t, :], iotab[:, :], pcol, None, ALU.is_equal)
                ins.then_inc(onehot_ok, 1)

            def tables(b):
                v.wait_ge(idx_mm, b + 1)
                k = [0]

                def chained(ins):
                    k[0] += 1
                    ins.then_inc(v_loop, 1)
                    v.wait_ge(v_loop, b * PER + k[0])

                chained(V.tensor_reduce(pair[:, :], ps[:, 7 * BANK:7 * BANK + VC].rearrange("p (a c) -> p a c", a=2),
                                        AX_X, ALU.add))
                chained(V.tensor_scalar(inval[:, :], pair[:, 0:1], 0.0, float(BIG_ROW), ALU.is_equal, ALU.mult))
                chained(V.scalar_tensor_tensor(out=desti[:, :], in0=pair[:, 0:1], scalar=-1.0, in1=inval[:, :],
                                               op0=ALU.add, op1=ALU.add))
                chained(V.tensor_copy(col(gater, b), pair[:, 1:2]))
                chained(V.tensor_copy(col(destr, b), desti[:, :]))
                chained(V.tensor_scalar(idxg[:, :], desti[:, :], (BIG_ROW >> 1) | (T - 1), None, ALU.bitwise_and))
                assert k[0] == PER
                v.sem_inc(idx_ok, 1)

            def low(b, wslot, rslot, piece):
                v.wait_ge(hi_ok, b * 3 + (piece + 1))
                c1 = 2048 - POOL_K * 256
                V.tensor_tensor(part(wlo, wslot, piece, 0, c1), raw[:, rslot, piece, 0:c1],
                                part(whi, wslot, piece, 0, c1).bitcast(F32), ALU.subtract).then_inc(lo_dve, 1)

            def times_up(b):
                v.wait_ge(silu_ok, b + 1)
                V.scalar_tensor_tensor(out=act_s[:, :, :].rearrange("p k q -> p q k"),
                                       in0=sg[:, :].rearrange("p (q k) -> p q k", k=KF), scalar=col(gater, b),
                                       in1=bank(2)[:, F:2 * F].rearrange("p (q k) -> p q k", k=KF),
                                       op0=ALU.mult, op1=ALU.mult).then_inc(act_ok, 1)

            def ht_low(b):
                v.wait_ge(hthi_ok, b + 1)
                V.tensor_tensor(htlo[:, :, :], bank(0, 2).rearrange("p (k q) -> p k q", k=KD),
                                hthi[:, :, :].bitcast(F32), ALU.subtract).then_inc(htlo_ok, 1)

            def acts_split(b):
                v.wait_ge(at_tr, b + 1)
                src = bank(3)[:, 0:F].rearrange("p (k q) -> p k q", k=KF)
                V.tensor_copy(acthi[:, :, :], src).then_inc(acthi_ok, 1)
                v.wait_ge(acthi_ok, b + 1)
                V.tensor_tensor(actlo[:, :, :], src, acthi[:, :, :].bitcast(F32), ALU.subtract).then_inc(actlo_ok, 1)

            def rows_of(b):
                if not (isinstance(b, int) and b == 0):
                    v.wait_ge(scattered, b * 16)
                V.tensor_copy(idxs[:, :], col(destr, b)).then_inc(idxs_ok, 1)

            def one(b, wslot, rslot, first):
                low(b, wslot, rslot, 0)
                low(b, wslot, rslot, 1)
                if first >= 1:
                    times_up(b - 1)
                ht_low(b)
                tables(b + 1)
                onehot(b + 2)
                low(b, wslot, rslot, 2)
                if first >= 1:
                    acts_split(b - 1)
                if first >= 2:
                    rows_of(b - 2)

            onehot(0)
            shared_act(2)
            tables(0)
            onehot(1)
            shared_act(3)
            one(0, 0, 0, 0)
            over_count()
            one(1, 1, 1, 1)
            over_select()
            one(2, 0, 0, 2)
            over_tables()
            one(3, 1, 1, 2)
            v.wait_ge(fill_ok, 1)
            with v.Fori(2, E // 2) as i:
                for s in range(2):
                    one(i * 2 + s, s, s, 2)
            n = v.value_load(nover[0:1, 0:1], min_val=0, max_val=OVER)
            with v.If(n > 0):
                with v.Fori(E, n + E) as b:
                    one(b, b % 2, 0, 2)
            times_up(n + (E - 1))
            acts_split(n + (E - 1))
            rows_of(n + (E - 2))
            rows_of(n + (E - 1))

            for t in range(TT):
                v.wait_ge(y_in[t], 16)
                for r in range(1, 9):
                    ins = V.tensor_tensor(yall[:, t, 0, :], yall[:, t, 0, :], yall[:, t, r, :], ALU.add)
                    ins.then_inc(ysum_ok, 1) if r == 8 else then(ins)
                factor(ST_S, D, t, t + 1)
                then(V.scalar_tensor_tensor(out=yall[:, t, 0, :], in0=yall[:, t, 0, :], scalar=rs[:, ST_S, t:t + 1],
                                            in1=ga2[:, :], op0=ALU.mult, op1=ALU.mult))
                V.tensor_tensor(xs[:, t, :], xs[:, t, :], yall[:, t, 0, :], ALU.add).then_inc(out_ok, 1)


_INS = ['x', 'c', 'w_ada', 'b_ada', 'g_pre_mix', 'w_in', 'ln_sgu_g', 'ln_sgu_b', 'w_spatial', 'b_spatial',
        'g_branch', 'w_out', 'g_post_mix', 'g_pre_ffn', 'w_router', 'router_bias', 'w_gate', 'w_up',
        'w_down', 'ws_gate', 'ws_up', 'ws_down', 'g_post_ffn']


def kernel(**inputs):
    import numpy as _np
    import concourse.bacc as _bacc
    from concourse import mybir as _mybir
    from concourse.bass_utils import run_bass_kernel_spmd as _run

    nc = _bacc.Bacc("TRN2", target_bir_lowering=False, num_devices=1)
    arrays, args = {}, []
    for name in _INS:
        a = _np.ascontiguousarray(inputs[name])
        a = a.reshape(a.shape[1:])
        arrays[f"in_{name}_dram"] = a
        args.append(nc.dram_tensor(f"in_{name}_dram", a.shape, _mybir.dt.from_np(a.dtype),
                                   kind="ExternalInput").ap())
    args.append(nc.dram_tensor("out_0_dram", (T, D), _mybir.dt.float32, kind="ExternalOutput").ap())
    block_kernel(nc, *args)
    r = _run(nc, [arrays], core_ids=[0])
    return r.results[0]["out_0_dram"].reshape(1, T, D)
```

```python
from contextlib import ExitStack

import concourse.bass as bass
from concourse import mybir

F32 = mybir.dt.float32
F32R = mybir.dt.float32r
BF16 = mybir.dt.bfloat16
I32 = mybir.dt.int32
ALU = mybir.AluOpType
ACT = mybir.ActivationFunctionType
AX_X = mybir.AxisListType.X

P = 128
D = 1024
T = 512
TT = T // P
KD = D // P
KH = KD // 2
WO_RING = 3
DG = 512
GROUPS = 4
HEADS = 8
HD = 64
CHUNK = 64
E = 64
TOPK = 8
EG = 8
EPG = E // EG
TOPG = 4
F = 256
KF = F // P
SCALE_ROUTED = 2.5
EPS = 1e-6
NEG = -1.0e30
BANK = 512
OVER = TOPK * T // P
COLS = E + OVER + 2
VC = 6
BIG_ROW = 1 << 17
POOL_K = 2


def block_kernel(nc, x, c, w_ada, b_ada, g_pre_mix, w_in, ln_sgu_g, ln_sgu_b, w_spatial, b_spatial,
                 g_branch, w_out, g_post_mix, g_pre_ffn, w_router, router_bias, w_gate, w_up,
                 w_down, ws_gate, ws_up, ws_down, g_post_ffn, out):
    with ExitStack() as ctx:
        def sem(name):
            return ctx.enter_context(nc.semaphore(name))

        base = 16512

        def at(name, shape, dt, off):
            return nc.alloc_sbuf_tensor_at(name, shape, dt, offset=base + off)

        KB = 1024
        raw = at("raw", [P, 2, 3, 2048], F32, 0)
        whi = at("whi", [P, 2, 3, 2048], F32R, 48 * KB)
        wlo = at("wlo", [P, 2, 3, 2048], F32R, 96 * KB)
        yall = at("yall", [P, TT, 9, D], F32, 0)
        ada = [at("ada0", [P, 2, D], F32, 0), at("ada1", [P, 2, D], F32, 8 * KB),
               at("ada2", [P, 2, D], F32, 136 * KB)]
        acc = at("acc", [P, 2, D], F32, 16 * KB)
        grow = at("grow", [P, D], F32, 24 * KB)
        lng = at("lng", [P, DG], F32, 28 * KB)
        lnb = at("lnb", [P, DG], F32, 30 * KB)
        h1hi = at("h1hi", [P, KD, T], F32R, 32 * KB)
        h1lo = at("h1lo", [P, KD, T], F32R, 96 * KB)
        wraw = at("wraw", [P, 2, KH, 512], F32, 48 * KB)
        wphi = at("wphi", [P, 2, KH, 512], F32R, 64 * KB)
        wplo = at("wplo", [P, 2, KH, 512], F32R, 80 * KB)
        h1f = at("h1f", [P, 2, T], F32, 188 * KB)
        mixhi = [at("mixghi", [P, 4, T], F32R, 168 * KB),
                 at("mixshi", [P, 4, T], F32R, 96 * KB)]
        mixlo = [at("mixglo", [P, 4, T], F32R, 160 * KB), at("mixslo", [P, 4, T], F32R, 104 * KB)]
        woraw = at("woraw", [P, WO_RING, 512], F32, 42 * KB)
        wohi = at("wohi", [P, KD, D], F32R, 48 * KB)
        wolo = at("wolo", [P, KD, D], F32R, 0)
        qt = at("qt", [P, 4, T], F32, 112 * KB)
        kt = at("kt", [P, 4, T], F32, 120 * KB)
        h2t = at("h2t", [P, KD, T], F32, 120 * KB)
        vv = at("vv", [P, TT, 512], F32, 128 * KB)
        wsd = at("wsd", [P, KF, D], F32, 72 * KB)
        ga1 = at("ga1", [P, D], F32, 136 * KB)
        a2 = at("a2", [P, D], F32, 140 * KB)
        beta = at("beta", [P, 2, 1280], F32, 32 * KB)
        rest = at("rest", [P, 2, 1280], F32, 80 * KB)
        wsgu = at("wsgu", [P, 2, KD, F], F32, 80 * KB)
        xs = at("xs", [P, TT, D], F32, 144 * KB)
        z1 = at("z1", [P, TT, KD, P], F32, 160 * KB)
        u_sb = at("u_sb", [P, TT, DG], F32, 128 * KB)
        v_sb = at("v_sb", [P, TT, DG], F32, 168 * KB)
        o_sb = at("o_sb", [P, 2, D], F32, 32 * KB)
        h2p = at("h2p", [P, 2, KD, P], F32, 112 * KB)
        hg = at("hg", [P, KD, P], F32, 160 * KB)
        hthi = at("hthi", [P, KD, P], F32R, 164 * KB)
        htlo = at("htlo", [P, KD, P], F32R, 168 * KB)
        ysb = at("ysb", [P, D], F32, 172 * KB)
        b2 = at("b2", [P, D], F32, 176 * KB)
        ga2 = at("ga2", [P, D], F32, 180 * KB)
        junk = at("junk", [P, D], F32, 184 * KB)
        at_sb = at("at_sb", [P, 2, 1280], F32, 184 * KB)
        scores = at("scores", [P, TT, E], F32, 184 * KB)
        biased = at("biased", [P, TT, E], F32, 185 * KB)
        masked = at("masked", [P, TT, E], F32, 186 * KB)
        picked = at("picked", [P, TT, E], F32, 187 * KB)
        sel = at("sel", [P, TT, E], F32, 188 * KB)
        gates = at("gates", [P, TT, E], F32, 189 * KB)
        posm = at("posm", [P, TT, E], F32, 191 * KB)
        rank = at("rank", [P, TT, E], F32, 192 * KB)
        selb = at("selb", [P, TT, E], BF16, 193 * KB)
        small0 = 194 * KB
        smalls = [small0]

        def small(name, shape, dt):
            n = 1
            for s in shape[1:]:
                n *= s
            n *= 2 if dt == BF16 else 4
            t = at(name, shape, dt, smalls[0])
            smalls[0] += -(-n // 32) * 32
            return t

        posb = small("posb", [P, TT, COLS], F32)
        vtab = small("vtab", [P, TT, COLS, VC], BF16)
        restart = at("restart", [P, 1280], F32, 90 * KB)
        negmask = at("negmask", [P, P], BF16, small0 + 1024)
        wsp = at("wsp", [P, GROUPS, P], F32, small0 + 1280)
        sq = at("sq", [P, T], F32, small0 + 1280)
        wspt = at("wspt", [P, GROUPS, P], F32, small0 + 3328)
        ident = small("ident", [P, P], F32)
        identb = small("identb", [P, P], BF16)
        ones = small("ones", [P, P], F32)
        ustrb = small("ustrb", [P, P], BF16)
        onesb = small("onesb", [P, P], BF16)
        iotab = small("iotab", [P, P], BF16)
        s_onehot = at("s_onehot", [P, TT, P], BF16, 186 * KB)
        sg = small("sg", [P, F], F32)
        act_s = small("act_s", [P, KF, P], F32)
        acthi = at("acthi", [P, KF, P], F32R, 184 * KB)
        actlo = at("actlo", [P, KF, P], F32R, 185 * KB)
        sht = at("sht", [P, 2, KF, P], F32, 136 * KB)
        ysh = [at("ysh0", [P, D], F32, 140 * KB), at("ysh1", [P, D], F32, 172 * KB)]
        c_col = small("c_col", [P, KD], F32)
        sc_col = small("sc_col", [P, KD], F32)
        a1c = small("a1c", [P, KD], F32)
        b1c = small("b1c", [P, KD], F32)
        bsc = small("bsc", [P, KD], F32)
        bsh = small("bsh", [P, KD], F32)
        gpm = small("gpm", [P, KD], F32)
        gb = small("gb", [P, KD], F32)
        bsp = small("bsp", [P, GROUPS], F32)
        rb = small("rb", [P, E], F32)
        wr = at("wr", [P, KD, E], F32, 190 * KB)
        stat = small("stat", [P, 6, TT], F32)
        var = small("var", [P, 6, TT], F32)
        root = small("root", [P, 6, TT], F32)
        rs = small("rs", [P, 6, TT], F32)
        nt = small("nt", [P, TT], F32)
        top2 = at("top2", [P, TT, EG, 8], F32, 186 * KB)
        gs = small("gs", [P, TT, EG], F32)
        gcmp = at("gcmp", [P, TT, EG, EG], F32, 187 * KB)
        gcmp2 = at("gcmp2", [P, TT, EG, EG], F32, 188 * KB)
        gtri = at("gtri", [P, EG, EG], F32, 193 * KB + 512)
        gm = small("gm", [P, TT, EG], F32)
        top8 = small("top8", [P, TT, 8], F32)
        wsum = small("wsum", [P, TT], F32)
        ext = small("ext", [E, 2], F32)
        extb = small("extb", [E, 1], BF16)
        iot32 = small("iot32", [E, OVER], F32)
        iote = small("iote", [E, 1], F32)
        tmp32 = small("tmp32", [E, OVER], F32)
        selx = small("selx", [E, OVER], F32)
        jm = small("jm", [E, OVER], F32)
        nover = small("nover", [1, 1], I32)
        eid = small("eid", [1, OVER], I32)
        offs = small("offs", [P, OVER], F32)
        pair = small("pair", [P, 2], F32)
        inval = small("inval", [P, 1], F32)
        desti = small("desti", [P, 1], I32)
        idxg = small("idxg", [P, 1], I32)
        idxs = small("idxs", [P, 1], I32)
        vcur = small("vcur", [P, TT, VC], BF16)
        destr = at("destr", [P, COLS], I32, 187 * KB)
        gater = at("gater", [P, COLS], F32, 187 * KB + 512)
        assert base + smalls[0] <= nc.sbuf_usable_end, (base + smalls[0], nc.sbuf_usable_end)

        ps = ctx.enter_context(nc.psum_tensor("ps", [P, 8 * BANK], F32))

        def bank(b, n=1):
            return ps[:, b * BANK:(b + n) * BANK]

        h_rows = nc.dram_tensor("h_rows", [T, D], F32, kind="Internal").ap()
        y_rows = nc.dram_tensor("y_rows", [9 * T, D], F32, kind="Internal").ap()

        c_in = sem("c_in")
        x_in = [sem(f"x_in{t}") for t in range(TT)]
        vec_in = sem("vec_in")
        row_in = sem("row_in")
        grow_in = sem("grow_in")
        ada_in = [sem(f"ada_in{s}") for s in range(3)]
        ada_used = sem("ada_used")
        win_in = [sem(f"win_in{s}") for s in range(2)]
        wphi_ok = sem("wphi_ok")
        wplo_dve = sem("wplo_dve")
        wplo_pool = sem("wplo_pool")
        wo_in = [sem(f"wo_in{s}") for s in range(WO_RING)]
        wohi_ok = sem("wohi_ok")
        wolo_ok = sem("wolo_ok")
        wsgu_in = sem("wsgu_in")
        wsd_in = sem("wsd_in")
        wr_in = sem("wr_in")
        const_ok = sem("const_ok")
        pool_step = sem("pool_step")
        v_step = sem("v_step")
        a_step = sem("a_step")
        sc_ok = sem("sc_ok")
        sumsq = sem("sumsq")
        var_ok = sem("var_ok")
        root_ok = sem("root_ok")
        rs_g_ok = sem("rs_g_ok")
        rs_sb_ok = sem("rs_sb_ok")
        z_ok = sem("z_ok")
        acc_ok = sem("acc_ok")
        mod_mm = sem("mod_mm")
        row_ok = sem("row_ok")
        ab_ok = sem("ab_ok")
        h1_tr = sem("h1_tr")
        h1_act = sem("h1_act")
        h1_dve = sem("h1_dve")
        wsp_tr = sem("wsp_tr")
        wsp_ok = sem("wsp_ok")
        proj_mm = sem("proj_mm")
        proj_ev = sem("proj_ev")
        vmean_ok = sem("vmean_ok")
        vn_ok = sem("vn_ok")
        mixed_mm = sem("mixed_mm")
        og_ok = sem("og_ok")
        og_tr = sem("og_tr")
        og_ev = sem("og_ev")
        og_lo = sem("og_lo")
        z_mm = sem("z_mm")
        restart_ok = sem("restart_ok")
        beta_ok = sem("beta_ok")
        att_ok = sem("att_ok")
        att_tr = sem("att_tr")
        a_ok = sem("a_ok")
        o_mm = sem("o_mm")
        o_ev = sem("o_ev")
        o_lo = sem("o_lo")
        rs_x_ok = sem("rs_x_ok")
        ss_mm = sem("ss_mm")
        wo_mm = sem("wo_mm")
        wo_a = sem("wo_a")
        wo_o = sem("wo_o")
        wo_x = sem("wo_x")
        h2_ok = sem("h2_ok")
        h2_out = [sem(f"h2_out{s}") for s in range(2)]
        h2_tr = sem("h2_tr")
        h2_ev = sem("h2_ev")
        lg_mm = sem("lg_mm")
        sig_ok = sem("sig_ok")
        sgu_mm = sem("sgu_mm")
        ssg_ok = sem("ssg_ok")
        sact_ok = sem("sact_ok")
        sat_tr = sem("sat_tr")
        sat_ev = sem("sat_ev")
        sdn_mm = sem("sdn_mm")
        sdn_ev = sem("sdn_ev")
        ysh_out = [sem(f"ysh_out{s}") for s in range(2)]
        sel_ok = sem("sel_ok")
        cnt_mm = sem("cnt_mm")
        count_mm = sem("count_mm")
        ext_ok = sem("ext_ok")
        start_mm = sem("start_mm")
        selx_ok = sem("selx_ok")
        over_mm = sem("over_mm")
        over_ok = sem("over_ok")
        fill_ok = sem("fill_ok")
        w_in_sem = [[sem(f"w_in{s}{p}") for p in range(3)] for s in range(2)]
        wx_in = [sem(f"wx_in{p}") for p in range(3)]
        hi_ok = sem("hi_ok")
        lo_dve = sem("lo_dve")
        lo_pool = sem("lo_pool")
        onehot_ok = sem("onehot_ok")
        idx_mm = sem("idx_mm")
        idx_ok = sem("idx_ok")
        gather_go = sem("gather_go")
        scatter_go = sem("scatter_go")
        gathered = sem("gathered")
        ht_tr = sem("ht_tr")
        hthi_ok = sem("hthi_ok")
        htlo_ok = sem("htlo_ok")
        gu_mm = sem("gu_mm")
        silu_ok = sem("silu_ok")
        act_ok = sem("act_ok")
        at_tr = sem("at_tr")
        acthi_ok = sem("acthi_ok")
        actlo_ok = sem("actlo_ok")
        dn_mm = sem("dn_mm")
        y_ok = sem("y_ok")
        idxs_ok = sem("idxs_ok")
        scattered = sem("scattered")
        v_loop = sem("v_loop")
        y_in = [sem(f"y_in{t}_{g}") for t in range(TT) for g in range(3)]
        ypool_ok = sem("ypool_ok")
        ysum_ok = sem("ysum_ok")
        out_ok = sem("out_ok")
        out_done = sem("out_done")

        ada_v = w_ada.rearrange("(p k) n -> p k n", k=KD)
        win_v = w_in.rearrange("(p k) n -> p k n", k=KD)
        wo_v = w_out.rearrange("(k p) n -> p k n", p=P)
        wg_v = w_gate.rearrange("e (p k) f -> e p (k f)", k=KD)
        wu_v = w_up.rearrange("e (p k) f -> e p (k f)", k=KD)
        wd_v = w_down.rearrange("e (p k) n -> e p (k n)", k=KF)
        y_v = y_rows.rearrange("(r t p) n -> t p r n", r=9, p=P)

        SC1, SH1, GA1, SC2, SH2, GA2 = 1, 0, 2, 4, 3, 5
        def ada_slot(n):
            slots = [m % 3 if m < 9 else m % 2 for m in range(n + 1)]
            same = [m for m in range(n + 1) if slots[m] == slots[n]]
            return slots[n], len(same), same[-2] if len(same) > 1 else None

        CHUNKS = [SC1, SH1, GA1, SC2, SH2, GA2]
        COLG = [DG, 0, 2 * DG, 2 * DG + 512, 2 * DG + 1024]
        PIECES = 2 * len(COLG)

        H1_BANK = [0, 1, 2, 3, 4, 5, 6, 4]
        H2_BANK = [6, 2, 0, 4]
        SH_BANK = [3, 1, 1, 3]

        ZOFF = {3: 0, 2: 512, 0: 896, 1: 1024}
        ZW = {t: P * (t + 1) for t in range(TT)}
        AOFF = {j: ZOFF[TT - 1 - j] for j in range(TT)}
        AW = {j: T - P * j for j in range(TT)}

        ST_X, ST_VS, ST_V, ST_G, ST_S, ST_O = range(6)

        def part(tile, slot, piece, c0, c1):
            if tile is whi:
                piece = (1, 2, 0)[piece]
            if isinstance(slot, int):
                return tile[:, slot, piece, c0:c1]
            return tile[:, bass.ds(slot, 1), piece, c0:c1].rearrange("p s f -> p (s f)")

        def pair_out(ac, A, ct):
            ac.wait_ge(o_mm, 2 * ct + 2)
            if ct >= 1:
                ac.wait_ge(ss_mm, ct)
            A(sq[:, :], bank(6), ACT.Square)
            A(mixhi[1][:, ct, :], bank(6), ACT.Copy, scale=gb[:, 4 + ct:5 + ct]).then_inc(o_ev, 1)

        block = ctx.enter_context(nc.Block())

        @block.sync
        def _(sp):
            sp.dma_start(c_col[:, :], c.rearrange("(p k) -> p k", k=KD)).then_inc(c_in, 16)
            for n in range(4 * len(CHUNKS)):
                g, q = CHUNKS[n // 4], n % 4
                if n == 2:
                    for t in range(TT):
                        sp.dma_start(xs[:, t, :], x[t * P:(t + 1) * P, :]).then_inc(x_in[t], 16)
                slot, _, before = ada_slot(n)
                if before is not None:
                    sp.wait_ge(ada_used, before + 1)
                if n == 16:
                    sp.wait_ge(row_ok, 1)
                    sp.dma_start(grow[:, :], g_pre_ffn.partition_broadcast(P)).then_inc(grow_in, 16)
                if n == 21:
                    sp.wait_ge(row_ok, 2)
                    sp.dma_start(grow[:, :], g_post_ffn.partition_broadcast(P)).then_inc(grow_in, 16)
                sp.dma_start(ada[slot][:, :, :], ada_v[:, 2 * q:2 * q + 2, g * D:(g + 1) * D])\
                  .then_inc(ada_in[slot], 16)

            sp.wait_ge(proj_mm, 4 * PIECES)
            for n in range(2 * KD):
                if n >= WO_RING:
                    sp.wait_ge(wohi_ok, n - WO_RING + 1)
                    sp.wait_ge(wolo_ok, n - WO_RING + 1)
                sp.dma_start(woraw[:, n % WO_RING], wo_v[:, n // 2, (n % 2) * 512:(n % 2 + 1) * 512])\
                  .then_inc(wo_in[n % WO_RING], 16)

            def load_piece(e, slot, sems, p_):
                sp.dma_start(raw[:, slot, p_, :], (wg_v, wu_v, wd_v)[p_][bass.ds(e, 1)].rearrange("e p f -> p (e f)"))\
                  .then_inc(sems[p_], 16)

            def load(e, slot, sems, before):
                for p_ in range(3):
                    before(p_)
                    load_piece(e, slot, sems, p_)

            def freed(n):
                sp.wait_ge(lo_dve, n)
                sp.wait_ge(lo_pool, n)

            for t in range(TT):
                if t == TT - 1:
                    sp.wait_ge(wo_mm, TT)
                    for p_ in range(3):
                        load_piece(0, 0, w_in_sem[0], p_)
                    load_piece(1, 1, w_in_sem[1], 0)
                sp.wait_ge(h2_ok, t + 1)
                sp.dma_start(h_rows[t * P:(t + 1) * P, :], h2p[:, t % 2].rearrange("p k q -> p (k q)"))\
                  .then_inc(h2_out[t % 2], 16)
            load_piece(1, 1, w_in_sem[1], 1)
            load_piece(1, 1, w_in_sem[1], 2)
            for t in range(TT):
                for p_ in ((0,), (1,), (2, 3, 4), ())[t]:
                    freed(1 + p_)
                    load_piece(2 + p_ // 3, p_ // 3, w_in_sem[p_ // 3], p_ % 3)
                sp.wait_ge(sdn_ev, t + 1)
                sp.dma_start(y_rows[8 * T + t * P:8 * T + (t + 1) * P, :], ysh[t % 2][:, :])\
                  .then_inc(ysh_out[t % 2], 16)
            freed(6)
            load_piece(3, 1, w_in_sem[1], 2)
            with sp.Fori(2, E // 2) as i:
                for s in range(2):
                    load(i * 2 + s, s, w_in_sem[s], lambda p_: freed(i * 6 + (3 * s - 5 + p_)))
            sp.wait_ge(over_ok, 1)
            n = sp.value_load(nover[0:1, 0:1], min_val=0, max_val=OVER)
            with sp.If(n > 0):
                with sp.Fori(0, n) as j:
                    e = sp.value_load(eid[0:1, bass.ds(j, 1)], min_val=0, max_val=E - 1)
                    load(e, 0, wx_in, lambda p_: freed(j * 3 + (3 * (E - 1) + 1 + p_)))
            sp.wait_ge(scattered, n * 16 + 16 * E)
            for t in range(TT):
                if t == 0:
                    sp.wait_ge(ysh_out[0], 16 * TT // 2)
                    sp.wait_ge(ysh_out[1], 16 * TT // 2)
                for g in range(3):
                    sp.dma_start(yall[:, t, 3 * g:3 * g + 3], y_v[t][:, 3 * g:3 * g + 3]).then_inc(y_in[3 * t + g], 16)
            for t in range(TT):
                sp.wait_ge(out_ok, t + 1)
                sp.dma_start(out[t * P:(t + 1) * P, :], xs[:, t, :]).then_inc(out_done, 16)
            sp.wait_ge(out_done, 16 * TT)

        @block.gpsimd
        def _(gp):
            step = [0]

            def then(ins):
                step[0] += 1
                ins.then_inc(pool_step, 1)
                gp.wait_ge(pool_step, step[0])

            last_row, last_routed = gp.to_reg(T - 1), gp.to_reg(TOPK * T - 1)

            def pick(tile, op, fill, pattern, mult, base_=0):
                return gp.affine_select(out=tile, in_=tile, compare_op=op, fill=fill, base=base_,
                                        pattern=pattern, channel_multiplier=mult)

            gp.memset(ones[:, :], 1.0)
            gp.memset(onesb[:, :], 1.0)
            gp.memset(ident[:, :], 0.0)
            gp.memset(identb[:, :], 0.0)
            gp.memset(negmask[:, :], 0.0)
            gp.memset(ustrb[:, :], 1.0)
            gp.iota(iotab[:, :], [[1, P]], base=0, channel_multiplier=0, allow_small_or_imprecise_dtypes=True)
            gp.iota(iot32[:, :], [[1, OVER]], base=0, channel_multiplier=0, allow_small_or_imprecise_dtypes=True)
            then(gp.iota(iote[:, :], [[0, 1]], base=0, channel_multiplier=1, allow_small_or_imprecise_dtypes=True))
            pick(ident[:, :], ALU.not_equal, 1.0, [[-1, P]], 1)
            pick(identb[:, :], ALU.not_equal, 1.0, [[-1, P]], 1)
            pick(negmask[:, :], ALU.is_gt, NEG, [[-1, P]], 1)
            then(pick(ustrb[:, :], ALU.is_gt, 0.0, [[1, P]], -1))
            gp.sem_inc(const_ok, 1)

            for i in range(PIECES + 1):
                if i < PIECES:
                    if i == 0:
                        gp.wait_ge(ada_used, 6)
                    if i >= 2:
                        gp.wait_ge(wphi_ok, i - 1)
                        gp.wait_ge(wplo_dve, i - 1)
                        gp.wait_ge(wplo_pool, i - 1)
                    g, h = i // 2, i % 2
                    gp.dma_start(wraw[:, i % 2], win_v[:, KH * h:KH * (h + 1), COLG[g]:COLG[g] + 512])\
                      .then_inc(win_in[i % 2], 16)
                if i >= 1:
                    j = i - 1
                    gp.wait_ge(wphi_ok, j + 1)
                    gp.tensor_tensor(wplo[:, j % 2, KH // 2:], wraw[:, j % 2, KH // 2:],
                                     wphi[:, j % 2, KH // 2:].bitcast(F32), ALU.subtract).then_inc(wplo_pool, 1)
            gp.wait_ge(proj_mm, 4 * PIECES)
            then(gp.memset(restart[:, :], 0.0))
            for t in range(TT):
                ins = gp.memset(restart[:, ZOFF[t] + ZW[t] - 1:ZOFF[t] + ZW[t]], 1.0)
            ins.then_inc(restart_ok, 1)
            gp.wait_ge(row_ok, 4)
            for j in range(2 * KD):
                gp.wait_ge(wohi_ok, j + 1)
                cols = slice((j % 2) * 512, (j % 2 + 1) * 512)
                gp.tensor_tensor(wolo[:, j // 2, cols], woraw[:, j % WO_RING], wohi[:, j // 2, cols].bitcast(F32),
                                 ALU.subtract).then_inc(wolo_ok, 1)
            gp.wait_ge(o_mm, HEADS)
            gp.wait_ge(a_ok, HEADS)
            gp.dma_start(wsgu[:, 0], ws_gate.rearrange("(p k) f -> p k f", k=KD)).then_inc(wsgu_in, 16)
            gp.dma_start(wsgu[:, 1], ws_up.rearrange("(p k) f -> p k f", k=KD)).then_inc(wsgu_in, 16)
            gp.dma_start(wr[:, :, :], w_router.rearrange("(p k) e -> p k e", k=KD)).then_inc(wr_in, 16)
            gp.wait_ge(wo_mm, TT)
            gp.dma_start(wsd[:, :, :], ws_down.rearrange("(p k) n -> p k n", k=KF)).then_inc(wsd_in, 16)
            gp.memset(posb[:, :, E:COLS], -1.0)
            then(gp.memset(vtab[:, :, :, :], 0.0))
            for t in range(TT):
                then(gp.iota(vtab[:, t, :, 0], [[0, COLS]], base=t * P, channel_multiplier=0,
                             allow_small_or_imprecise_dtypes=True))
                then(gp.iota(vtab[:, t, :, 1], [[0, COLS]], base=1, channel_multiplier=1,
                             allow_small_or_imprecise_dtypes=True))
            gp.sem_inc(const_ok, 1)

            def gather(b):
                gp.wait_ge(idx_ok, b + 1)
                gp.sem_inc(gather_go, 1)
                gp.indirect_dma_start(out=hg[:, :, :].rearrange("p k q -> p (k q)"), out_offset=None,
                                      in_=h_rows, in_offset=bass.IndirectOffsetOnAxis(ap=idxg[:, 0:1], axis=0),
                                      bounds_check=last_row, oob_is_err=False).then_inc(gathered, 16)

            def scatter(b):
                gp.wait_ge(y_ok, b + 1)
                gp.wait_ge(idxs_ok, b + 1)
                gp.sem_inc(scatter_go, 1)
                gp.indirect_dma_start(out=y_rows, out_offset=bass.IndirectOffsetOnAxis(ap=idxs[:, 0:1], axis=0),
                                      in_=ysb[:, :], in_offset=None,
                                      bounds_check=last_routed, oob_is_err=False).then_inc(scattered, 16)

            def low_raw(b, wslot, rslot, piece):
                gp.wait_ge(hi_ok, b * 3 + (piece + 1))
                c0 = 2048 - POOL_K * 256
                gp.tensor_tensor(part(wlo, wslot, piece, c0, 2048), raw[:, rslot, piece, c0:2048],
                                 part(whi, wslot, piece, c0, 2048).bitcast(F32), ALU.subtract)\
                  .then_inc(lo_pool, 1)

            def one(b, wslot, rslot, first):
                low_raw(b, wslot, rslot, 0)
                low_raw(b, wslot, rslot, 1)
                gather(b + 1)
                low_raw(b, wslot, rslot, 2)
                if first != 0 and first != 1:
                    scatter(b - 2)

            gp.wait_ge(wo_mm, TT)
            then(gp.memset(hg[:, :, :], 0.0))
            gp.wait_ge(h2_out[0], 16 * TT // 2)
            gp.wait_ge(h2_out[1], 16 * TT // 2)
            for p_ in range(3):
                gp.wait_ge(hi_ok, p_ + 1)
                gp.tensor_tensor(part(wlo, 0, p_, 0, 2048), raw[:, 0, p_, :],
                                 part(whi, 0, p_, 0, 2048).bitcast(F32), ALU.subtract).then_inc(lo_pool, 1)
            gp.wait_ge(idx_ok, 1)
            gp.indirect_dma_start(out=hg[:, :, :].rearrange("p k q -> p (k q)"), out_offset=None,
                                  in_=h_rows, in_offset=bass.IndirectOffsetOnAxis(ap=idxg[:, 0:1], axis=0),
                                  bounds_check=last_row, oob_is_err=False).then_inc(gathered, 16)
            gather(1)
            one(1, 1, 1, 1)
            one(2, 0, 0, 2)
            gp.wait_ge(over_ok, 1)
            n = gp.value_load(nover[0:1, 0:1], min_val=0, max_val=OVER)
            with gp.If(n > 0):
                with gp.Fori(0, n) as j:
                    e = gp.value_load(eid[0:1, bass.ds(j, 1)], min_val=0, max_val=E - 1)
                    gp.tensor_tensor(posb[:, :, bass.ds(j + E, 1)].rearrange("p t b -> p (t b)"),
                                     posb[:, :, bass.ds(e, 1)].rearrange("p t b -> p (t b)"),
                                     offs[:, bass.ds(j, 1)].to_broadcast([P, TT]), ALU.add)
                    gp.tensor_copy(vtab[:, :, bass.ds(j + E, 1), :].rearrange("p t b v -> p t (b v)"),
                                   vtab[:, :, bass.ds(e, 1), :].rearrange("p t b v -> p t (b v)"))
            gp.sem_inc(fill_ok, 1)
            one(3, 1, 1, 2)
            with gp.Fori(2, E // 2) as i:
                for s in range(2):
                    one(i * 2 + s, s, s, 2)
            with gp.If(n > 0):
                with gp.Fori(E, n + E) as b:
                    one(b, b % 2, 0, 2)
            scatter(n + (E - 2))
            scatter(n + (E - 1))
            for t in range(TT):
                gp.wait_ge(y_in[3 * t + 1], 16)
                then(gp.tensor_tensor(yall[:, t, 3], yall[:, t, 3], yall[:, t, 4], ALU.add))
                gp.tensor_tensor(yall[:, t, 3], yall[:, t, 3], yall[:, t, 5], ALU.add).then_inc(ypool_ok, 1)

        @block.scalar
        def _(ac):
            A = nc.scalar.activation
            step = [0]

            def then(ins):
                step[0] += 1
                ins.then_inc(a_step, 1)
                ac.wait_ge(a_step, step[0])

            def load(dst, src):
                ac.dma_start(dst, src).then_inc(vec_in, 16)

            def load_row(dst, src):
                ac.dma_start(dst, src).then_inc(row_in, 16)

            load(bsc[:, :], b_ada[SC1 * D:(SC1 + 1) * D].rearrange("(p k) -> p k", k=KD))
            load(bsh[:, :], b_ada[SH1 * D:(SH1 + 1) * D].rearrange("(p k) -> p k", k=KD))
            load(gpm[:, :], g_pre_mix.rearrange("(p k) -> p k", k=KD))
            load(wsp[:, :, :], w_spatial.rearrange("g i j -> i g j"))
            with nc.allow_non_contiguous_dma(reason="two short vectors by column"):
                load(gb[:, :], g_branch.rearrange("(k p) -> p k", p=P))
                load(bsp[:, :], b_spatial.rearrange("g i -> i g"))
            ac.wait_ge(c_in, 16)
            A(sc_col[:, :], c_col[:, :], ACT.Silu).then_inc(sc_ok, 1)
            roots = [0]

            def take_root(st, c0=0, c1=TT):
                roots[0] += 1
                ac.wait_ge(var_ok, roots[0])
                A(root[:, st, c0:c1], var[:, st, c0:c1], ACT.Sqrt).then_inc(root_ok, 1)

            for t in range(TT):
                ac.wait_ge(x_in[t], 16)
                ins = A(junk[:, :], xs[:, t, :], ACT.Square, accum_out=stat[:, ST_X, t:t + 1])
                ins.then_inc(sumsq, 1) if t == TT - 1 else then(ins)
            take_root(ST_X)
            ac.wait_ge(rs_x_ok, 1)
            for t in range(TT):
                A(z1[:, t].rearrange("p k q -> p q k"), xs[:, t, :].rearrange("p (q k) -> p q k", k=KD),
                  ACT.Copy, scale=rs[:, ST_X, t:t + 1]).then_inc(z_ok, 1)
            def piece_high(i):
                ac.wait_ge(win_in[i % 2], 16 * (i // 2 + 1))
                if i >= 2:
                    ac.wait_ge(proj_mm, 4 * (i - 1))
                A(wphi[:, i % 2], wraw[:, i % 2], ACT.Copy).then_inc(wphi_ok, 1)

            ac.wait_ge(ab_ok, 1)
            for k in range(KD):
                ac.wait_ge(h1_tr, k + 1)
                if k >= 2:
                    ac.wait_ge(h1_dve, k - 1)
                A(h1f[:, k % 2], bank(H1_BANK[k]), ACT.Identity, bias=b1c[:, k:k + 1], scale=a1c[:, k:k + 1])\
                    .then_inc(h1_act, 1)
                if k == KH - 1:
                    piece_high(0)

            def evacuate(g):
                for m in range(4):
                    ac.wait_ge(proj_mm, 8 * g + 4 + m + 1)
                    src = bank(m)
                    if g == 0:
                        ins = A(v_sb[:, m, :], src, ACT.Gelu_apprx_tanh, accum_out=stat[:, ST_VS, m:m + 1])
                    elif g == 1:
                        ins = A(u_sb[:, m, :], src, ACT.Gelu_apprx_tanh)
                    elif g == 2:
                        ins = A(qt[:, m, :], src, ACT.Copy, scale=HD ** -0.5)
                    elif g == 3:
                        ins = A(kt[:, m, :], src, ACT.Copy)
                    else:
                        ins = A(vv[:, m, :], src, ACT.Copy)
                    ins.then_inc(proj_ev, 1)

            def gated_out(k):
                ac.wait_ge(og_tr, k + 1)
                A(mixhi[0][:, k, :], bank(4 + k % 2), ACT.Copy, scale=gb[:, k:k + 1]).then_inc(og_ev, 1)

            piece_high(1)
            piece_high(2)
            evacuate(0)
            ac.wait_ge(ada_used, 9)
            load_row(lng[:, :], ln_sgu_g.partition_broadcast(P))
            load_row(lnb[:, :], ln_sgu_b.partition_broadcast(P))
            load_row(ga1[:, :], b_ada[GA1 * D:(GA1 + 1) * D].partition_broadcast(P))
            load_row(a2[:, :], b_ada[SC2 * D:(SC2 + 1) * D].partition_broadcast(P))
            load_row(b2[:, :], b_ada[SH2 * D:(SH2 + 1) * D].partition_broadcast(P))
            load_row(ga2[:, :], b_ada[GA2 * D:(GA2 + 1) * D].partition_broadcast(P))
            load_row(rb[:, :], router_bias.partition_broadcast(P))
            ac.dma_start(grow[:, :], g_post_mix.partition_broadcast(P)).then_inc(grow_in, 16)

            piece_high(3)
            piece_high(4)
            ac.wait_ge(vmean_ok, 1)
            for t in range(TT):
                ins = A(junk[:, 0:DG], v_sb[:, t, :], ACT.Square, accum_out=stat[:, ST_V, t:t + 1])
                ins.then_inc(sumsq, 1) if t == TT - 1 else then(ins)
            take_root(ST_V)
            evacuate(1)
            piece_high(5)
            piece_high(6)
            evacuate(2)
            piece_high(7)
            piece_high(8)
            evacuate(3)
            gated_out(0)
            gated_out(1)
            piece_high(9)
            gated_out(2)
            gated_out(3)
            for t in range(TT):
                ins = A(junk[:, 0:DG], u_sb[:, t, :], ACT.Square, accum_out=stat[:, ST_G, t:t + 1])
                ins.then_inc(sumsq, 1) if t == TT - 1 else then(ins)
            ac.wait_ge(sumsq, 3)
            evacuate(4)
            take_root(ST_G)
            for h in range(HEADS + 1):
                if h < HEADS:
                    ac.wait_ge(z_mm, h + 1)
                    if h >= 2:
                        ac.wait_ge(att_tr, h - 1)
                    A(beta[:, h % 2], ps[:, 0:1280], ACT.Sigmoid).then_inc(beta_ok, 1)
                    A(rest[:, h % 2], ps[:, 0:1280], ACT.Sigmoid, scale=-1.0).then_inc(beta_ok, 1)
                if h >= 1:
                    g = h - 1
                    ac.wait_ge(att_tr, g + 1)
                    if g >= 2:
                        ac.wait_ge(o_mm, g - 1)
                    A(at_sb[:, g % 2, :], ps[:, 3 * BANK:3 * BANK + 1280], ACT.Copy).then_inc(a_ok, 1)
                if h < HEADS:
                    for n in (2 * h, 2 * h + 1):
                        ac.wait_ge(wo_in[n % WO_RING], 16 * (n // WO_RING + 1))
                        A(wohi[:, n // 2, (n % 2) * 512:(n % 2 + 1) * 512], woraw[:, n % WO_RING], ACT.Copy)\
                            .then_inc(wohi_ok, 1)
                if h >= 3 and h % 2 == 1:
                    pair_out(ac, A, (h - 3) // 2)
            pair_out(ac, A, 3)
            take_root(ST_X)
            def shared_silu(t):
                ac.wait_ge(sgu_mm, t + 1)
                if t >= 1:
                    ac.wait_ge(sact_ok, t)
                A(sg[:, :], bank(SH_BANK[t])[:, 0:F], ACT.Silu).then_inc(ssg_ok, 1)

            def shared_evac(t):
                ac.wait_ge(sat_tr, t + 1)
                if t >= 2:
                    ac.wait_ge(sdn_mm, t - 1)
                A(sht[:, t % 2], bank(6)[:, 0:F].rearrange("p (k q) -> p k q", k=KF), ACT.Copy)\
                    .then_inc(sat_ev, 1)

            def shared_rows(t):
                ac.wait_ge(sdn_mm, t + 1)
                if t >= 2:
                    ac.wait_ge(ysh_out[t % 2], 16)
                A(ysh[t % 2][:, :], bank(4, 2), ACT.Copy).then_inc(sdn_ev, 1)

            def high(b, wslot, rslot, piece, landed):
                ac.wait_ge(*landed)
                A(part(whi, wslot, piece, 0, 2048), raw[:, rslot, piece, :], ACT.Copy).then_inc(hi_ok, 1)

            def branch_g(t):
                ac.wait_ge(wo_mm, t + 1)
                if t == 0:
                    ac.wait_ge(rs_g_ok, 1)
                    ac.wait_ge(rs_sb_ok, 1)
                if t >= 2:
                    ac.wait_ge(h2_ok, t - 1)
                b0 = (t % 2) * 4
                A(o_sb[:, t % 2, :], bank(b0, 2), ACT.Copy, scale=rs[:, ST_G, t:t + 1]).then_inc(wo_a, 1)

            def squares_s(t):
                ac.wait_ge(wo_o, t + 1)
                A(junk[:, :], o_sb[:, t % 2, :], ACT.Square, accum_out=stat[:, ST_S, t:t + 1]).then_inc(sumsq, 1)

            def squares_o(t):
                ac.wait_ge(wo_x, t + 1)
                A(junk[:, :], xs[:, t, :], ACT.Square, accum_out=stat[:, ST_O, t:t + 1]).then_inc(sumsq, 1)

            def rows_out(t):
                ac.wait_ge(h2_tr, t + 1)
                A(h2t[:, :, t * P:(t + 1) * P], bank(H2_BANK[t], 2).rearrange("p (k q) -> p k q", k=KD), ACT.Copy)\
                    .then_inc(h2_ev, 1)

            def silu(b):
                ac.wait_ge(gu_mm, b + 1)
                A(sg[:, :], bank(2)[:, 0:F], ACT.Silu).then_inc(silu_ok, 1)

            def ht_high(b):
                ac.wait_ge(ht_tr, b + 1)
                A(hthi[:, :, :], bank(0, 2).rearrange("p (k q) -> p k q", k=KD), ACT.Copy).then_inc(hthi_ok, 1)

            for t in range(TT):
                branch_g(t)
                if t >= 2:
                    rows_out(t - 2)
                if t >= 1:
                    take_root(ST_O, t - 1, t)
                squares_s(t)
                take_root(ST_S, t, t + 1)
                if t == TT - 1:
                    rows_out(2)
                squares_o(t)
            take_root(ST_O, TT - 1, TT)
            shared_silu(0)
            high(0, 0, 0, 0, (w_in_sem[0][0], 16))
            rows_out(TT - 1)
            ac.wait_ge(lg_mm, 1)
            A(scores[:, :, :], ps[:, 2 * BANK:2 * BANK + TT * E].rearrange("p (t e) -> p t e", t=TT),
              ACT.Sigmoid).then_inc(sig_ok, 1)
            high(0, 0, 0, 1, (w_in_sem[0][1], 16))
            shared_evac(0)
            shared_silu(1)
            shared_rows(0)
            shared_evac(1)
            high(0, 0, 0, 2, (w_in_sem[0][2], 16))
            shared_rows(1)
            shared_silu(2)
            shared_silu(3)
            shared_evac(2)
            ht_high(0)
            high(1, 1, 1, 0, (w_in_sem[1][0], 16))
            shared_evac(3)
            high(1, 1, 1, 1, (w_in_sem[1][1], 16))
            shared_rows(2)
            ac.wait_ge(sact_ok, TT)
            silu(0)
            ht_high(1)
            shared_rows(3)
            ac.wait_ge(ysh_out[0], 16 * TT // 2)
            high(1, 1, 1, 2, (w_in_sem[1][2], 16))

            def y_out(b):
                ac.wait_ge(scattered, b * 16)
                A(ysb[:, :], bank(4, 2), ACT.Copy).then_inc(y_ok, 1)

            def one(b, wslot, rslot, landed, first):
                high(b, wslot, rslot, 0, landed[0])
                high(b, wslot, rslot, 1, landed[1])
                silu(b - 1)
                ht_high(b)
                ac.wait_ge(dn_mm, b - 1)
                high(b, wslot, rslot, 2, landed[2])
                if first:
                    ac.wait_ge(ysh_out[1], 16 * TT // 2)
                    A(ysb[:, :], bank(4, 2), ACT.Copy).then_inc(y_ok, 1)
                else:
                    y_out(b - 2)

            one(2, 0, 0, [(w_in_sem[0][p_], 32) for p_ in range(3)], True)
            one(3, 1, 1, [(w_in_sem[1][p_], 32) for p_ in range(3)], False)
            with ac.Fori(2, E // 2) as i:
                for s in range(2):
                    one(i * 2 + s, s, s, [(w_in_sem[s][p_], i * 16 + 16) for p_ in range(3)], False)
            ac.wait_ge(over_ok, 1)
            n = ac.value_load(nover[0:1, 0:1], min_val=0, max_val=OVER)
            with ac.If(n > 0):
                with ac.Fori(E, n + E) as b:
                    one(b, b % 2, 0, [(wx_in[p_], b * 16 - 16 * (E - 1)) for p_ in range(3)], False)
            silu(n + (E - 1))
            ac.wait_ge(dn_mm, n + (E - 1))
            y_out(n + (E - 2))
            ac.wait_ge(dn_mm, n + E)
            y_out(n + (E - 1))
            for t in range(TT):
                ac.wait_ge(ysum_ok, t + 1)
                A(junk[:, :], yall[:, t, 0, :], ACT.Square, accum_out=stat[:, ST_S, t:t + 1]).then_inc(sumsq, 1)
                take_root(ST_S, t, t + 1)

        @block.tensor
        def _(pe):
            mm = pe.matmul

            def transpose(o, i):
                return pe.transpose(o, i, ident[:, :])

            pe.wait_ge(const_ok, 1)
            pe.wait_ge(z_ok, TT)

            def h1_transposes(k):
                for t in range(TT):
                    ins = transpose(bank(H1_BANK[k])[:, t * P:(t + 1) * P], z1[:, t, k, :])
                ins.then_inc(h1_tr, 1)

            for k in range(KD - 1):
                h1_transposes(k)
            for ch in range(2):
                pe.wait_ge(acc_ok, ch + 1)
                cols = acc[:, ch, :].rearrange("p (q k) -> p k q", k=KD)
                for k in range(KD):
                    ins = mm(ps[:, 7 * BANK + ch * KD + k:7 * BANK + ch * KD + k + 1], cols[:, k, :],
                             ones[:, 0:1], start=True, stop=True)
                ins.then_inc(mod_mm, 1)
            pe.wait_ge(h1_act, H1_BANK[KD - 1] + 1)
            h1_transposes(KD - 1)

            def modulation_row(ch):
                pe.wait_ge(acc_ok, ch + 1)
                if ch > 2:
                    pe.wait_ge(row_ok, ch - 2)
                for hf in range(2):
                    ins = mm(bank(6 + hf), ones[:, :], acc[:, ch % 2, hf * 512:(hf + 1) * 512],
                             start=True, stop=True)
                ins.then_inc(mod_mm, 1)

            def project(i):
                g, h = i // 2, i % 2
                pe.wait_ge(wplo_dve, i + 1)
                pe.wait_ge(wplo_pool, i + 1)
                if i < 2:
                    pe.wait_ge(h1_dve, KH * (i + 1))
                for m in range(4):
                    if h == 0 and g >= 1:
                        pe.wait_ge(proj_ev, 4 * (g - 1) + m + 1)
                    for k in range(KH):
                        wh, wl = wphi[:, i % 2, k, :], wplo[:, i % 2, k, :]
                        hh, hl = h1hi[:, KH * h + k, :], h1lo[:, KH * h + k, :]
                        for n, (w, x_) in enumerate(((wh, hh), (wl, hh), (wh, hl))):
                            if g in (2, 3):
                                st, mv = w[:, m * P:(m + 1) * P], x_
                            else:
                                st, mv = x_[:, m * P:(m + 1) * P], w
                            ins = mm(bank(m), st, mv, start=(h == 0 and k == 0 and n == 0),
                                     stop=(h == 1 and k == KH - 1 and n == 2))
                    ins.then_inc(proj_mm, 1)

            def mix(g):
                if g >= 2:
                    pe.wait_ge(og_ok, g - 1)
                mm(bank(4 + g % 2), wspt[:, g, :], v_sb[:, :, g * P:(g + 1) * P], start=True, stop=True)\
                    .then_inc(mixed_mm, 1)

            def gated_tr(k):
                if k >= 2:
                    pe.wait_ge(og_lo, k - 1)
                for t in range(TT):
                    ins = transpose(bank(4 + k % 2)[:, t * P:(t + 1) * P], u_sb[:, t, k * P:(k + 1) * P])
                ins.then_inc(og_tr, 1)

            project(0)
            project(1)
            pe.wait_ge(h1_act, KD)
            pe.wait_ge(vec_in, 16 * 6)
            for g in range(GROUPS):
                ins = transpose(bank(4)[:, g * P:(g + 1) * P], wsp[:, g, :])
            ins.then_inc(wsp_tr, 1)
            project(2)
            project(3)
            modulation_row(2)
            project(4)
            project(5)
            modulation_row(3)
            pe.wait_ge(wsp_ok, 1)
            pe.wait_ge(vn_ok, 1)
            mix(0)
            mix(1)
            project(6)
            mix(2)
            mix(3)
            project(7)
            modulation_row(4)
            pe.wait_ge(og_ok, GROUPS)
            gated_tr(0)
            gated_tr(1)
            project(8)
            gated_tr(2)
            gated_tr(3)
            project(9)
            pe.wait_ge(og_lo, 4)
            pe.wait_ge(proj_ev, 20)

            def scores_mm(h):
                r0, ct = HD * (h % 2), h // 2
                if h >= 1:
                    pe.wait_ge(beta_ok, 2 * h)
                for t in (3, 2, 0, 1):
                    mm(ps[:, ZOFF[t]:ZOFF[t] + ZW[t]], qt[r0:r0 + HD, ct, t * P:(t + 1) * P],
                       kt[r0:r0 + HD, ct, 0:ZW[t]], start=(t != 0), stop=True, skip_group_check=True)
                for t in (3, 2, 0, 1):
                    o = ZOFF[t] + P * t
                    ins = mm(ps[:, o:o + P], identb[:, :], negmask[:, :], start=False, stop=True,
                             skip_group_check=True)
                ins.then_inc(z_mm, 1)

            def weights_tr(h):
                pe.wait_ge(att_ok, h + 1)
                if h >= 1:
                    pe.wait_ge(a_ok, h)
                for t in range(TT):
                    for j in range(t + 1):
                        o = 3 * BANK + AOFF[j] + P * (t - j)
                        i = ZOFF[t] + P * j
                        ins = transpose(ps[:, o:o + P], beta[:, h % 2, i:i + P])
                ins.then_inc(att_tr, 1)

            def values_mm(h):
                r0, ct = HD * (h % 2), h // 2
                pe.wait_ge(a_ok, h + 1)
                if h % 2 == 0 and h >= 2:
                    pe.wait_ge(o_lo, ct)
                for j in range(TT):
                    ins = mm(bank(6)[r0:r0 + HD, j * P:T], vv[:, j, h * HD:(h + 1) * HD],
                             at_sb[:, h % 2, AOFF[j]:AOFF[j] + AW[j]], start=(j == 0), stop=(j == TT - 1),
                             skip_group_check=True)
                ins.then_inc(o_mm, 1)

            def squares_mm(ct):
                pe.wait_ge(o_ev, ct + 1)
                for t in range(TT):
                    ins = mm(ps[:, 7 * BANK + 4 * t + ct:7 * BANK + 4 * t + ct + 1], sq[:, t * P:(t + 1) * P],
                             ones[:, 0:1], start=True, stop=True)
                ins.then_inc(ss_mm, 1)

            for h in range(HEADS + 2):
                if h < HEADS:
                    scores_mm(h)
                if h == 0:
                    modulation_row(5)
                if h == 2:
                    pe.wait_ge(row_ok, 4)
                if 1 <= h <= HEADS:
                    weights_tr(h - 1)
                if h >= 2:
                    values_mm(h - 2)
                if h >= 4 and h % 2 == 0:
                    squares_mm((h - 4) // 2)
            squares_mm(3)

            def out_proj(t):
                b0 = (t % 2) * 4
                if t == 0:
                    pe.wait_ge(wolo_ok, 2 * KD)
                    pe.wait_ge(o_lo, 4)
                if t == 1:
                    pe.wait_ge(rs_sb_ok, 1)
                if t >= 2:
                    pe.wait_ge(wo_o, t - 1)
                for br in range(2):
                    if t == 3 and br == 1:
                        pe.wait_ge(h2_ev, 1)
                    for hf in range(2):
                        for k in range(4):
                            for n, (m_, w) in enumerate(((mixhi, wohi), (mixhi, wolo), (mixlo, wohi))):
                                ins = mm(bank(b0 + 2 * br + hf), m_[br][:, k, t * P:(t + 1) * P],
                                         w[:, 4 * br + k, hf * 512:(hf + 1) * 512],
                                         start=(k == 0 and n == 0), stop=(k == 3 and n == 2))
                ins.then_inc(wo_mm, 1)

            def h2_transposes(t):
                pe.wait_ge(h2_ok, t + 1)
                pe.wait_ge(wo_o, (2, 3, 3, 4)[t])
                for k in range(KD):
                    ins = transpose(ps[:, H2_BANK[t] * BANK + k * P:H2_BANK[t] * BANK + (k + 1) * P],
                                    h2p[:, t % 2, k, :])
                ins.then_inc(h2_tr, 1)

            def router(t):
                pe.wait_ge(h2_ev, t + 1)
                for k in range(KD):
                    ins = mm(ps[:, 2 * BANK + t * E:2 * BANK + (t + 1) * E], h2t[:, k, t * P:(t + 1) * P],
                             wr[:, k, :], start=(k == 0), stop=(k == KD - 1))
                if t == TT - 1:
                    ins.then_inc(lg_mm, 1)

            def shared_up(t):
                for k in range(KD):
                    ins = mm(bank(SH_BANK[t]), h2t[:, k, t * P:(t + 1) * P], wsgu[:, :, k, :],
                             start=(k == 0), stop=(k == KD - 1))
                ins.then_inc(sgu_mm, 1)

            def shared_tr(t):
                pe.wait_ge(sact_ok, t + 1)
                if t == 0:
                    pe.wait_ge(h2_ok, TT)
                else:
                    pe.wait_ge(sat_ev, t)
                for k in range(KF):
                    ins = transpose(bank(6)[:, k * P:(k + 1) * P], act_s[:, k, :])
                ins.then_inc(sat_tr, 1)

            def shared_down(t):
                pe.wait_ge(sat_ev, t + 1)
                if t >= 1:
                    pe.wait_ge(sdn_ev, t)
                for hf in range(2):
                    for k in range(KF):
                        ins = mm(bank(4 + hf), sht[:, t % 2, k, :], wsd[:, k, hf * 512:(hf + 1) * 512],
                                 start=(k == 0), stop=(k == KF - 1))
                ins.then_inc(sdn_mm, 1)

            def positions():
                pe.wait_ge(sel_ok, 1)
                for t in range(TT):
                    for t2 in range(t + 1):
                        ins = mm(ps[:, 7 * BANK + t * E:7 * BANK + (t + 1) * E], (ustrb if t2 == t else onesb)[:, :],
                                 selb[:, t2, :], start=(t2 == 0), stop=(t2 == t))
                ins.then_inc(cnt_mm, 1)

            def indices(b):
                pe.wait_ge(onehot_ok, b + 1)
                for t in range(TT):
                    ins = mm(ps[:, 7 * BANK:7 * BANK + VC], s_onehot[:, t, :], vcur[:, t, :],
                             start=(t == 0), stop=(t == TT - 1))
                ins.then_inc(idx_mm, 1)

            def rows_in(b):
                pe.wait_ge(gathered, b * 16 + 16)
                for k in range(KD):
                    ins = transpose(ps[:, k * P:(k + 1) * P], hg[:, k, :])
                ins.then_inc(ht_tr, 1)

            def wpart(tile, slot, lo, n_, k):
                if n_ == 2:
                    q = 1 if tile is whi else 0
                    return tile[:, slot, q:q + 2, k * F:(k + 1) * F] if isinstance(slot, int) else \
                        tile[:, bass.ds(slot, 1), q:q + 2, k * F:(k + 1) * F].rearrange("p s g f -> p (s g) f")
                return part(tile, slot, 2, k * 512, (k + 1) * 512)

            def gate_up(b, slot):
                pe.wait_ge(lo_dve, b * 3 + 2)
                pe.wait_ge(lo_pool, b * 3 + 2)
                pe.wait_ge(htlo_ok, b + 1)
                for k in range(KD):
                    hi, lo = wpart(whi, slot, 0, 2, k), wpart(wlo, slot, 0, 2, k)
                    mm(bank(2), hthi[:, k, :], hi, start=(k == 0), stop=False)
                    mm(bank(2), hthi[:, k, :], lo, start=False, stop=False)
                    ins = mm(bank(2), htlo[:, k, :], hi, start=False, stop=(k == KD - 1))
                ins.then_inc(gu_mm, 1)

            def down(b, slot, first=False):
                pe.wait_ge(lo_dve, b * 3 + 3)
                pe.wait_ge(lo_pool, b * 3 + 3)
                pe.wait_ge(actlo_ok, b + 1)
                if not first:
                    pe.wait_ge(y_ok, b)
                for k in range(KF):
                    for st, w in ((acthi, whi), (acthi, wlo), (actlo, whi)):
                        for hf in range(2):
                            ins = mm(bank(4 + hf), st[:, k, :], wpart(w, slot, 2, 1, 2 * k + hf),
                                     start=(k == 0 and st is acthi and w is whi),
                                     stop=(k == KF - 1 and st is actlo))
                ins.then_inc(dn_mm, 1)

            def acts_tr(b):
                pe.wait_ge(act_ok, b + 1)
                for k in range(KF):
                    ins = transpose(ps[:, 3 * BANK + k * P:3 * BANK + (k + 1) * P], act_s[:, k, :])
                ins.then_inc(at_tr, 1)

            def one(b, slot, prev, first):
                gate_up(b, slot)
                rows_in(b + 1)
                down(b - 1, prev, first == 1)
                indices(b + 2)
                acts_tr(b)

            out_proj(0)
            out_proj(1)
            out_proj(2)
            h2_transposes(0)
            out_proj(3)
            h2_transposes(1)
            h2_transposes(2)
            pe.wait_ge(h2_ev, 2)
            pe.wait_ge(wsgu_in, 32)
            shared_up(0)
            pe.wait_ge(wr_in, 16)
            router(0)
            router(1)
            h2_transposes(3)
            router(2)
            router(3)
            shared_tr(0)
            shared_up(1)
            pe.wait_ge(wsd_in, 16)
            shared_down(0)
            shared_tr(1)
            positions()
            shared_down(1)
            shared_up(2)
            indices(0)
            shared_up(3)
            indices(1)
            shared_tr(2)
            rows_in(0)
            shared_tr(3)
            shared_down(2)
            gate_up(0, 0)
            rows_in(1)
            acts_tr(0)
            shared_down(3)
            for t in range(TT):
                ins = mm(ps[0:E, 6 * BANK:6 * BANK + 1], selb[:, t, :], onesb[:, 0:1],
                         start=(t == 0), stop=(t == TT - 1))
            ins.then_inc(count_mm, 1)
            indices(2)
            pe.wait_ge(ext_ok, 1)
            mm(ps[0:E, 6 * BANK + 1:6 * BANK + 2], ustrb[0:E, 0:E], extb[:, :], start=True, stop=True)
            mm(ps[0:1, 6 * BANK + 2:6 * BANK + 3], extb[:, :], onesb[0:E, 0:1], start=True, stop=True)\
                .then_inc(start_mm, 1)
            one(1, 1, 0, 1)
            pe.wait_ge(selx_ok, 1)
            mm(ps[0:1, 6 * BANK + 64:6 * BANK + 64 + OVER], iote[:, :], selx[:, :], start=True, stop=True)
            mm(ps[:, 6 * BANK + 128:6 * BANK + 128 + OVER], ones[0:E, :], jm[:, :], start=True, stop=True)\
                .then_inc(over_mm, 1)
            with pe.Fori(1, E // 2) as i:
                for s in range(2):
                    one(i * 2 + s, s, 1 - s, 2)
            pe.wait_ge(over_ok, 1)
            n = pe.value_load(nover[0:1, 0:1], min_val=0, max_val=OVER)
            with pe.If(n > 0):
                with pe.Fori(E, n + E) as b:
                    one(b, b % 2, (b + 1) % 2, 2)
            down(n + (E - 1), (n + 1) % 2)

        @block.vector
        def _(v):
            V = nc.vector
            step = [0]

            def then(ins):
                step[0] += 1
                ins.then_inc(v_step, 1)
                v.wait_ge(v_step, step[0])

            sums = [0]
            vars_ = [0]

            def factor(st, width, c0=0, c1=TT, src=None, wait=True):
                if wait:
                    sums[0] += 1
                    v.wait_ge(sumsq, sums[0])
                vv_, rr, r = var[:, st, c0:c1], root[:, st, c0:c1], rs[:, st, c0:c1]
                V.tensor_scalar(vv_, stat[:, st, c0:c1] if src is None else src, 1.0 / width, EPS,
                                ALU.mult, ALU.add).then_inc(var_ok, 1)
                vars_[0] += 1
                v.wait_ge(root_ok, vars_[0])
                then(V.reciprocal(r, rr))
                then(V.tensor_tensor(nt[:, c0:c1], r, r, ALU.mult))
                then(V.tensor_tensor(nt[:, c0:c1], nt[:, c0:c1], vv_, ALU.mult))
                then(V.tensor_scalar(nt[:, c0:c1], nt[:, c0:c1], -0.5, 1.5, ALU.mult, ALU.add))
                then(V.tensor_tensor(r, r, nt[:, c0:c1], ALU.mult))

            v.wait_ge(sc_ok, 1)

            def weigh_piece(n):
                ch, q = n // 4, n % 4
                if q == 0 and ch >= 2:
                    v.wait_ge(mod_mm, ch - 1)
                slot, count, _ = ada_slot(n)
                v.wait_ge(ada_in[slot], 16 * count)
                for r in range(2):
                    k = 2 * q + r
                    src = ada[slot][:, r, :]
                    if k == 0:
                        ins = V.tensor_scalar(acc[:, ch % 2, :], src, sc_col[:, 0:1], None, ALU.mult)
                    else:
                        ins = V.scalar_tensor_tensor(out=acc[:, ch % 2, :], in0=src, scalar=sc_col[:, k:k + 1],
                                                     in1=acc[:, ch % 2, :], op0=ALU.mult, op1=ALU.add)
                    if r == 0:
                        then(ins)
                    else:
                        ins.then_inc(ada_used, 1)
                        v.wait_ge(ada_used, n + 1)
                if q == 3:
                    v.sem_inc(acc_ok, 1)

            def low_out(br, k, src):
                return V.scalar_tensor_tensor(out=mixlo[br][:, k, :], in0=src,
                                              scalar=gb[:, 4 * br + k:4 * br + k + 1],
                                              in1=mixhi[br][:, k, :].bitcast(F32), op0=ALU.mult, op1=ALU.subtract)

            def gated_low(k):
                v.wait_ge(og_ev, k + 1)
                low_out(0, k, bank(4 + k % 2)).then_inc(og_lo, 1)

            for n in range(8):
                weigh_piece(n)
                if n == 2:
                    factor(ST_X, D)
                    v.sem_inc(rs_x_ok, 1)
            v.wait_ge(vec_in, 16 * 6)
            v.wait_ge(mod_mm, 2)
            m = ps[:, 7 * BANK:7 * BANK + 2 * KD]
            then(V.scalar_tensor_tensor(out=a1c[:, :], in0=m[:, 0:KD], scalar=1.0, in1=bsc[:, :],
                                        op0=ALU.add, op1=ALU.add))
            then(V.tensor_tensor(a1c[:, :], a1c[:, :], gpm[:, :], ALU.mult))
            V.tensor_tensor(b1c[:, :], m[:, KD:2 * KD], bsh[:, :], ALU.add).then_inc(ab_ok, 1)
            v.wait_ge(ab_ok, 1)
            def piece_low(i):
                v.wait_ge(wphi_ok, i + 1)
                V.tensor_tensor(wplo[:, i % 2, 0:KH // 2], wraw[:, i % 2, 0:KH // 2],
                                wphi[:, i % 2, 0:KH // 2].bitcast(F32), ALU.subtract).then_inc(wplo_dve, 1)

            for k in range(KD):
                v.wait_ge(h1_act, k + 1)
                then(V.tensor_copy(h1hi[:, k, :], h1f[:, k % 2]))
                V.tensor_tensor(h1lo[:, k, :], h1f[:, k % 2], h1hi[:, k, :].bitcast(F32), ALU.subtract)\
                    .then_inc(h1_dve, 1)
                if k == KH - 1:
                    piece_low(0)

            def mod_row(ch, dst, gain, plus_one):
                v.wait_ge(mod_mm, ch + 1)
                if plus_one:
                    ins = V.scalar_tensor_tensor(out=dst[:, :], in0=bank(6, 2), scalar=1.0, in1=dst[:, :],
                                                 op0=ALU.add, op1=ALU.add)
                else:
                    ins = V.tensor_tensor(dst[:, :], bank(6, 2), dst[:, :], ALU.add)
                if gain:
                    then(ins)
                    v.wait_ge(grow_in, 16 * gain)
                    ins = V.tensor_tensor(dst[:, :], dst[:, :], grow[:, :], ALU.mult)
                ins.then_inc(row_ok, 1)

            def gate(g):
                v.wait_ge(mixed_mm, g + 1)
                V.scalar_tensor_tensor(out=u_sb[:, :, g * P:(g + 1) * P],
                                       in0=bank(4 + g % 2).rearrange("p (t q) -> p t q", t=TT),
                                       scalar=bsp[:, g:g + 1], in1=u_sb[:, :, g * P:(g + 1) * P],
                                       op0=ALU.add, op1=ALU.mult).then_inc(og_ok, 1)

            piece_low(1)
            for i in range(2, PIECES):
                if i == 4:
                    v.wait_ge(row_in, 16 * 7)
                if i == 5:
                    mod_row(2, ga1, 1, False)
                if i == 7:
                    mod_row(3, a2, 2, True)
                if i == 9:
                    mod_row(4, b2, 0, False)
                if i == 3:
                    v.wait_ge(proj_ev, 4)
                    then(V.tensor_scalar(nt[:, :], stat[:, ST_VS, :], -1.0 / DG, None, ALU.mult))
                    for t in range(TT):
                        ins = V.tensor_scalar(v_sb[:, t, :], v_sb[:, t, :], nt[:, t:t + 1], None, ALU.add)
                    ins.then_inc(vmean_ok, 1)
                if i == 7:
                    gate(0)
                    gate(1)
                if i == 8:
                    gate(2)
                    gate(3)
                if i == 9:
                    gated_low(0)
                    gated_low(1)
                piece_low(i)
                if i == 4:
                    factor(ST_V, DG)
                    for t in range(TT):
                        then(V.scalar_tensor_tensor(out=v_sb[:, t, :], in0=v_sb[:, t, :],
                                                    scalar=rs[:, ST_V, t:t + 1], in1=lng[:, :],
                                                    op0=ALU.mult, op1=ALU.mult))
                        ins = V.tensor_tensor(v_sb[:, t, :], v_sb[:, t, :], lnb[:, :], ALU.add)
                        ins.then_inc(vn_ok, 1) if t == TT - 1 else then(ins)
                weigh_piece(2 * i + 4)
                weigh_piece(2 * i + 5)
                if i == 3:
                    v.wait_ge(wsp_tr, 1)
                    then(V.tensor_copy(wspt[:, :, :], bank(4).rearrange("p (g q) -> p g q", g=GROUPS)))
                    V.memset(wspt[CHUNK:P, :, 0:CHUNK], 0.0).then_inc(wsp_ok, 1)
            gated_low(2)
            gated_low(3)
            factor(ST_G, DG)
            v.sem_inc(rs_g_ok, 1)
            mod_row(5, ga2, 3, False)

            def pair_low(ct):
                v.wait_ge(o_ev, ct + 1)
                low_out(1, ct, bank(6)).then_inc(o_lo, 1)

            v.wait_ge(restart_ok, 1)
            for h in range(HEADS):
                v.wait_ge(beta_ok, 2 * h + 2)
                then(V.tensor_tensor_scan(rest[:, h % 2, ::-1], rest[:, h % 2, ::-1], restart[:, ::-1], 1.0,
                                          ALU.mult, ALU.max))
                V.tensor_tensor(beta[:, h % 2, 0:1279], beta[:, h % 2, 0:1279], rest[:, h % 2, 1:1280], ALU.mult)\
                    .then_inc(att_ok, 1)
                if h >= 3 and h % 2 == 1:
                    pair_low((h - 3) // 2)
            pair_low(3)
            v.wait_ge(ss_mm, 4)
            then(V.tensor_reduce(stat[:, ST_X, :],
                                 ps[:, 7 * BANK:7 * BANK + 16].rearrange("p (t c) -> p t c", t=TT), AX_X, ALU.add))
            factor(ST_X, DG, wait=False)
            v.sem_inc(rs_sb_ok, 1)
            def project_out(t):
                v.wait_ge(wo_a, t + 1)
                o = o_sb[:, t % 2, :]
                V.scalar_tensor_tensor(out=o, in0=bank((t % 2) * 4 + 2, 2), scalar=rs[:, ST_X, t:t + 1], in1=o,
                                       op0=ALU.mult, op1=ALU.add).then_inc(wo_o, 1)

            def residual(t):
                o = o_sb[:, t % 2, :]
                factor(ST_S, D, t, t + 1)
                then(V.scalar_tensor_tensor(out=o, in0=o, scalar=rs[:, ST_S, t:t + 1], in1=ga1[:, :],
                                            op0=ALU.mult, op1=ALU.mult))
                V.tensor_tensor(xs[:, t, :], xs[:, t, :], o, ALU.add).then_inc(wo_x, 1)

            def second_norm(t):
                o = o_sb[:, t % 2, :]
                factor(ST_O, D, t, t + 1)
                then(V.scalar_tensor_tensor(out=o, in0=xs[:, t, :], scalar=rs[:, ST_O, t:t + 1], in1=a2[:, :],
                                            op0=ALU.mult, op1=ALU.mult))
                if t >= 2:
                    v.wait_ge(h2_out[t % 2], 16)
                    v.wait_ge(h2_tr, t - 1)
                V.tensor_tensor(h2p[:, t % 2].rearrange("p k q -> p q k"),
                                o.rearrange("p (q k) -> p q k", k=KD),
                                b2[:, :].rearrange("p (q k) -> p q k", k=KD), ALU.add).then_inc(h2_ok, 1)

            for t in range(TT):
                project_out(t)
                if t >= 1:
                    second_norm(t - 1)
                residual(t)
            second_norm(TT - 1)

            def shared_act(t):
                v.wait_ge(ssg_ok, t + 1)
                if t >= 1:
                    v.wait_ge(sat_tr, t)
                V.tensor_tensor(act_s[:, :, :].rearrange("p k q -> p q k"),
                                bank(SH_BANK[t])[:, F:2 * F].rearrange("p (q k) -> p q k", k=KF),
                                sg[:, :].rearrange("p (q k) -> p q k", k=KF), ALU.mult).then_inc(sact_ok, 1)

            v.sem_inc(lo_dve, 3)
            shared_act(0)
            v.wait_ge(sig_ok, 1)
            then(V.tensor_tensor(biased[:, :, :], scores[:, :, :],
                                 rb[:, :].unsqueeze(1).to_broadcast([P, TT, E]), ALU.add))
            for t in range(TT):
                for g in range(EG):
                    ins = V.max(top2[:, t, g, :], biased[:, t, g * EPG:(g + 1) * EPG])
            then(ins)
            then(V.tensor_tensor(gs[:, :, :], top2[:, :, :, 0], top2[:, :, :, 1], ALU.add))
            mine = gs[:, :, :].unsqueeze(3).to_broadcast([P, TT, EG, EG])
            other = gs[:, :, :].unsqueeze(2).to_broadcast([P, TT, EG, EG])
            then(V.memset(gtri[:, :, :], 0.0))
            for g in range(1, EG):
                ins = V.memset(gtri[:, g, 0:g], 1.0)
            then(ins)
            then(V.tensor_tensor(gcmp[:, :, :, :], other, mine, ALU.is_gt))
            then(V.tensor_tensor(gcmp2[:, :, :, :], other, mine, ALU.is_equal))
            for t in range(TT):
                ins = V.tensor_tensor(gcmp2[:, t], gcmp2[:, t], gtri[:, :, :], ALU.mult)
            then(ins)
            then(V.tensor_tensor(gcmp[:, :, :, :], gcmp[:, :, :, :], gcmp2[:, :, :, :], ALU.add))
            then(V.tensor_reduce(gm[:, :, :], gcmp[:, :, :, :], AX_X, ALU.add))
            then(V.tensor_scalar(gm[:, :, :], gm[:, :, :], float(TOPG), None, ALU.is_lt))
            shared_act(1)
            gmb = gm[:, :, :].unsqueeze(3).to_broadcast([P, TT, EG, EPG])
            then(V.tensor_tensor(masked[:, :, :].rearrange("p t (g e) -> p t g e", g=EG),
                                 biased[:, :, :].rearrange("p t (g e) -> p t g e", g=EG), gmb, ALU.mult))
            then(V.tensor_scalar(gm[:, :, :], gm[:, :, :], -NEG, NEG, ALU.mult, ALU.add))
            then(V.tensor_tensor(masked[:, :, :].rearrange("p t (g e) -> p t g e", g=EG),
                                 masked[:, :, :].rearrange("p t (g e) -> p t g e", g=EG), gmb, ALU.add))
            for t in range(TT):
                ins = V.max(top8[:, t, :], masked[:, t, :])
            then(ins)
            for t in range(TT):
                ins = V.match_replace(picked[:, t, :], top8[:, t, :], masked[:, t, :], 3.0e38)
            then(ins)
            then(V.tensor_tensor(sel[:, :, :], picked[:, :, :], masked[:, :, :], ALU.not_equal))
            V.tensor_copy(selb[:, :, :], sel[:, :, :]).then_inc(sel_ok, 1)
            then(V.tensor_tensor(gates[:, :, 0:E], scores[:, :, :], sel[:, :, :], ALU.mult))
            then(V.tensor_reduce(wsum[:, :], gates[:, :, 0:E], AX_X, ALU.add))
            then(V.reciprocal(wsum[:, :], wsum[:, :]))
            for t in range(TT):
                ins = V.tensor_scalar(gates[:, t, 0:E], gates[:, t, 0:E], wsum[:, t:t + 1], SCALE_ROUTED,
                                      ALU.mult, ALU.mult)
            then(ins)
            for t in range(TT):
                ins = V.tensor_tensor_scan(rank[:, t, :], ones[:, 0:E], sel[:, t, :], 0.0, ALU.mult, ALU.add)
            then(ins)
            then(V.tensor_tensor(rank[:, :, :], rank[:, :, :], sel[:, :, :], ALU.subtract))
            then(V.tensor_scalar(rank[:, :, :], rank[:, :, :], float(T), None, ALU.mult))
            v.wait_ge(const_ok, 2)
            V.tensor_copy(vtab[:, :, 0:E, 2], rank[:, :, :])
            for part_ in range(3):
                then(V.tensor_copy(vtab[:, :, 0:E, 3 + part_], gates[:, :, :]))
                if part_ < 2:
                    then(V.tensor_tensor(gates[:, :, :], gates[:, :, :], vtab[:, :, 0:E, 3 + part_], ALU.subtract))
            v.wait_ge(cnt_mm, 1)
            then(V.scalar_tensor_tensor(out=posm[:, :, :],
                                        in0=ps[:, 7 * BANK:7 * BANK + TT * E].rearrange("p (t e) -> p t e", t=TT),
                                        scalar=1.0, in1=sel[:, :, :], op0=ALU.add, op1=ALU.mult))
            then(V.tensor_scalar(posb[:, :, 0:E], posm[:, :, :], -1.0, None, ALU.add))

            def over_count():
                v.wait_ge(count_mm, 1)
                cnt = ps[0:E, 6 * BANK:6 * BANK + 1]
                then(V.tensor_scalar(ext[:, 0:1], cnt, 128.5, None, ALU.is_gt))
                for lim in (256.5, 384.5):
                    then(V.scalar_tensor_tensor(out=ext[:, 0:1], in0=cnt, scalar=lim, in1=ext[:, 0:1],
                                                op0=ALU.is_gt, op1=ALU.add))
                V.tensor_copy(extb[:, :], ext[:, 0:1]).then_inc(ext_ok, 1)

            def over_select():
                v.wait_ge(start_mm, 1)
                then(V.tensor_copy(ext[:, 1:2], ps[0:E, 6 * BANK + 1:6 * BANK + 2]))
                V.tensor_copy(nover[:, :], ps[0:1, 6 * BANK + 2:6 * BANK + 3])
                then(V.tensor_scalar(tmp32[:, :], iot32[:, :], ext[:, 1:2], None, ALU.subtract))
                then(V.tensor_scalar(selx[:, :], tmp32[:, :], 0.0, None, ALU.is_ge))
                then(V.scalar_tensor_tensor(out=selx[:, :], in0=tmp32[:, :], scalar=ext[:, 0:1], in1=selx[:, :],
                                            op0=ALU.is_lt, op1=ALU.mult))
                then(V.scalar_tensor_tensor(out=jm[:, :], in0=tmp32[:, :], scalar=1.0, in1=selx[:, :],
                                            op0=ALU.add, op1=ALU.mult))
                V.tensor_scalar(jm[:, :], jm[:, :], -float(P), None, ALU.mult).then_inc(selx_ok, 1)

            def over_tables():
                v.wait_ge(over_mm, 1)
                V.tensor_copy(offs[:, :], ps[:, 6 * BANK + 128:6 * BANK + 128 + OVER])
                V.tensor_copy(eid[:, :], ps[0:1, 6 * BANK + 64:6 * BANK + 64 + OVER]).then_inc(over_ok, 1)

            PER = 6

            def col(tile, b, *rest):
                if isinstance(b, int):
                    return tile[:, b:b + 1]
                return tile[:, bass.ds(b, 1)]

            def onehot(b):
                src = vtab[:, :, b, :] if isinstance(b, int) else \
                    vtab[:, :, bass.ds(b, 1), :].rearrange("p t b v -> p t (b v)")
                V.tensor_copy(vcur[:, :, :], src)
                for t in range(TT):
                    pcol = posb[:, t, b:b + 1] if isinstance(b, int) else posb[:, t, bass.ds(b, 1)]
                    ins = V.tensor_scalar(s_onehot[:, t, :], iotab[:, :], pcol, None, ALU.is_equal)
                ins.then_inc(onehot_ok, 1)

            def tables(b):
                v.wait_ge(idx_mm, b + 1)
                k = [0]

                def chained(ins):
                    k[0] += 1
                    ins.then_inc(v_loop, 1)
                    v.wait_ge(v_loop, b * PER + k[0])

                chained(V.tensor_reduce(pair[:, :], ps[:, 7 * BANK:7 * BANK + VC].rearrange("p (a c) -> p a c", a=2),
                                        AX_X, ALU.add))
                chained(V.tensor_scalar(inval[:, :], pair[:, 0:1], 0.0, float(BIG_ROW), ALU.is_equal, ALU.mult))
                chained(V.scalar_tensor_tensor(out=desti[:, :], in0=pair[:, 0:1], scalar=-1.0, in1=inval[:, :],
                                               op0=ALU.add, op1=ALU.add))
                chained(V.tensor_copy(col(gater, b), pair[:, 1:2]))
                chained(V.tensor_copy(col(destr, b), desti[:, :]))
                chained(V.tensor_scalar(idxg[:, :], desti[:, :], (BIG_ROW >> 1) | (T - 1), None, ALU.bitwise_and))
                assert k[0] == PER
                v.sem_inc(idx_ok, 1)

            def low(b, wslot, rslot, piece):
                v.wait_ge(hi_ok, b * 3 + (piece + 1))
                c1 = 2048 - POOL_K * 256
                V.tensor_tensor(part(wlo, wslot, piece, 0, c1), raw[:, rslot, piece, 0:c1],
                                part(whi, wslot, piece, 0, c1).bitcast(F32), ALU.subtract).then_inc(lo_dve, 1)

            def times_up(b):
                v.wait_ge(silu_ok, b + 1)
                V.scalar_tensor_tensor(out=act_s[:, :, :].rearrange("p k q -> p q k"),
                                       in0=sg[:, :].rearrange("p (q k) -> p q k", k=KF), scalar=col(gater, b),
                                       in1=bank(2)[:, F:2 * F].rearrange("p (q k) -> p q k", k=KF),
                                       op0=ALU.mult, op1=ALU.mult).then_inc(act_ok, 1)

            def ht_low(b):
                v.wait_ge(hthi_ok, b + 1)
                V.tensor_tensor(htlo[:, :, :], bank(0, 2).rearrange("p (k q) -> p k q", k=KD),
                                hthi[:, :, :].bitcast(F32), ALU.subtract).then_inc(htlo_ok, 1)

            def acts_split(b):
                v.wait_ge(at_tr, b + 1)
                src = bank(3)[:, 0:F].rearrange("p (k q) -> p k q", k=KF)
                V.tensor_copy(acthi[:, :, :], src).then_inc(acthi_ok, 1)
                v.wait_ge(acthi_ok, b + 1)
                V.tensor_tensor(actlo[:, :, :], src, acthi[:, :, :].bitcast(F32), ALU.subtract).then_inc(actlo_ok, 1)

            def rows_of(b):
                if not (isinstance(b, int) and b == 0):
                    v.wait_ge(scattered, b * 16)
                V.tensor_copy(idxs[:, :], col(destr, b)).then_inc(idxs_ok, 1)

            def one(b, wslot, rslot):
                low(b, wslot, rslot, 0)
                low(b, wslot, rslot, 1)
                times_up(b - 1)
                ht_low(b)
                tables(b + 1)
                onehot(b + 2)
                low(b, wslot, rslot, 2)
                acts_split(b - 1)
                rows_of(b - 2)

            onehot(0)
            for s in range(2):
                v.wait_ge(h2_out[s], 16 * TT // 2)
            tables(0)
            onehot(1)
            shared_act(2)
            shared_act(3)
            ht_low(0)
            tables(1)
            low(1, 1, 1, 0)
            low(1, 1, 1, 1)
            onehot(2)
            v.wait_ge(sat_tr, TT)
            times_up(0)
            ht_low(1)
            over_count()
            tables(2)
            onehot(3)
            low(1, 1, 1, 2)
            acts_split(0)
            over_select()
            one(2, 0, 0)
            over_tables()
            one(3, 1, 1)
            v.wait_ge(fill_ok, 1)
            with v.Fori(2, E // 2) as i:
                for s in range(2):
                    one(i * 2 + s, s, s)
            n = v.value_load(nover[0:1, 0:1], min_val=0, max_val=OVER)
            with v.If(n > 0):
                with v.Fori(E, n + E) as b:
                    one(b, b % 2, 0)
            times_up(n + (E - 1))
            acts_split(n + (E - 1))
            rows_of(n + (E - 2))
            rows_of(n + (E - 1))

            for t in range(TT):
                for r in (1, 2, 3, 6, 7, 8):
                    if r == 1:
                        v.wait_ge(y_in[3 * t], 16)
                    if r == 3:
                        v.wait_ge(ypool_ok, t + 1)
                    if r == 6:
                        v.wait_ge(y_in[3 * t + 2], 16)
                    ins = V.tensor_tensor(yall[:, t, 0, :], yall[:, t, 0, :], yall[:, t, r, :], ALU.add)
                    ins.then_inc(ysum_ok, 1) if r == 8 else then(ins)
                factor(ST_S, D, t, t + 1)
                then(V.scalar_tensor_tensor(out=yall[:, t, 0, :], in0=yall[:, t, 0, :], scalar=rs[:, ST_S, t:t + 1],
                                            in1=ga2[:, :], op0=ALU.mult, op1=ALU.mult))
                V.tensor_tensor(xs[:, t, :], xs[:, t, :], yall[:, t, 0, :], ALU.add).then_inc(out_ok, 1)


_INS = ['x', 'c', 'w_ada', 'b_ada', 'g_pre_mix', 'w_in', 'ln_sgu_g', 'ln_sgu_b', 'w_spatial', 'b_spatial',
        'g_branch', 'w_out', 'g_post_mix', 'g_pre_ffn', 'w_router', 'router_bias', 'w_gate', 'w_up',
        'w_down', 'ws_gate', 'ws_up', 'ws_down', 'g_post_ffn']


def kernel(**inputs):
    import numpy as _np
    import concourse.bacc as _bacc
    from concourse import mybir as _mybir
    from concourse.bass_utils import run_bass_kernel_spmd as _run

    nc = _bacc.Bacc("TRN2", target_bir_lowering=False, num_devices=1)
    arrays, args = {}, []
    for name in _INS:
        a = _np.ascontiguousarray(inputs[name])
        a = a.reshape(a.shape[1:])
        arrays[f"in_{name}_dram"] = a
        args.append(nc.dram_tensor(f"in_{name}_dram", a.shape, _mybir.dt.from_np(a.dtype),
                                   kind="ExternalInput").ap())
    args.append(nc.dram_tensor("out_0_dram", (T, D), _mybir.dt.float32, kind="ExternalOutput").ap())
    block_kernel(nc, *args)
    r = _run(nc, [arrays], core_ids=[0])
    return r.results[0]["out_0_dram"].reshape(1, T, D)
```
